# Optimizing a Trainium2 kernel written in Bass

```python
import jax, jax.numpy as jnp
from jax import lax
import numpy as np

D_MODEL = 2048
BATCH = 1
SEQ = 512
DEPTH = 1
DEC_BATCH = 8
DEC_SEQ = 8
PAST_LEN = 4096
PAGE_SIZE = 128

POOL_WIDTH = D_MODEL // 2
POOL_GROUPS = 4
POOL_GROUP_DIM = POOL_WIDTH // POOL_GROUPS
POOL_WINDOWS = (2, 4, 8, 16)
POOL_BUF = max(POOL_WINDOWS) - 1
RET_WIDTH = D_MODEL - POOL_WIDTH
RET_HEADS = 4
RET_HEAD_DIM = RET_WIDTH // RET_HEADS
RET_CHUNK = 128
ROPE_BASE = 10000.0
IN_PROJ_WIDTH = POOL_WIDTH + 4 * RET_WIDTH
MEM_TOKENS = 256
MEM_HEADS = 4
MEM_HEAD_DIM = D_MODEL // MEM_HEADS
PEER_HEADS = 8
PEER_N_KEYS = 128
PEER_N_EXPERTS = PEER_N_KEYS * PEER_N_KEYS
PEER_TOPK = 16
PEER_QUERY_DIM = 256
PEER_HALF = PEER_QUERY_DIM // 2
PEER_BLOCK = 128
NORM_EPS = 1e-6

kernel_name = "hymba_pool_retnet_peer_decoder_step"

F32 = jnp.float32

def rmsnorm(x, g):
    xf = x.astype(F32)
    y = xf * lax.rsqrt(jnp.mean(jnp.square(xf), axis=-1, keepdims=True) + NORM_EPS)
    return (y * g.astype(F32)).astype(x.dtype)

def pool_mix(p_ext, pos, pool_w, pool_scale):
    B, L, W = p_ext.shape
    T = L - POOL_BUF
    pf = p_ext.astype(F32)
    c = jnp.pad(jnp.cumsum(pf, axis=1), ((0, 0), (1, 0), (0, 0)))
    end = c[:, POOL_BUF + 1:]
    means = []
    for gi, w in enumerate(POOL_WINDOWS):
        sl = slice(gi * POOL_GROUP_DIM, (gi + 1) * POOL_GROUP_DIM)
        start = c[:, POOL_BUF + 1 - w: POOL_BUF + 1 - w + T, sl]
        cnt = jnp.minimum(pos + 1, w).astype(F32)[None, :, None]
        means.append((end[..., sl] - start) / cnt)
    d = jnp.concatenate(means, axis=-1) - pf[:, POOL_BUF:]
    d = d.reshape(B, T, POOL_GROUPS, POOL_GROUP_DIM)
    y = jnp.einsum('btgc,gcd->btgd', d, pool_w.astype(F32)).reshape(B, T, W)
    return y * pool_scale.astype(F32)

def rotary(x, pos):
    half = x.shape[-1] // 2
    inv = 1.0 / (ROPE_BASE ** (jnp.arange(half, dtype=F32) / half))
    ang = pos.astype(F32)[:, None] * inv[None, :]
    cos, sin = jnp.cos(ang), jnp.sin(ang)
    x1, x2 = x[..., :half], x[..., half:]
    return jnp.concatenate([x1 * cos - x2 * sin, x1 * sin + x2 * cos], axis=-1)

def ret_log_gamma():
    return jnp.log(1.0 - 2.0 ** (-5.0 - jnp.arange(RET_HEADS, dtype=F32)))

def retention_chunk(q, k, v, s, log_gamma):
    C = q.shape[2]
    idx = jnp.arange(C, dtype=F32)
    diff = idx[:, None] - idx[None, :]
    lg = log_gamma[:, None, None]
    decay = jnp.where(diff >= 0, jnp.exp(lg * jnp.maximum(diff, 0.0)), 0.0)
    inner = jnp.einsum('bhid,bhjd->bhij', q, k) * decay[None]
    xi = jnp.exp(log_gamma[:, None] * (idx + 1.0))
    o = (jnp.einsum('bhij,bhjv->bhiv', inner, v)
         + jnp.einsum('bhid,bhdv->bhiv', q, s) * xi[None, :, :, None])
    zeta = jnp.exp(log_gamma[:, None] * (C - 1.0 - idx))
    s_new = (s * jnp.exp(log_gamma * C)[None, :, None, None]
             + jnp.einsum('bhjd,bhjv->bhdv', k * zeta[None, :, :, None], v))
    return o, s_new

def retention_seq(q, k, v, s0):
    B, H, T, dk = q.shape
    C = RET_CHUNK if T % RET_CHUNK == 0 else T
    n = T // C
    log_gamma = ret_log_gamma()

    def to_chunks(a):
        return jnp.moveaxis(a.reshape(B, H, n, C, a.shape[-1]), 2, 0)

    def step(s, qkv):
        qc, kc, vc = qkv
        o, s_new = retention_chunk(qc, kc, vc, s, log_gamma)
        return s_new, o

    s_fin, o = lax.scan(step, s0, (to_chunks(q), to_chunks(k), to_chunks(v)))
    o = jnp.moveaxis(o, 0, 2).reshape(B, H, T, -1)
    return o, s_fin

def retention_mixer(q, k, v, gate, pos, s0, ret_norm_g):
    B, T, _ = q.shape

    def heads(a):
        return a.reshape(B, T, RET_HEADS, RET_HEAD_DIM).transpose(0, 2, 1, 3).astype(F32)

    qh = rotary(heads(q), pos)
    kh = rotary(heads(k), pos) * (RET_HEAD_DIM ** -0.5)
    vh = heads(v)
    o, s_new = retention_seq(qh, kh, vh, s0.astype(F32))
    mu = jnp.mean(o, axis=-1, keepdims=True)
    var = jnp.mean(jnp.square(o - mu), axis=-1, keepdims=True)
    o = (o - mu) * lax.rsqrt(var + NORM_EPS)
    o = o.transpose(0, 2, 1, 3).reshape(B, T, RET_WIDTH) * ret_norm_g.astype(F32)
    return jax.nn.silu(gate.astype(F32)) * o, s_new

def mem_kv(mem, g_src, w_mk, w_mv):
    B, M, _ = mem.shape
    m = rmsnorm(mem, g_src)
    k = (m @ w_mk).reshape(B, M, MEM_HEADS, MEM_HEAD_DIM)
    v = (m @ w_mv).reshape(B, M, MEM_HEADS, MEM_HEAD_DIM)
    return k, v

def mem_attn(h, mk, mv, w_mq, w_mo):
    B, T, _ = h.shape
    q = (h @ w_mq).reshape(B, T, MEM_HEADS, MEM_HEAD_DIM)
    s = jnp.einsum('bthd,bmhd->bhtm', q.astype(F32), mk.astype(F32)) * (MEM_HEAD_DIM ** -0.5)
    p = jax.nn.softmax(s, axis=-1)
    o = jnp.einsum('bhtm,bmhd->bthd', p, mv.astype(F32)).reshape(B, T, D_MODEL)
    return o.astype(h.dtype) @ w_mo

def peer(h, peer_wq, peer_subkeys, peer_u, peer_v):
    B, T, D = h.shape
    n = B * T
    xt = h.reshape(n, D)
    pad = (-n) % PEER_BLOCK
    blocks = jnp.pad(xt, ((0, pad), (0, 0))).reshape(-1, PEER_BLOCK, D)
    subkeys = peer_subkeys.astype(F32)

    def one(xb):
        q = (xb @ peer_wq).reshape(PEER_BLOCK, PEER_HEADS, 2, PEER_HALF).astype(F32)
        s = jnp.einsum('thcd,hckd->thck', q, subkeys)
        sv, si = lax.top_k(s, PEER_TOPK)
        cand = sv[:, :, 0, :, None] + sv[:, :, 1, None, :]
        cidx = si[:, :, 0, :, None] * PEER_N_KEYS + si[:, :, 1, None, :]
        cand = cand.reshape(PEER_BLOCK, PEER_HEADS, PEER_TOPK * PEER_TOPK)
        cidx = cidx.reshape(PEER_BLOCK, PEER_HEADS, PEER_TOPK * PEER_TOPK)
        top_s, sel = lax.top_k(cand, PEER_TOPK)
        expert = jnp.take_along_axis(cidx, sel, axis=-1)
        g = jax.nn.softmax(top_s, axis=-1)
        u = jnp.take(peer_u, expert, axis=0).astype(F32)
        act = jax.nn.gelu(jnp.einsum('thkd,td->thk', u, xb.astype(F32)), approximate=False)
        vv = jnp.take(peer_v, expert, axis=0).astype(F32)
        return jnp.einsum('thk,thkd->td', g * act, vv).astype(h.dtype)

    out = lax.map(one, blocks).reshape(-1, D)[:n]
    return out.reshape(B, T, D)

def layer(x, pos, pool_prefix, s0, mk, mv, norm_mix_g, w_in, pool_w, pool_scale,
          ret_norm_g, w_out, norm_mem_g, w_mq, w_mo, norm_ffn_g, peer_wq,
          peer_subkeys, peer_u, peer_v):
    h = rmsnorm(x, norm_mix_g)
    proj = h @ w_in
    p = proj[..., :POOL_WIDTH]
    q, k, v, gate = jnp.split(proj[..., POOL_WIDTH:], 4, axis=-1)
    p_ext = jnp.concatenate([pool_prefix.astype(p.dtype), p], axis=1)
    a = pool_mix(p_ext, pos, pool_w, pool_scale)
    new_pool = p_ext[:, -POOL_BUF:]
    b, s_new = retention_mixer(q, k, v, gate, pos, s0, ret_norm_g)
    x = x + jnp.concatenate([a, b], axis=-1).astype(x.dtype) @ w_out
    x = x + mem_attn(rmsnorm(x, norm_mem_g), mk, mv, w_mq, w_mo)
    x = x + peer(rmsnorm(x, norm_ffn_g), peer_wq, peer_subkeys, peer_u, peer_v)
    return x, new_pool, s_new

def setup_inputs(seed: int = 0) -> dict:
    key = jax.random.key(seed)
    ks = jax.random.split(key, 32)
    nrm = lambda k, shape, s: jax.random.normal(k, shape, F32) * s
    gain = lambda k, shape: 1.0 + 0.02 * jax.random.normal(k, shape, F32)
    L = DEPTH
    D = D_MODEL
    return {
        "x_prompt": nrm(ks[0], (BATCH, SEQ, D), 1.0),
        "x_sample": nrm(ks[1], (DEC_BATCH, DEC_SEQ, D), 1.0),
        "state_pool": nrm(ks[2], (L, DEC_BATCH, POOL_BUF, POOL_WIDTH), 1.0),
        "state_ret": nrm(ks[3], (L, DEC_BATCH, RET_HEADS, RET_HEAD_DIM, RET_HEAD_DIM), 0.5),
        "cache_mem_k": nrm(ks[4], (L, DEC_BATCH, MEM_TOKENS, MEM_HEADS, MEM_HEAD_DIM), 1.0),
        "cache_mem_v": nrm(ks[5], (L, DEC_BATCH, MEM_TOKENS, MEM_HEADS, MEM_HEAD_DIM), 1.0),
        "mem_prompt": nrm(ks[6], (BATCH, MEM_TOKENS, D), 1.0),
        "norm_mix_g": gain(ks[7], (L, D)),
        "w_in": nrm(ks[8], (L, D, IN_PROJ_WIDTH), D ** -0.5),
        "pool_w": nrm(ks[9], (L, POOL_GROUPS, POOL_GROUP_DIM, POOL_GROUP_DIM), POOL_GROUP_DIM ** -0.5),
        "pool_scale": gain(ks[10], (L, POOL_WIDTH)),
        "ret_norm_g": gain(ks[11], (L, RET_WIDTH)),
        "w_out": nrm(ks[12], (L, D, D), D ** -0.5),
        "norm_mem_g": gain(ks[13], (L, D)),
        "norm_memsrc_g": gain(ks[14], (L, D)),
        "w_mq": nrm(ks[15], (L, D, D), D ** -0.5),
        "w_mk": nrm(ks[16], (L, D, D), D ** -0.5),
        "w_mv": nrm(ks[17], (L, D, D), D ** -0.5),
        "w_mo": nrm(ks[18], (L, D, D), D ** -0.5),
        "norm_ffn_g": gain(ks[19], (L, D)),
        "peer_wq": nrm(ks[20], (L, D, PEER_HEADS * PEER_QUERY_DIM), D ** -0.5),
        "peer_subkeys": nrm(ks[21], (L, PEER_HEADS, 2, PEER_N_KEYS, PEER_HALF), PEER_HALF ** -0.5),
        "peer_u": nrm(ks[22], (L, PEER_N_EXPERTS, D), D ** -0.5),
        "peer_v": nrm(ks[23], (L, PEER_N_EXPERTS, D), PEER_HEADS ** -0.5),
        "norm_final_g": gain(ks[24], (D,)),
    }

def reference(x_prompt, x_sample, state_pool, state_ret, cache_mem_k, cache_mem_v, mem_prompt,
              norm_mix_g, w_in, pool_w, pool_scale, ret_norm_g, w_out, norm_mem_g,
              norm_memsrc_g, w_mq, w_mk, w_mv, w_mo, norm_ffn_g, peer_wq, peer_subkeys,
              peer_u, peer_v, norm_final_g):
    Bp, Tp, _ = x_prompt.shape
    Bs, Ts, _ = x_sample.shape
    pos_p = jnp.arange(Tp, dtype=jnp.int32)
    pos_s = PAST_LEN + jnp.arange(Ts, dtype=jnp.int32)
    pool0 = jnp.zeros((Bp, POOL_BUF, POOL_WIDTH), x_prompt.dtype)
    ret0 = jnp.zeros((Bp, RET_HEADS, RET_HEAD_DIM, RET_HEAD_DIM), F32)

    yp, ys = x_prompt, x_sample
    pool_p_l, ret_p_l, mk_p_l, mv_p_l, pool_s_l, ret_s_l = [], [], [], [], [], []
    for l in range(DEPTH):
        w = (norm_mix_g[l], w_in[l], pool_w[l], pool_scale[l], ret_norm_g[l], w_out[l],
             norm_mem_g[l], w_mq[l], w_mo[l], norm_ffn_g[l], peer_wq[l], peer_subkeys[l],
             peer_u[l], peer_v[l])
        mk_p, mv_p = mem_kv(mem_prompt, norm_memsrc_g[l], w_mk[l], w_mv[l])
        yp, pool_p, ret_p = layer(yp, pos_p, pool0, ret0, mk_p, mv_p, *w)
        ys, pool_s, ret_s = layer(ys, pos_s, state_pool[l], state_ret[l],
                                  cache_mem_k[l], cache_mem_v[l], *w)
        pool_p_l.append(pool_p)
        ret_p_l.append(ret_p.astype(x_prompt.dtype))
        mk_p_l.append(mk_p)
        mv_p_l.append(mv_p)
        pool_s_l.append(pool_s.astype(state_pool.dtype))
        ret_s_l.append(ret_s.astype(state_ret.dtype))

    y_prompt = rmsnorm(yp, norm_final_g)
    y_sample = rmsnorm(ys, norm_final_g)
    return (y_prompt, y_sample, jnp.stack(pool_p_l), jnp.stack(ret_p_l), jnp.stack(mk_p_l),
            jnp.stack(mv_p_l), jnp.stack(pool_s_l), jnp.stack(ret_s_l))


_drawn_inputs = setup_inputs


def setup_inputs(seed=0):
    import zlib

    import numpy as np

    out = dict(_drawn_inputs(seed))
    spreads = {}
    factors = {'pool_scale': 3.188,
     'ret_norm_g': 3.968,
     'norm_mem_g': 8.0,
     'norm_memsrc_g': 2.786,
     'norm_final_g': 8.042,
     'norm_ffn_g': 6.193}
    for name, (base, spread) in spreads.items():
        noise = np.random.default_rng([zlib.crc32(name.encode()), seed]).standard_normal(out[name].shape)
        drawn = base * np.exp(spread * noise) if base else spread * noise
        out[name] = __import__('jax').numpy.asarray(drawn.astype(out[name].dtype))
    for name, factor in factors.items():
        out[name] = (out[name] * factor).astype(out[name].dtype)
    return out
```

```python
from contextlib import ExitStack, contextmanager

import concourse.bass as bass
import numpy as np
from concourse import mybir

F32 = mybir.dt.float32
F32R = mybir.dt.float32r
U32 = mybir.dt.uint32
ACT = mybir.ActivationFunctionType
ALU = mybir.AluOpType
AX = mybir.AxisListType

P = 128
D = 2048
KB = D // P
TP = 512
SB, SQ = 8, 8
TS = SB * SQ
T = TP + TS
HALF = T // 2
PAST = 4096
MEM = 256
GROUPS = 4
BUF = 15
RH, RD = 4, 256
MH, MD = 4, 512
EH = 8
NK = 128
TOPK = 16
TILES = 5
EPS = 1e-6
LOWEST = -3.0e38
HW = 1024
PG = 32
NPG = T // PG

B_MK, B_MV, B_POOL, B_RET, B_OUT, B_MQ, B_MO, B_WQ = 0, 16, 20, 28, 60, 76, 92, 108
H_MV, H_POOL, H_RET, H_OUT, H_MQ, H_MO, H_WQ, H_END = 32, 64, 80, 144, 176, 208, 240, 272

G_MIX, G_MEM, G_SRC, G_FFN, G_FIN, G_POOLS, G_RET = 0, 16, 32, 48, 64, 80, 88
T_DEC, T_DECS, T_XI, T_ZETA, T_ZETAS, T_G8, T_END = 0, 512, 576, 640, 644, 652, 653


def used(n):
    return n + 4


class Steps:

    def __init__(self, eng, sem):
        self.eng, self.sem, self.base, self.count, self.i, self.per = eng, sem, 0, 0, None, 0

    def link(self, ins):
        ins.then_inc(self.sem, 1)
        self.count += 1
        at = self.base + self.count
        self.eng.wait_ge(self.sem, at if self.i is None else self.i * self.per + at)

    @contextmanager
    def loop(self, n, per):
        self.base, self.count, self.per = self.base + self.count, 0, per
        with self.eng.Fori(0, n) as i:
            self.i = i
            yield i
        assert self.count == per, (self.count, per)
        self.base, self.count, self.i = self.base + n * per, 0, None


def build(nc, xT, memT, w_lin, gains, consts, spoolT, sret, kcT, vc, pool_w, rot, tabs, subk, uT, vE,
          yT, npoolT_p, nret_p, mkT, mv, npoolT_s, nret_s):
    with ExitStack() as ctx:
        def sb(name, shape, dt=F32):
            return ctx.enter_context(nc.sbuf_tensor(name, shape, dt))

        def sem(name):
            return ctx.enter_context(nc.semaphore(name))

        def dram(name, shape):
            return nc.dram_tensor(name, shape, F32, kind="Internal").ap()

        mixT = dram("mixT", (KB, P, T))
        x2T = dram("x2T", (KB, P, T))
        omT = dram("omT", (KB, P, T))
        x3T = dram("x3T", (KB, P, T))
        pmap = dram("pmap", (NPG, P, NK * PG))

        HL = sb("HL", [P, 2, KB, T], F32R)
        WS = sb("WS", [P, 4, 2, HW], F32R)
        WW = sb("WW", [P, 2, 2, 2, T], F32R)
        RAW = sb("RAW", [P, 2, HW])
        CS = sb("CS", [P, 2, T])
        CST = sb("CST", [P, 2, P])
        ONES = sb("ONES", [P, 2, P])
        GAINS = sb("GAINS", [P, 96])
        RC = sb("RC", [P, 16])
        AR = sb("AR", [P, 17440])
        PS = ctx.enter_context(nc.psum_tensor("PS", [P, 4096], F32))
        IDENT, IOTA = CST[:, 0, :], CST[:, 1, :]

        def ar(start, *dims, rows=P):
            n = int(np.prod(dims))
            v = AR[0:rows, start:start + n]
            if len(dims) == 1:
                return v
            names = "abcd"[:len(dims)]
            return v.rearrange(f"p ({' '.join(names)}) -> p {' '.join(names)}",
                               **{names[k]: dims[k] for k in range(1, len(dims))})

        def bank(b, n=512, rows=P, off=0):
            return PS[0:rows, 512 * b + off:512 * b + off + n]

        def pair(a):
            return PS[:, 1024 * a:1024 * a + 1024].rearrange("p (b n) -> p b n", b=2)[:, :, 0:HALF]

        def halves(v):
            return v.rearrange("p (b n) -> p b n", b=2)

        def wide(v, n):
            return v.unsqueeze(2).to_broadcast([v.shape[0], v.shape[1], n])

        X = ar(0, KB, T)
        N0 = KB * T
        NSQ, NACC, NVAR, NRS, NT = ar(N0, 2, T), ar(N0 + 1152, T), ar(N0 + 1728, T), ar(N0 + 2304, T), ar(N0 + 2880, 3, T)
        XM, KST, VST = ar(0, KB, MEM), ar(14000, 2, MEM), ar(14512, 2, 1024)
        PEX, PTA, PTB = ar(0, 2, BUF + TP), ar(1054, 2, BUF + TP), ar(2108, 2, BUF + TP)
        PSX, PSA, PSB = ar(3162, 2, SB, BUF + SQ), ar(3530, 2, SB, BUF + SQ), ar(3898, 2, SB, BUF + SQ)
        DT, AT, PW = ar(4266, 2, T), ar(5418, 2, T), ar(6570, 2, 256)
        RAWQ, RQ, RK = ar(0, 8, T), ar(4608, 2, T), ar(5760, 2, T)
        OT, SQD, RVAR = ar(0, 2, T), ar(5760, 2, T), ar(4608, T)
        INNER = [ar(1152 + o, TP - P * j) for j, o in enumerate((0, 512, 896, 1152))]
        VTOK, KTOK, KM = ar(6912, TILES, RD), ar(8192, TILES, RD), ar(9472, SB, RD, rows=TS)
        RT = ar(9472, 2, T)
        TAB, QX, SST = ar(11520, T_END), ar(12176, 2, TS), ar(12304, SB, 2, RD)
        SPR, INNERS = ar(16400, 2, RD), ar(16912, TS, rows=TS)
        QM, QZ, KT, VT = ar(0, 4, T), ar(2304, SB, 4, TS), ar(4352, 4, MEM), ar(5376, 2, MD)
        KS, VS = ar(6400, 4, 4, MEM), ar(10496, 2, 2, MD)
        PR, PT, OB = ar(12544, TILES, MEM), ar(13824, 2, T), ar(14976, 4, T)
        MX, NMX, SM, RSM = ar(17280, TILES), ar(17285, TILES), ar(17290, TILES), ar(17295, TILES)
        QP, SC, SV = ar(0, 2, T), ar(1152, 2, TILES, NK), ar(2432, 2, TILES, TOPK)
        SI, SIF = ar(2592, 2, TILES, TOPK).bitcast(U32), ar(2752, 2, TILES, TOPK)
        CAND, TV, TI = ar(2912, TILES, 256), ar(4192, TILES, TOPK), ar(4272, TILES, TOPK).bitcast(U32)
        TA, TAF = ar(4352, 2, TILES * TOPK).bitcast(U32), ar(4512, 2, TILES * TOPK)
        EQ, EQ2 = ar(4672, TILES * TOPK, TOPK), ar(5952, TILES * TOPK, TOPK)
        GS, IJ = ar(7232, TILES, P), ar(7872, 2, TILES, P)
        SMX = ar(4192, TILES * EH)
        SK = ar(13824, 2 * EH, NK)
        GIJ = ar(0, 3, T)
        AA, BB, STG = ar(1728, 2, 4, P), ar(2752, 2, 4, P), ar(9216, 2, NK, PG)
        GE, PP = ar(9216, 2, T), ar(10368, 2, NPG, 2, PG)

        names = (
            "in_const in_x in_mem in_tab in_pw in_pool in_sub in_p0 in_p1 in_t0 in_t1 in_t2 raw0 raw1 "
            "ks_in0 ks_in1 ks_in2 ks_in3 vs_in0 vs_in1 in_kt in_st "
            "out_k0 out_k1 out_v0 out_v1 out_pool out_a out_spr out_sst out_b out_x out_om out_p0 out_p1 out_y0 out_y1 out_y2 "
            "consts_set waited_p waited_v dve_step act_step raw_free used hi_done split_done lin_evac "
            "sq_ready sq_used sum_done var_ready sd_ready t_ready hi_ready lo_ready "
            "pool_d pool_mm pool_evac rot_done qx_done vt_done v_evac kt_done k_evac km_done qk_done inner_done "
            "o_done o_evac spr_evac mean_done sqd_ready rvar_done rvar_ready rsd_ready ks_mm sst_new b_done "
            "x_added qz_done mx_done p_exp p_done pt_done pt_evac om_evac ks_used vs_used "
            "sk_done sc_evac cand_done sel_done soft_in soft_exp soft_done gt_done gt_evac "
            "pa_ready p_mm pbank_free gelu_done w_done whi_done ww_ready v_done v_free"
        ).split()
        S = {n: sem(n) for n in names}

        block = ctx.enter_context(nc.Block())

        @block.sync
        def _(sp):
            def load_halves(src, n_pairs, first):
                with sp.Fori(0, n_pairs) as i:
                    for s in range(2):
                        sp.wait_ge(S["raw_free"], i * 2 + (first + s + 1))
                        sp.dma_start(RAW[:, s, :], src(i * 2 + s)).then_inc(S[f"raw{s}"], 16)

            for dst, src in ((CST[:, :, :], consts[:, 0:256].rearrange("p (a n) -> p a n", a=2)),
                             (RC[:, :], consts[:, 256:272]), (GAINS[:, :], gains), (CS[:, :, :], rot)):
                sp.dma_start(dst, src).then_inc(S["in_const"], 16)
            sp.dma_start(XM, memT.rearrange("k p m -> p k m")).then_inc(S["in_mem"], 16)
            load_halves(lambda n: w_lin[bass.ds(n, 1)].rearrange("a p n -> p (a n)"), H_MQ // 2, 0)

            sp.wait_ge(S["lo_ready"], 16 * 4)
            sp.wait_ge(S["out_x"], 16)
            with sp.Fori(0, MH) as h:
                sp.wait_ge(S["vs_used"], h * SB + 2)
                sp.dma_start(KT, mkT[bass.ts(h, 4)].rearrange("c p m -> p c m")).then_inc(S["in_kt"], 16)
                sp.dma_start(VT, mv.rearrange("(m p) n -> p m n", p=P)[:, :, bass.ts(h, MD)]).then_inc(S["in_kt"], 16)

                def load_k(b):
                    sp.wait_ge(S["ks_used"], h * SB + (b + 1))
                    sp.dma_start(KS[:, b % 4], kcT[b, bass.ds(h, 1)].rearrange("a (c p) m -> p (a c) m", p=P))\
                        .then_inc(S[f"ks_in{b % 4}"], 16)

                for b in range(4):
                    load_k(b)
                for n in range(8):
                    sp.wait_ge(S["raw_free"], h * 8 + (H_MQ + n + 1))
                    sp.dma_start(RAW[:, n % 2, :], w_lin[bass.ds(h * 8 + (H_MQ + n), 1)].rearrange("a p n -> p (a n)"))\
                        .then_inc(S[f"raw{n % 2}"], 16)
                for b in range(4, SB):
                    load_k(b)
                for b in range(SB):
                    sp.wait_ge(S["vs_used"], h * SB + (b + 1))
                    sp.dma_start(VS[:, b % 2], vc[b].rearrange("(m p) n -> p m n", p=P)[:, :, bass.ts(h, MD)])\
                        .then_inc(S[f"vs_in{b % 2}"], 16)
            load_halves(lambda n: w_lin[bass.ds(n + H_MO, 1)].rearrange("a p n -> p (a n)"), (H_END - H_MO) // 2, H_MO)

            def load_u(pr, n0, i):
                for n in range(4):
                    s = n % 2
                    sp.wait_ge(S["raw_free"], n0(n) + 1)
                    sp.dma_start(RAW[:, s, :], uT[bass.ds(pr * 4 + n, 1)].rearrange("a p n -> p (a n)"))\
                        .then_inc(S[f"raw{s}"], 16)

            def load_v(pr, n0, i):
                for n in range(4):
                    s = n % 2
                    sp.wait_ge(S["raw_free"], n0(n) + 1)
                    sp.dma_start(RAW[:, s, :], vE[bass.ds(pr * 2 + n % 2, 1), :, HW * (n // 2):HW * (n // 2 + 1)]
                                 .rearrange("a p n -> p (a n)")).then_inc(S[f"raw{s}"], 16)

            load_u(0, lambda n: H_END + n, None)
            with sp.Fori(0, NK // 2 - 1) as i:
                load_u(i + 1, lambda n: i * 8 + (H_END + 4 + n), i)
                load_v(i, lambda n: i * 8 + (H_END + 8 + n), i)
            load_v(NK // 2 - 1, lambda n: H_END + 8 * (NK // 2) - 4 + n, None)

        @block.gpsimd
        def _(pool):
            pool.memset(ONES[:, 0, :], 1.0 / D).then_inc(S["consts_set"], 1)
            pool.memset(ONES[:, 1, :], 1.0 / RD).then_inc(S["consts_set"], 1)
            pool.sem_inc(S["raw_free"], 2)

            def split4(n, r):
                for s2 in range(2):
                    for s in range(2):
                        k = 2 * s2 + s
                        pool.wait_ge(S[f"raw{s}"], r * 16 + 16 * (s2 + 1))
                        pool.wait_ge(S["used"], n + (k + 1))
                        pool.sem_inc(S["waited_p"], 1)
                        pool.tensor_copy(WS[:, k, 0, :], RAW[:, s, :]).then_inc(S["hi_done"], 1)
                    for s in range(2):
                        k = 2 * s2 + s
                        pool.wait_ge(S["hi_done"], n + (k + 1))
                        pool.tensor_tensor(WS[:, k, 1, :], RAW[:, s, :], WS[:, k, 0, :].bitcast(F32), ALU.subtract)\
                            .then_inc(S["split_done"], 1)
                        pool.wait_ge(S["split_done"], n + (k + 1))
                        pool.sem_inc(S["raw_free"], 1)

            with pool.Fori(0, H_END // 4) as i:
                split4(i * 4, i * 2)
            with pool.Fori(0, NK) as i:
                split4(i * 4 + H_END, i * 2 + H_END // 2)

        @block.tensor
        def _(pe):
            mm = pe.matmul
            pe.sem_inc(S["used"], 4)
            pe.sem_inc(S["p_mm"], 2)
            pe.sem_inc(S["ks_used"], 4)
            pe.sem_inc(S["vs_used"], 2)

            def projection(n, m, a, slot, cols=((0, HALF), (HALF, HALF))):
                pe.wait_ge(S["lin_evac"], m + 1)
                for hf in range(2):
                    pe.wait_ge(S["split_done"], n + (hf + 1))
                    for k in range(KB // 2):
                        kb = hf * (KB // 2) + k
                        first, last = kb == 0, kb == KB - 1
                        for wp, xp in ((0, 0), (0, 1), (1, 0)):
                            for c, (at, w) in enumerate(cols):
                                ins = mm(bank(2 * a + c, w), WS[:, slot + hf, wp, k * P:(k + 1) * P],
                                         HL[:, xp, kb, at:at + w], start=first and (wp, xp) == (0, 0),
                                         stop=last and wp == 1, skip_group_check=True)
                    ins.then_inc(S["used"], 1)

            def norm_sum(k, cols=((0, HALF), (HALF, HALF))):
                pe.wait_ge(S["sq_used"], 16 * (k + 1))
                for c, (at, w) in enumerate(cols):
                    ins = mm(bank(6 + c, w), ONES[:, 0, :], NACC[:, at:at + w], start=True, stop=True)
                ins.then_inc(S["sum_done"], 1)

            pe.wait_ge(S["consts_set"], 2)
            pe.wait_ge(S["in_const"], 64)
            norm_sum(0, ((0, MEM),))
            pe.wait_ge(S["lo_ready"], 16)
            with pe.Fori(0, 8) as i:
                for s in range(2):
                    projection(i * 4 + 2 * s, i * 2 + (B_MK + s), s, 2 * s, ((0, MEM),))
            with pe.Fori(0, 2) as i:
                for a in range(2):
                    pe.wait_ge(S["lin_evac"], i * 2 + (B_MV + a + 1))
                    for q in range(8):
                        n = i * 16 + (H_MV + 8 * a + q)
                        pe.wait_ge(S["split_done"], n + 1)
                        for k in range(2):
                            kb = 2 * q + k
                            for xp, wp in ((0, 0), (0, 1), (1, 0)):
                                for t in range(2):
                                    ins = mm(bank(2 * a + t), HL[:, xp, kb, t * P:(t + 1) * P],
                                             WS[:, q % 4, wp, k * 512:(k + 1) * 512],
                                             start=kb == 0 and (xp, wp) == (0, 0), stop=kb == KB - 1 and xp == 1,
                                             skip_group_check=True)
                        ins.then_inc(S["used"], 1)

            norm_sum(1)
            pe.wait_ge(S["lo_ready"], 32)
            with pe.Fori(0, GROUPS) as g:
                for s in range(2):
                    projection(g * 4 + (H_POOL + 2 * s), g * 2 + (B_POOL + s), s, 2 * s)
                pe.wait_ge(S["pool_d"], g + 1)
                pe.wait_ge(S["in_pw"], g * 16 + 16)
                pe.wait_ge(S["pool_evac"], g)
                for o in range(2):
                    for c in range(2):
                        for ch in range(2):
                            ins = mm(bank(4 + 2 * o + ch, HALF), PW[:, c, o * P:(o + 1) * P],
                                     DT[:, c, ch * HALF:(ch + 1) * HALF], start=c == 0, stop=c == 1,
                                     skip_group_check=True)
                ins.then_inc(S["pool_mm"], 1)

            with pe.Fori(0, RH) as h:
                for m in range(8):
                    projection(h * 16 + (H_RET + 2 * m), h * 8 + (B_RET + m), m % 2, 2 * (m % 2))
                pe.wait_ge(S["lin_evac"], h * 8 + (B_RET + 6 + 2))
                pe.wait_ge(S["b_done"], h)
                pe.wait_ge(S["pool_evac"], GROUPS)
                for t in range(TILES):
                    w = P if t < 4 else TS
                    for c in range(2):
                        ins = pe.transpose(PS[0:w, 2048 + RD * t + P * c:2048 + RD * t + P * c + P],
                                           RAWQ[:, 4 + c, P * t:P * t + w], IDENT)
                ins.then_inc(S["vt_done"], 1)
                pe.wait_ge(S["rot_done"], h + 1)
                pe.wait_ge(S["v_evac"], h + 1)
                for t in range(TILES):
                    w = P if t < 4 else TS
                    for c in range(2):
                        ins = pe.transpose(PS[0:w, 2048 + RD * t + P * c:2048 + RD * t + P * c + P],
                                           RK[:, c, P * t:P * t + w], IDENT)
                ins.then_inc(S["kt_done"], 1)
                pe.wait_ge(S["k_evac"], h + 1)
                for j in range(4):
                    for c in range(2):
                        mm(bank(4 + j, TP - P * j), RK[:, c, P * j:P * (j + 1)], RQ[:, c, P * j:TP],
                           start=c == 0, stop=c == 1)
                for c in range(2):
                    ins = mm(bank(7, TS, TS, 256), RK[:, c, TP:T], RQ[:, c, TP:T], start=c == 0, stop=c == 1)
                ins.then_inc(S["qk_done"], 1)
                pe.wait_ge(S["inner_done"], h + 1)
                pe.wait_ge(S["qx_done"], h + 1)
                pe.wait_ge(S["in_st"], h * 128 + 128)
                for c in range(2):
                    for j in range(4):
                        mm(bank(4 + c, TP - P * j, off=P * j), VTOK[:, j, P * c:P * (c + 1)], INNER[j],
                           start=j == 0, stop=j == 3, skip_group_check=True)
                    mm(bank(6, TS, off=TS * c), VTOK[0:TS, 4, P * c:P * (c + 1)], INNERS,
                       start=True, stop=False, skip_group_check=True)
                    for b in range(SB):
                        for k in range(2):
                            ins = mm(bank(6, SQ, off=TS * c + SQ * b), SST[:, b, k, P * c:P * (c + 1)],
                                     QX[:, k, SQ * b:SQ * (b + 1)], start=False, stop=k == 1, skip_group_check=True)
                ins.then_inc(S["o_done"], 1)
                for c in range(2):
                    for j in range(4):
                        ins = mm(bank(7, RD, off=RD * c), KTOK[:, j, P * c:P * (c + 1)], VTOK[:, j, :],
                                 start=j == 0, stop=j == 3, skip_group_check=True)
                ins.then_inc(S["o_done"], 1)
                pe.wait_ge(S["o_evac"], h + 1)
                pe.wait_ge(S["spr_evac"], h + 1)
                for ch in range(2):
                    for c in range(2):
                        ins = mm(bank(6 + ch, HALF), ONES[:, 1, :], OT[:, c, ch * HALF:(ch + 1) * HALF],
                                 start=c == 0, stop=c == 1)
                ins.then_inc(S["mean_done"], 1)
                pe.wait_ge(S["km_done"], h + 1)
                for b in range(SB):
                    if b >= 2:
                        pe.wait_ge(S["sst_new"], h * SB + (b - 1))
                    for c in range(2):
                        ins = mm(bank(4 + b % 2, RD, off=RD * c), KM[:, b, P * c:P * (c + 1)], VTOK[0:TS, 4, :],
                                 start=True, stop=True, skip_group_check=True)
                    ins.then_inc(S["ks_mm"], 1)
                pe.wait_ge(S["sqd_ready"], h + 1)
                for ch in range(2):
                    for c in range(2):
                        ins = mm(bank(6 + ch, HALF), ONES[:, 1, :], SQD[:, c, ch * HALF:(ch + 1) * HALF],
                                 start=c == 0, stop=c == 1)
                ins.then_inc(S["rvar_done"], 1)

            pe.wait_ge(S["lo_ready"], 48)
            with pe.Fori(0, 8) as i:
                for s in range(2):
                    projection(i * 4 + (H_OUT + 2 * s), i * 2 + (B_OUT + s), s, 2 * s)
            norm_sum(2)
            pe.wait_ge(S["lo_ready"], 64)

            with pe.Fori(0, MH) as h:
                pe.wait_ge(S["om_evac"], h)
                for m in range(4):
                    projection(h * 8 + (H_MQ + 2 * m), h * 4 + (B_MQ + m), m % 2, 2 * (m % 2))
                pe.wait_ge(S["lin_evac"], h * 4 + (B_MQ + 4 + 2))
                pe.wait_ge(S["in_kt"], h * 32 + 32)
                for t in range(4):
                    for c in range(4):
                        mm(bank(4, MEM, off=MEM * t), QM[:, c, P * t:P * (t + 1)], KT[:, c, :],
                           start=c == 0, stop=c == 3, skip_group_check=True)
                pe.wait_ge(S["qz_done"], h + 1)
                for b in range(SB):
                    pe.wait_ge(S[f"ks_in{b % 4}"], h * 32 + 16 * (b // 4 + 1))
                    for c in range(4):
                        ins = mm(bank(6, MEM, TS), QZ[:, b, c, :], KS[:, b % 4, c, :],
                                 start=b == 0 and c == 0, stop=b == 7 and c == 3, skip_group_check=True)
                    ins.then_inc(S["ks_used"], 1)
                pe.wait_ge(S["p_done"], h + 1)
                for m in range(2):
                    for t in range(4):
                        pe.transpose(bank(4 + m, P, off=P * t), PR[:, t, P * m:P * (m + 1)], IDENT)
                    ins = pe.transpose(bank(6, TS, off=TS * m), PR[0:TS, 4, P * m:P * (m + 1)], CST[0:TS, 0, 0:TS])
                ins.then_inc(S["pt_done"], 1)
                pe.wait_ge(S["pt_evac"], h + 1)
                for c in range(4):
                    for m in range(2):
                        mm(bank(4 + c), VT[:, m, P * c:P * (c + 1)], PT[:, m, 0:TP], start=m == 0, stop=m == 1)
                for b in range(SB):
                    pe.wait_ge(S[f"vs_in{b % 2}"], h * 64 + 16 * (b // 2 + 1))
                    for c in range(4):
                        for m in range(2):
                            ins = mm(bank(0, SQ, off=TS * c + SQ * b), VS[:, b % 2, m, P * c:P * (c + 1)],
                                     PT[:, m, TP + SQ * b:TP + SQ * (b + 1)], start=m == 0, stop=m == 1,
                                     skip_group_check=True)
                    ins.then_inc(S["vs_used"], 1)

            pe.wait_ge(S["om_evac"], MH)
            pe.wait_ge(S["lo_ready"], 80)
            with pe.Fori(0, 8) as i:
                for s in range(2):
                    projection(i * 4 + (H_MO + 2 * s), i * 2 + (B_MO + s), s, 2 * s)
            norm_sum(3)
            pe.wait_ge(S["lo_ready"], 96)

            pe.wait_ge(S["in_sub"], 16)
            with pe.Fori(0, EH) as h:
                for s in range(2):
                    projection(h * 4 + (H_WQ + 2 * s), h * 2 + (B_WQ + s), s, 2 * s)
                pe.wait_ge(S["lin_evac"], h * 2 + (B_WQ + 2 + 2))
                pe.wait_ge(S["sc_evac"], h)
                for c in range(2):
                    keys = SK[:, bass.ds(h * 2 + c, 1), :].rearrange("p a n -> p (a n)")
                    for t in range(TILES):
                        w = P if t < 4 else TS
                        ins = mm(PS[0:w, 512 * (4 + 2 * c) + P * t:512 * (4 + 2 * c) + P * (t + 1)],
                                 QP[:, c, P * t:P * t + w], keys, start=True, stop=True, skip_group_check=True)
                ins.then_inc(S["sk_done"], 1)
            pe.wait_ge(S["soft_done"], 1)
            pe.wait_ge(S["sc_evac"], EH)
            pe.wait_ge(S["lin_evac"], B_WQ + 16 + 2)
            for k, src in enumerate((GS, IJ[:, 0], IJ[:, 1])):
                for t in range(4):
                    pe.transpose(bank(2 * k, P, off=P * t), src[:, t, :], IDENT)
                ins = pe.transpose(bank(2 * k + 1, TS), src[0:TS, 4, :], CST[0:TS, 0, 0:TS])
            ins.then_inc(S["gt_done"], 1)
            pe.wait_ge(S["gt_evac"], 1)
            with pe.Fori(0, NPG) as g:
                for q in range(PG // 4):
                    n = g * (PG // 4) + q
                    pe.wait_ge(S["pa_ready"], n + 1)
                    pe.wait_ge(S["pbank_free"], n + 1)
                    for k in range(4):
                        ins = mm(bank(4 + q % 2, P, off=P * k), BB[:, q % 2, k, :], AA[:, q % 2, k, :],
                                 start=True, stop=True, skip_group_check=True)
                    ins.then_inc(S["p_mm"], 1)

            def up(n, m):
                for e in range(2):
                    projection(n + 2 * e, m + e, e, 2 * e)

            def down(n, v, w, par):
                pe.wait_ge(S["ww_ready"], w)
                for dh in range(2):
                    for e in range(2):
                        pe.wait_ge(S["split_done"], n + (2 * dh + e + 1))
                    for d8 in range(8):
                        d = 8 * dh + d8
                        pe.wait_ge(S["v_free"], v + (d + 1))
                        for e in range(2):
                            for vp, wp in ((0, 0), (0, 1), (1, 0)):
                                for ch in range(2):
                                    ins = mm(bank(4 + 2 * (d % 2) + ch, HALF), WS[:, 2 * dh + e, vp, P * d8:P * (d8 + 1)],
                                             WW[:, par, e, wp, ch * HALF:(ch + 1) * HALF],
                                             start=e == 0 and (vp, wp) == (0, 0), stop=e == 1 and vp == 1,
                                             skip_group_check=True)
                        if d8 < 7:
                            ins.then_inc(S["v_done"], 1)
                    ins.then_inc(S["used"], 2)

            up(H_END, B_WQ + 16)
            with pe.Fori(0, NK // 4 - 1) as i:
                for s in range(2):
                    up(i * 16 + (H_END + 4 + 8 * s), i * 4 + (B_WQ + 18 + 2 * s))
                    down(i * 16 + (H_END + 8 + 8 * s), i * 32 + 16 * s, i * 4 + (2 * s + 2), s)
            n = H_END + 16 * (NK // 4 - 1)
            up(n + 4, B_WQ + 16 + NK - 2)
            down(n + 8, 16 * (NK // 2 - 2), NK - 2, 0)
            down(n + 12, 16 * (NK // 2 - 1), NK, 1)
            norm_sum(4)

        @block.scalar
        def _(act):
            step = Steps(act, S["act_step"])
            copy = lambda out, in_, **kw: act.activation(out, in_, ACT.Identity, **kw)
            act.sem_inc(S["lin_evac"], 2)
            act.sem_inc(S["pbank_free"], 2)
            act.wait_ge(S["in_const"], 64)

            def squares(k, x, n=T):
                for b in range(KB):
                    if k or b >= 2:
                        act.wait_ge(S["sq_used"], 16 * k + max(b - 1, 0))
                    act.activation(NSQ[:, b % 2, 0:n], x[:, b, :], ACT.Square).then_inc(S["sq_ready"], 1)

            def root(k, n=T):
                act.wait_ge(S["var_ready"], k + 1)
                act.activation(NRS[:, 0:n], NVAR[:, 0:n], ACT.Sqrt).then_inc(S["sd_ready"], 1)

            def highs(t, hi, n=T):
                for b in range(KB):
                    act.wait_ge(S["t_ready"], t + b + 1)
                    copy(HL[:, 0, b, 0:n], NT[:, b % 3, 0:n]).then_inc(S["hi_ready"], 1)

            def load_split(src, r, lo):
                def load(b):
                    if b >= 3:
                        act.wait_ge(S["lo_ready"], lo + b - 2)
                    act.dma_start(NT[:, b % 3, :], src[b]).then_inc(S[f"in_t{b % 3}"], 16)
                for b in range(3):
                    load(b)
                for b in range(KB):
                    act.wait_ge(S[f"in_t{b % 3}"], 16 * (r * (6 if b % 3 == 0 else 5) + b // 3 + 1))
                    copy(HL[:, 0, b, :], NT[:, b % 3, :]).then_inc(S["hi_ready"], 1)
                    if b >= 1 and b + 2 < KB:
                        load(b + 2)

            act.wait_ge(S["in_mem"], 16)
            squares(0, XM, MEM)
            root(0, MEM)
            highs(0, 0, MEM)
            act.wait_ge(S["lo_ready"], 16)
            act.dma_start(X, xT.rearrange("k p t -> p k t")).then_inc(S["in_x"], 16)
            act.wait_ge(S["in_x"], 16)
            squares(1, X)
            with act.Fori(0, 8) as i:
                for s in range(2):
                    act.wait_ge(S["used"], i * 4 + used(2 * s + 2))
                    act.wait_ge(S[f"out_k{s}"], i * 16)
                    copy(KST[:, s, :], bank(2 * s, MEM)).then_inc(S["lin_evac"], 1)
                    act.wait_ge(S["lin_evac"], i * 2 + (B_MK + s + 3))
                    act.dma_start(mkT[bass.ds(i * 2 + s, 1)].rearrange("a p m -> p (a m)"), KST[:, s, :])\
                        .then_inc(S[f"out_k{s}"], 16)
            with act.Fori(0, 2) as i:
                for s in range(2):
                    act.wait_ge(S["used"], i * 16 + used(H_MV + 8 * s + 8))
                    act.wait_ge(S[f"out_v{s}"], i * 16)
                    copy(VST[:, s, :], PS[:, 1024 * s:1024 * s + 1024]).then_inc(S["lin_evac"], 1)
                    act.wait_ge(S["lin_evac"], i * 2 + (B_MV + s + 3))
                    act.dma_start(mv.rearrange("(m p) n -> p m n", p=P)[:, :, bass.ts(i * 2 + s, 512)],
                                  VST[:, s, :].rearrange("p (m n) -> p m n", m=2)).then_inc(S[f"out_v{s}"], 16)
            root(1)
            highs(16, 16)
            act.wait_ge(S["lo_ready"], 32)
            for g in range(GROUPS):
                if g:
                    act.wait_ge(S["pool_mm"], g)
                    act.wait_ge(S["pool_d"], g)
                    act.wait_ge(S["out_pool"], 64 * g)
                act.dma_start(PW, pool_w[g].rearrange("(c p) d -> p c d", p=P)).then_inc(S["in_pw"], 16)
                for c in range(2):
                    act.dma_start(PSX[:, c, :, 0:BUF], spoolT[2 * g + c]).then_inc(S["in_pool"], 16)
                if g == 0:
                    act.wait_ge(S["x_added"], 1)
                for c in range(2):
                    act.wait_ge(S["used"], used(H_POOL + 4 * g + 2 * c + 2))
                    copy(PEX[:, c, BUF:BUF + HALF], bank(2 * c, HALF))
                    copy(PEX[:, c, BUF + HALF:BUF + TP], bank(2 * c + 1, TP - HALF))
                    copy(PSX[:, c, :, BUF:BUF + SQ],
                         bank(2 * c + 1, TS, off=TP - HALF).rearrange("p (b q) -> p b q", b=SB)).then_inc(S["lin_evac"], 1)
                act.wait_ge(S["lin_evac"], B_POOL + 2 * g + 4)
                act.wait_ge(S["in_pool"], 32 * (g + 1))
                for c in range(2):
                    act.dma_start(npoolT_p[2 * g + c], PEX[:, c, TP:TP + BUF]).then_inc(S["out_pool"], 16)
                    act.dma_start(npoolT_s[2 * g + c], PSX[:, c, :, SQ:SQ + BUF]).then_inc(S["out_pool"], 16)
                act.wait_ge(S["pool_mm"], g + 1)
                if g:
                    act.wait_ge(S["out_a"], 16 * g)
                for o in range(2):
                    ins = copy(halves(AT[:, o, :]), pair(2 + o), scale=GAINS[:, G_POOLS + 2 * g + o:G_POOLS + 2 * g + o + 1])
                ins.then_inc(S["pool_evac"], 1)
                act.wait_ge(S["pool_evac"], g + 1)
                act.dma_start(mixT[2 * g:2 * g + 2].rearrange("k p t -> p k t"), AT).then_inc(S["out_a"], 16)
            act.wait_ge(S["pool_d"], GROUPS)
            act.wait_ge(S["out_pool"], 64 * GROUPS)
            act.wait_ge(S["out_a"], 16 * GROUPS)
            for s in range(2):
                act.wait_ge(S[f"out_k{s}"], 128)
                act.wait_ge(S[f"out_v{s}"], 32)
            with act.Fori(0, RH) as h:
                act.wait_ge(S["b_done"], h)
                act.wait_ge(S["out_sst"], h * 128)
                act.dma_start(TAB, tabs[bass.ds(h, 1)].rearrange("a p n -> p (a n)")).then_inc(S["in_tab"], 16)
                for b in range(SB):
                    act.dma_start(SST[:, b], sret[b, bass.ds(h, 1)].rearrange("a (c p) v -> p (a c) v", p=P))\
                        .then_inc(S["in_st"], 16)
                act.wait_ge(S["out_b"], h * 16)
                act.wait_ge(S["out_spr"], h * 16)
                for m in range(8):
                    act.wait_ge(S["used"], h * 16 + used(H_RET + 2 * m + 2))
                    kw = {"scale": RD ** -0.5} if m in (2, 3) else {}
                    act.activation(halves(RAWQ[:, m, :]), pair(m % 2), ACT.Silu if m >= 6 else ACT.Identity, **kw)\
                        .then_inc(S["lin_evac"], 1)
                act.wait_ge(S["vt_done"], h + 1)
                copy(VTOK[:, 0:4, :], PS[:, 2048:3072].rearrange("p (t n) -> p t n", t=4))
                copy(VTOK[0:TS, 4, :], bank(6, RD, TS)).then_inc(S["v_evac"], 1)
                act.wait_ge(S["kt_done"], h + 1)
                act.wait_ge(S["in_tab"], h * 16 + 16)
                for t in range(4):
                    copy(KTOK[:, t, :], PS[:, 2048 + RD * t:2048 + RD * (t + 1)], scale=TAB[:, T_ZETA + t:T_ZETA + t + 1])
                copy(KTOK[0:TS, 4, :], bank(6, RD, TS)).then_inc(S["k_evac"], 1)
                act.wait_ge(S["o_done"], h * 2 + 1)
                copy(OT[:, :, 0:TP], PS[:, 2048:3072].rearrange("p (c n) -> p c n", c=2))
                copy(OT[:, :, TP:T], bank(6, 2 * TS).rearrange("p (c n) -> p c n", c=2)).then_inc(S["o_evac"], 1)
                act.wait_ge(S["o_done"], h * 2 + 2)
                copy(SPR, bank(7).rearrange("p (c n) -> p c n", c=2)).then_inc(S["spr_evac"], 1)
                act.wait_ge(S["spr_evac"], h + 1)
                act.dma_start(nret_p[bass.ds(h, 1)].rearrange("a (c p) v -> p (a c) v", p=P), SPR).then_inc(S["out_spr"], 16)
                for b in range(SB):
                    act.wait_ge(S["sst_new"], h * SB + (b + 1))
                    act.dma_start(nret_s[b, bass.ds(h, 1)].rearrange("a (c p) v -> p (a c) v", p=P), SST[:, b])\
                        .then_inc(S["out_sst"], 16)
                act.wait_ge(S["rvar_ready"], h + 1)
                act.activation(RVAR, RVAR, ACT.Sqrt).then_inc(S["rsd_ready"], 1)
                act.wait_ge(S["b_done"], h + 1)
                act.dma_start(mixT[bass.ds(h * 2 + 8, 2)].rearrange("k p t -> p k t"), OT).then_inc(S["out_b"], 16)
            act.wait_ge(S["out_sst"], 128 * RH)
            act.wait_ge(S["out_spr"], 16 * RH)
            act.wait_ge(S["out_b"], 16 * RH)

            act.dma_start(X, xT.rearrange("k p t -> p k t")).then_inc(S["in_x"], 16)
            load_split(mixT, 0, 32)
            act.wait_ge(S["x_added"], 17)
            act.dma_start(x2T.rearrange("k p t -> p k t"), X).then_inc(S["out_x"], 16)
            squares(2, X)
            root(2)
            highs(32, 48)
            act.wait_ge(S["lo_ready"], 64)
            act.wait_ge(S["out_x"], 16)

            with act.Fori(0, MH) as h:
                act.wait_ge(S["ks_used"], h * SB + 4)
                for m in range(4):
                    act.wait_ge(S["used"], h * 8 + used(H_MQ + 2 * m + 2))
                    copy(halves(QM[:, m, :]), pair(m % 2)).then_inc(S["lin_evac"], 1)
                act.wait_ge(S["mx_done"], h + 1)
                for t in range(TILES):
                    w = P if t < 4 else TS
                    ins = act.activation(PR[0:w, t, :], PS[0:w, 2048 + MEM * t:2048 + MEM * (t + 1)], ACT.Exp,
                                         bias=NMX[0:w, t:t + 1], scale=MD ** -0.5, accum_out=SM[0:w, t:t + 1])
                ins.then_inc(S["p_exp"], 1)
                act.wait_ge(S["pt_done"], h + 1)
                copy(PT[:, :, 0:TP], PS[:, 2048:3072].rearrange("p (m n) -> p m n", m=2))
                copy(PT[:, :, TP:T], bank(6, 2 * TS).rearrange("p (m n) -> p m n", m=2)).then_inc(S["pt_evac"], 1)
                act.wait_ge(S["vs_used"], h * SB + (SB + 2))
                act.wait_ge(S["out_om"], h * 16)
                copy(OB[:, :, 0:TP], PS[:, 2048:4096].rearrange("p (c n) -> p c n", c=4))
                copy(OB[:, :, TP:T], bank(0, 4 * TS).rearrange("p (c n) -> p c n", c=4)).then_inc(S["om_evac"], 1)
                act.wait_ge(S["om_evac"], h + 1)
                act.dma_start(omT[bass.ts(h, 4)].rearrange("k p t -> p k t"), OB).then_inc(S["out_om"], 16)
            act.wait_ge(S["out_om"], 16 * MH)
            act.dma_start(X, x2T.rearrange("k p t -> p k t")).then_inc(S["in_x"], 16)
            load_split(omT, 1, 64)
            act.wait_ge(S["x_added"], 33)
            act.dma_start(x3T.rearrange("k p t -> p k t"), X).then_inc(S["out_x"], 16)
            squares(3, X)
            root(3)
            highs(48, 80)
            act.wait_ge(S["lo_ready"], 96)
            act.wait_ge(S["out_x"], 32)

            act.dma_start(SK, subk).then_inc(S["in_sub"], 16)
            act.wait_ge(S["x_added"], 34)
            with act.Fori(0, EH) as h:
                act.wait_ge(S["sk_done"], h)
                for c in range(2):
                    act.wait_ge(S["used"], h * 4 + used(H_WQ + 2 * c + 2))
                    copy(halves(QP[:, c, :]), pair(c)).then_inc(S["lin_evac"], 1)
                act.wait_ge(S["sk_done"], h + 1)
                act.wait_ge(S["cand_done"], h)
                copy(SC[:, :, 0:4, :].rearrange("p c t n -> p c (t n)"),
                     PS[:, 2048:4096].rearrange("p (c n) -> p c n", c=2)[:, :, 0:512])
                copy(SC[0:TS, :, 4, :], PS[0:TS, 2048:4096].rearrange("p (c n) -> p c n", c=2)[:, :, 512:512 + NK])\
                    .then_inc(S["sc_evac"], 1)
            act.wait_ge(S["soft_in"], 1)
            act.activation(CAND.rearrange("p t n -> p (t n)")[:, 0:640], EQ.rearrange("p a n -> p (a n)")[:, 0:640], ACT.Exp)\
                .then_inc(S["soft_exp"], 1)
            act.wait_ge(S["gt_done"], 1)
            for k in range(3):
                copy(GIJ[:, k, 0:TP], bank(2 * k))
                ins = copy(GIJ[:, k, TP:T], bank(2 * k + 1, TS))
            ins.then_inc(S["gt_evac"], 1)
            with act.Fori(0, NPG // 2) as g:
                for par in range(2):
                    act.wait_ge(S[f"out_p{par}"], g * 16)
                    for q in range(PG // 4):
                        n = g * (PG // 2) + (par * (PG // 4) + q)
                        act.wait_ge(S["p_mm"], n + 3)
                        copy(STG[:, par, :, 4 * q:4 * q + 4].rearrange("p i t -> p t i"),
                             bank(4 + q % 2).rearrange("p (t i) -> p t i", t=4)).then_inc(S["pbank_free"], 1)
                    act.wait_ge(S["pbank_free"], n + 3)
                    act.dma_start(pmap[bass.ds(g * 2 + par, 1)].rearrange("a p n -> p (a n)"),
                                  STG[:, par].rearrange("p i t -> p (i t)")).then_inc(S[f"out_p{par}"], 16)
            for par in range(2):
                act.wait_ge(S[f"out_p{par}"], 16 * (NPG // 2))
            act.dma_start(X, x3T.rearrange("k p t -> p k t")).then_inc(S["in_x"], 16)

            def load_p(pr, par):
                act.dma_start(PP[:, par].rearrange("p g e t -> p g (e t)"),
                              pmap.rearrange("g p n -> p g n")[:, :, bass.ts(pr, 2 * PG)]).then_inc(S[f"in_p{par}"], 16)

            def expert_pair(pr, n, w, par, more=True):
                for e in range(2):
                    act.wait_ge(S["used"], n + used(2 * e + 2))
                    act.wait_ge(S["ww_ready"], w + (e - 1))
                    act.activation(halves(GE[:, e, :]), pair(e), ACT.Gelu).then_inc(S["lin_evac"], 1)
                    act.wait_ge(S["w_done"], w + (e + 1))
                    copy(WW[:, par, e, 0, :], GE[:, e, :]).then_inc(S["whi_done"], 1)
                if more:
                    load_p(pr + 2, par)

            load_p(0, 0)
            load_p(1, 1)
            for e in range(2):
                act.wait_ge(S["used"], used(H_END + 2 * e + 2))
                act.activation(halves(GE[:, e, :]), pair(e), ACT.Gelu).then_inc(S["lin_evac"], 1)
                act.wait_ge(S["w_done"], e + 1)
                copy(WW[:, 0, e, 0, :], GE[:, e, :]).then_inc(S["whi_done"], 1)
            load_p(2, 0)
            with act.Fori(0, NK // 4 - 2) as i:
                for s in range(2):
                    expert_pair(i * 2 + (1 + s), i * 16 + (H_END + 4 + 8 * s), i * 4 + (2 + 2 * s), 1 - s)
            for pr in range(NK // 2 - 3, NK // 2):
                expert_pair(pr, H_END + 8 * pr - 4, 2 * pr, pr % 2, more=pr + 2 < NK // 2)

            act.wait_ge(S["x_added"], 35)
            squares(4, X)
            root(4)
            for b in range(KB):
                act.wait_ge(S["t_ready"], 64 + b + 1)
                act.dma_start(yT[b], NT[:, b % 3, :]).then_inc(S[f"out_y{b % 3}"], 16)
            for k in range(3):
                act.wait_ge(S[f"out_y{k}"], 16 * (6 if k == 0 else 5))

        @block.vector
        def _(dve):
            step = Steps(dve, S["dve_step"])
            link = step.link
            tt, ts, stt = dve.tensor_tensor, dve.tensor_scalar, dve.scalar_tensor_tensor
            dve.sem_inc(S["v_free"], 2)
            dve.wait_ge(S["in_const"], 64)

            def rstd(k, n=T):
                for b in range(KB):
                    dve.wait_ge(S["sq_ready"], 16 * k + b + 1)
                    if b:
                        dve.wait_ge(S["sq_used"], 16 * k + b)
                        tt(NACC[:, 0:n], NACC[:, 0:n], NSQ[:, b % 2, 0:n], ALU.add).then_inc(S["sq_used"], 1)
                    else:
                        dve.tensor_copy(NACC[:, 0:n], NSQ[:, 0, 0:n]).then_inc(S["sq_used"], 1)
                dve.wait_ge(S["sum_done"], k + 1)
                if n == T:
                    ts(halves(NVAR), pair(3), EPS, None, ALU.add).then_inc(S["var_ready"], 1)
                else:
                    ts(NVAR[:, 0:n], bank(6, n), EPS, None, ALU.add).then_inc(S["var_ready"], 1)
                dve.wait_ge(S["sd_ready"], k + 1)
                link(dve.reciprocal(NVAR[:, 0:n], NRS[:, 0:n]))

            def normed(k, x, gain, n=T, lo=None, free=None):
                def low(b):
                    dve.wait_ge(S["hi_ready"], lo + b + 1)
                    tt(HL[:, 1, b, 0:n], NT[:, b % 3, 0:n], HL[:, 0, b, 0:n].bitcast(F32), ALU.subtract)\
                        .then_inc(S["lo_ready"], 1)
                for b in range(KB):
                    if free and b >= 3:
                        dve.wait_ge(S[f"out_y{b % 3}"], 16 * (b // 3))
                    if lo is not None and b >= 3:
                        dve.wait_ge(S["lo_ready"], lo + b - 2)
                    stt(NT[:, b % 3, 0:n], x[:, b, :], GAINS[:, gain + b:gain + b + 1], NVAR[:, 0:n], ALU.mult, ALU.mult)\
                        .then_inc(S["t_ready"], 1)
                    if lo is not None and b >= 1:
                        low(b - 1)
                if lo is not None:
                    low(KB - 1)

            def lows(lo):
                for b in range(KB):
                    dve.wait_ge(S["hi_ready"], lo + b + 1)
                    tt(HL[:, 1, b, :], NT[:, b % 3, :], HL[:, 0, b, :].bitcast(F32), ALU.subtract)\
                        .then_inc(S["lo_ready"], 1)

            rstd(0, MEM)
            normed(0, XM, G_SRC, MEM, lo=0)
            rstd(1)
            dve.wait_ge(S["used"], used(H_POOL))
            normed(1, X, G_MIX, lo=16)
            dve.wait_ge(S["lo_ready"], 32)
            dve.memset(PEX[:, :, 0:BUF], 0.0).then_inc(S["x_added"], 1)
            for g in range(GROUPS):
                w = 2 << g
                if g:
                    dve.wait_ge(S["pool_d"], g)
                dve.wait_ge(S["lin_evac"], B_POOL + 2 * g + 4)
                dve.wait_ge(S["in_pool"], 32 * (g + 1))
                src, ssrc, other = PEX, PSX, [(PTA, PSA), (PTB, PSB)]
                lo = 0
                for s in range(g + 1):
                    sh = 1 << s
                    lo += sh
                    dst, sdst = other[s % 2]
                    tt(dst[:, :, lo:], src[:, :, lo:], src[:, :, lo - sh:BUF + TP - sh], ALU.add)
                    link(tt(sdst[:, :, :, lo:], ssrc[:, :, :, lo:], ssrc[:, :, :, lo - sh:BUF + SQ - sh], ALU.add))
                    src, ssrc = dst, sdst
                if g:
                    dve.wait_ge(S["pool_mm"], g)
                link(stt(DT[:, :, 0:TP], src[:, :, BUF:], 1.0 / w, PEX[:, :, BUF:], ALU.mult, ALU.subtract))
                tmp = other[(g + 1) % 2][0][:, :, 0:w - 1]
                link(tt(tmp, src[:, :, BUF:BUF + w - 1], RC[:, 0:w - 1].unsqueeze(1).to_broadcast([P, 2, w - 1]), ALU.mult))
                tt(DT[:, :, 0:w - 1], tmp, PEX[:, :, BUF:BUF + w - 1], ALU.subtract)
                for c in range(2):
                    ins = stt(DT[:, c, TP:T].rearrange("p (b q) -> p b q", b=SB), ssrc[:, c, :, BUF:], 1.0 / w,
                              PSX[:, c, :, BUF:], ALU.mult, ALU.subtract)
                ins.then_inc(S["pool_d"], 1)
            dve.wait_ge(S["pool_d"], GROUPS)
            dve.wait_ge(S["pool_mm"], GROUPS)
            dve.wait_ge(S["out_a"], 16 * GROUPS)
            dve.wait_ge(S["out_pool"], 64 * GROUPS)
            cos, sin = CS[:, 0, :], CS[:, 1, :]
            with step.loop(RH, 11) as h:
                dve.wait_ge(S["lin_evac"], h * 8 + (B_RET + 4 + 2))
                for r, x1, x2 in ((RQ, RAWQ[:, 0], RAWQ[:, 1]), (RK, RAWQ[:, 2], RAWQ[:, 3])):
                    for o, a, b, op in ((0, cos, sin, ALU.subtract), (1, sin, cos, ALU.add)):
                        tt(r[:, o, :], x1, a, ALU.mult)
                        link(tt(RT[:, o, :], x2, b, ALU.mult))
                        ins = tt(r[:, o, :], r[:, o, :], RT[:, o, :], op)
                    link(ins)
                dve.sem_inc(S["rot_done"], 1)
                dve.wait_ge(S["in_tab"], h * 16 + 16)
                tt(QX, RQ[:, :, TP:T], TAB[:, T_XI:T_XI + TS].unsqueeze(1).to_broadcast([P, 2, TS]), ALU.mult)\
                    .then_inc(S["qx_done"], 1)
                dve.wait_ge(S["k_evac"], h + 1)
                for b in range(SB):
                    ins = ts(KM[:, b, :], KTOK[0:TS, 4, :], TAB[0:TS, T_ZETAS + b:T_ZETAS + b + 1], None, ALU.mult)
                ins.then_inc(S["km_done"], 1)
                dve.wait_ge(S["qk_done"], h + 1)
                for j in range(4):
                    tt(INNER[j], bank(4 + j, TP - P * j), TAB[:, T_DEC:T_DEC + TP - P * j], ALU.mult)
                tt(INNERS, bank(7, TS, TS, 256), TAB[0:TS, T_DECS:T_DECS + TS], ALU.mult).then_inc(S["inner_done"], 1)
                dve.wait_ge(S["o_evac"], h + 1)
                dve.wait_ge(S["mean_done"], h + 1)
                for c in range(2):
                    ins = tt(halves(OT[:, c, :]), halves(OT[:, c, :]), pair(3), ALU.subtract)
                link(ins)
                tt(SQD, OT, OT, ALU.mult).then_inc(S["sqd_ready"], 1)
                for b in range(SB):
                    dve.wait_ge(S["ks_mm"], h * SB + (b + 1))
                    stt(SST[:, b], SST[:, b], TAB[:, T_G8:T_G8 + 1], bank(4 + b % 2).rearrange("p (c n) -> p c n", c=2),
                        ALU.mult, ALU.add).then_inc(S["sst_new"], 1)
                dve.wait_ge(S["rvar_done"], h + 1)
                ts(halves(RVAR), pair(3), EPS, None, ALU.add).then_inc(S["rvar_ready"], 1)
                dve.wait_ge(S["rsd_ready"], h + 1)
                link(dve.reciprocal(RVAR, RVAR))
                gr = GAINS[:, bass.ds(h * 2 + G_RET, 2)]
                for c in range(2):
                    ins = tt(OT[:, c, :], OT[:, c, :], RVAR, ALU.mult)
                link(ins)
                link(tt(OT, OT, wide(gr, T), ALU.mult))
                link(tt(OT, OT, RAWQ[:, 6:8, :], ALU.mult))
                dve.sem_inc(S["b_done"], 1)

            def add_residual(first):
                for n in range(KB):
                    dve.wait_ge(S["used"], used(first + 2 * n + 2))
                    tt(halves(X[:, n, :]), halves(X[:, n, :]), pair(n % 2), ALU.add).then_inc(S["x_added"], 1)
                    dve.wait_ge(S["x_added"], (1 if first == H_OUT else 17) + n + 1)
                    dve.sem_inc(S["lin_evac"], 1)

            lows(32)
            dve.wait_ge(S["in_x"], 32)
            add_residual(H_OUT)
            rstd(2)
            normed(2, X, G_MEM, lo=48)
            dve.wait_ge(S["lo_ready"], 64)
            dve.wait_ge(S["out_x"], 16)
            dve.memset(AR[:, 17280:17300], 1.0)
            link(dve.memset(QZ, 0.0))
            with step.loop(MH, 3) as h:
                dve.wait_ge(S["lin_evac"], h * 4 + (B_MQ + 4 + 2))
                for b in range(SB):
                    ins = dve.tensor_copy(QZ[:, b, :, SQ * b:SQ * (b + 1)], QM[:, :, TP + SQ * b:TP + SQ * (b + 1)])
                ins.then_inc(S["qz_done"], 1)
                dve.wait_ge(S["ks_used"], h * SB + (SB + 4))
                dve.tensor_reduce(MX[:, 0:4], PS[:, 2048:3072].rearrange("p (t n) -> p t n", t=4), AX.X, ALU.max)
                link(dve.tensor_reduce(MX[0:TS, 4:5], bank(6, MEM, TS), AX.X, ALU.max))
                ts(NMX, MX, -(MD ** -0.5), None, ALU.mult).then_inc(S["mx_done"], 1)
                dve.wait_ge(S["p_exp"], h + 1)
                link(dve.reciprocal(RSM, SM))
                for t in range(TILES):
                    w = P if t < 4 else TS
                    ins = ts(PR[0:w, t, :], PR[0:w, t, :], RSM[0:w, t:t + 1], None, ALU.mult)
                link(ins)
                dve.sem_inc(S["p_done"], 1)
            lows(64)
            dve.wait_ge(S["in_x"], 48)
            add_residual(H_MO)
            rstd(3)
            normed(3, X, G_FFN, lo=80)

            dve.wait_ge(S["lo_ready"], 96)
            dve.wait_ge(S["out_x"], 32)
            dve.memset(AR[:, 1152:2912], 0.0).then_inc(S["x_added"], 1)
            dve.wait_ge(S["x_added"], 34)

            def top16(items):
                def holds():
                    dve.sem_inc(S["waited_v"], 1)

                holds()
                for vals, sv, _ in items:
                    ins = dve.max(sv[:, 0:8], vals)
                link(ins)
                holds()
                for vals, sv, si in items:
                    ins = dve.max_index(si[:, 0:8], sv[:, 0:8], vals)
                link(ins)
                holds()
                for vals, sv, _ in items:
                    ins = dve.match_replace(vals, sv[:, 0:8], vals, LOWEST)
                link(ins)
                holds()
                for vals, sv, _ in items:
                    ins = dve.max(sv[:, 8:16], vals)
                link(ins)
                holds()
                for vals, sv, si in items:
                    ins = dve.max_index(si[:, 8:16], sv[:, 8:16], vals)
                link(ins)

            with step.loop(EH, 16) as h:
                dve.wait_ge(S["sc_evac"], h + 1)
                top16([(SC[:, c, t, :], SV[:, c, t, :], SI[:, c, t, :]) for c in range(2) for t in range(TILES)])
                dve.sem_inc(S["cand_done"], 1)
                dve.tensor_copy(SIF, SI)
                for t in range(TILES):
                    ins = tt(CAND[:, t, :].rearrange("p (a b) -> p a b", a=TOPK), wide(SV[:, 0, t, :], TOPK),
                             SV[:, 1, t, :].unsqueeze(1).to_broadcast([P, TOPK, TOPK]), ALU.add)
                link(ins)
                top16([(CAND[:, t, :], TV[:, t, :], TI[:, t, :]) for t in range(TILES)])
                ti = TI.rearrange("p t k -> p (t k)")
                ts(TA[:, 0, :], ti, 4, None, ALU.logical_shift_right)
                link(ts(TA[:, 1, :], ti, 15, None, ALU.bitwise_and))
                link(dve.tensor_copy(TAF, TA))
                dve.tensor_copy(GS[:, :, bass.ts(h, TOPK)], TV)
                iota16 = IOTA[:, 0:TOPK].unsqueeze(1).to_broadcast([P, TILES * TOPK, TOPK])
                for c, eq in ((0, EQ), (1, EQ2)):
                    ins = tt(eq, wide(TAF[:, c, :], TOPK), iota16, ALU.is_equal)
                link(ins)
                for c, eq in ((0, EQ), (1, EQ2)):
                    for t in range(TILES):
                        v = eq[:, TOPK * t:TOPK * (t + 1), :]
                        ins = tt(v, v, SIF[:, c, t, :].unsqueeze(1).to_broadcast([P, TOPK, TOPK]), ALU.mult)
                link(ins)
                for c, eq in ((0, EQ), (1, EQ2)):
                    ins = dve.tensor_reduce(IJ[:, c, :, bass.ts(h, TOPK)], eq.rearrange("p (t k) a -> p t k a", t=TILES),
                                            AX.X, ALU.add)
                link(ins)
            gs3 = GS.rearrange("p t (h k) -> p (t h) k", k=TOPK)
            eq3 = EQ[:, 0:TILES * EH, :]
            ex3 = CAND.rearrange("p t n -> p (t n)")[:, 0:640].rearrange("p (a k) -> p a k", k=TOPK)
            tt(eq3, gs3, gs3[:, :, 0:1].to_broadcast([P, TILES * EH, TOPK]), ALU.subtract).then_inc(S["soft_in"], 1)
            dve.wait_ge(S["soft_exp"], 1)
            link(dve.tensor_reduce(SMX, ex3, AX.X, ALU.add))
            link(dve.reciprocal(SMX, SMX))
            tt(gs3, ex3, wide(SMX, TOPK), ALU.mult).then_inc(S["soft_done"], 1)
            dve.wait_ge(S["gt_evac"], 1)
            with dve.Fori(0, NPG) as g:
                for q in range(PG // 4):
                    dve.wait_ge(S["p_mm"], g * (PG // 4) + (q + 1))
                    for k in range(4):
                        t = g * PG + (4 * q + k)
                        ins = ts(AA[:, q % 2, k, :], IOTA, GIJ[:, 1, bass.ds(t, 1)], GIJ[:, 0, bass.ds(t, 1)],
                                 ALU.is_equal, ALU.mult)
                    tt(BB[:, q % 2], IOTA.unsqueeze(1).to_broadcast([P, 4, P]),
                       wide(GIJ[:, 2, bass.ds(g * PG + 4 * q, 4)], P), ALU.is_equal).then_inc(S["pa_ready"], 1)

            def weigh(w, par, loads):
                dve.wait_ge(S[f"in_p{par}"], loads)
                for e in range(2):
                    dve.wait_ge(S["lin_evac"], w + (B_WQ + 16 + 2 + e + 1))
                    ge = GE[:, e, :].rearrange("p (g t) -> p g t", t=PG)
                    tt(ge, ge, PP[:, par, :, e, :], ALU.mult).then_inc(S["w_done"], 1)
                    dve.wait_ge(S["whi_done"], w + (e + 1))
                    tt(WW[:, par, e, 1, :], GE[:, e, :], WW[:, par, e, 0, :].bitcast(F32), ALU.subtract)\
                        .then_inc(S["ww_ready"], 1)

            def accumulate(v, n):
                for d in range(KB):
                    if d % 8 < 7:
                        dve.wait_ge(S["v_done"], v + (d + 1 - d // 8))
                    else:
                        dve.wait_ge(S["used"], n + used(2 * (d // 8) + 2))
                    tt(halves(X[:, d, :]), halves(X[:, d, :]), pair(2 + d % 2), ALU.add).then_inc(S["v_free"], 1)

            weigh(0, 0, 16)
            dve.wait_ge(S["in_x"], 64)
            with dve.Fori(0, NK // 4 - 1) as i:
                for s in range(2):
                    weigh(i * 4 + (2 + 2 * s), 1 - s, i * 16 + (16 if s == 0 else 32))
                    accumulate(i * 28 + 14 * s, i * 16 + (H_END + 8 + 8 * s))
            weigh(NK - 2, 1, 16 * (NK // 4))
            accumulate(14 * (NK // 2 - 2), H_END + 4 * NK - 8)
            accumulate(14 * (NK // 2 - 1), H_END + 4 * NK - 4)
            dve.wait_ge(S["v_free"], 2 + 8 * NK)
            dve.sem_inc(S["x_added"], 1)
            rstd(4)
            normed(4, X, G_FIN, free=True)


def rotary_tables():
    half = RD // 2
    inv = (np.float32(1.0) / (np.float32(10000.0) ** (np.arange(half, dtype=np.float32) / np.float32(half)))).astype(np.float32)
    pos = np.concatenate([np.arange(TP), np.tile(PAST + np.arange(SQ), SB)]).astype(np.float32)
    ang = (inv[:, None] * pos[None, :]).astype(np.float32).astype(np.float64)
    return np.ascontiguousarray(np.stack([np.cos(ang), np.sin(ang)], 1).astype(np.float32))


def retention_tables():
    tab = np.zeros((RH, P, T_END), np.float32)
    lgs = np.log((1.0 - 2.0 ** (-5.0 - np.arange(RH))).astype(np.float32)).astype(np.float32)
    power = lambda lg, n: np.exp(np.float64(lg) * n).astype(np.float32)
    p, i = np.arange(P)[:, None], np.arange(TP)[None, :]
    s, q = np.arange(TS)[:, None], np.arange(TS)[None, :]
    for h in range(RH):
        lg = lgs[h]
        tab[h, :, T_DEC:T_DEC + TP] = np.where(i >= p, power(lg, np.maximum(i - p, 0)), 0.0)
        same = (s // SQ == q // SQ) & (q >= s)
        tab[h, :TS, T_DECS:T_DECS + TS] = np.where(same, power(lg, np.maximum(q - s, 0)), 0.0)
        tab[h, :, T_XI:T_XI + TS] = power(lg, np.arange(TS) % SQ + 1.0)[None]
        tab[h, :, T_ZETA:T_ZETA + 4] = power(lg, TP - 1.0 - (np.arange(4)[None] * P + p))
        tab[h, :TS, T_ZETAS:T_ZETAS + SB] = np.where(s // SQ == np.arange(SB)[None], power(lg, SQ - 1.0 - s % SQ), 0.0)
        tab[h, :, T_G8] = power(lg, float(SQ))
    return tab


def constants():
    c = np.zeros((P, 272), np.float32)
    c[:, 0:128] = np.eye(P)
    c[:, 128:256] = np.arange(P)[None]
    c[:, 256:272] = 1.0 / (np.arange(16) + 1.0)
    return c


def kernel(**inputs):
    import concourse.bacc as bacc
    from concourse.bass_utils import run_bass_kernel_spmd as run

    a = {k: np.asarray(v) for k, v in inputs.items()}

    def blocks(w):
        n = w.shape[1] // P
        return w.reshape(2, KB // 2, P, n, P).transpose(3, 0, 2, 1, 4).reshape(2 * n, P, HW)

    def blocks_wide(w):
        n = w.shape[1] // 512
        return w.reshape(KB // 2, 2, P, n, 512).transpose(3, 0, 2, 1, 4).reshape(8 * n, P, HW)

    w_in = blocks(a["w_in"][0])
    heads = [w_in[16:].reshape(4, RH, 4, P, HW)[:, h].reshape(16, P, HW) for h in range(RH)]
    w_lin = np.concatenate([blocks(a["w_mk"][0]), blocks_wide(a["w_mv"][0]), w_in[:16], *heads,
                            blocks(a["w_out"][0]), blocks(a["w_mq"][0]), blocks(a["w_mo"][0]), blocks(a["peer_wq"][0])])
    xs = np.concatenate([a["x_prompt"][0], a["x_sample"].reshape(TS, D)], 0)
    gains = np.concatenate([a[n].reshape(-1, P).T for n in
                            ("norm_mix_g", "norm_mem_g", "norm_memsrc_g", "norm_ffn_g", "norm_final_g",
                             "pool_scale", "ret_norm_g")], 1)
    arrays = {
        "xT": xs.T.reshape(KB, P, T),
        "memT": a["mem_prompt"][0].T.reshape(KB, P, MEM),
        "w_lin": w_lin,
        "gains": gains,
        "consts": constants(),
        "spoolT": a["state_pool"][0].transpose(2, 0, 1).reshape(8, P, SB, BUF),
        "sret": a["state_ret"][0],
        "kcT": a["cache_mem_k"][0].transpose(0, 2, 3, 1),
        "vc": a["cache_mem_v"][0].reshape(SB, MEM, D),
        "pool_w": a["pool_w"][0],
        "rot": rotary_tables(),
        "tabs": retention_tables(),
        "subk": a["peer_subkeys"][0].reshape(2 * EH, NK, P).transpose(2, 0, 1),
        "uT": a["peer_u"][0].reshape(NK, P, 2, KB // 2, P).transpose(0, 2, 4, 3, 1).reshape(2 * NK, P, HW),
        "vE": a["peer_v"][0].reshape(NK, P, D),
    }
    outs = {
        "yT": (KB, P, T), "npoolT_p": (8, P, BUF), "nret_p": (RH, RD, RD), "mkT": (KB, P, MEM), "mv": (MEM, D),
        "npoolT_s": (8, P, SB, BUF), "nret_s": (SB, RH, RD, RD),
    }
    nc = bacc.Bacc("TRN2", target_bir_lowering=False, num_devices=1)
    ins, args = {}, []
    for name, v in arrays.items():
        v = np.ascontiguousarray(v)
        ins[f"in_{name}"] = v
        args.append(nc.dram_tensor(f"in_{name}", v.shape, mybir.dt.from_np(v.dtype), kind="ExternalInput").ap())
    for name, shape in outs.items():
        args.append(nc.dram_tensor(f"out_{name}", shape, F32, kind="ExternalOutput").ap())
    build(nc, *args)
    r = run(nc, [ins], core_ids=[0]).results[0]
    o = {name: r[f"out_{name}"] for name in outs}
    y = o["yT"].reshape(D, T).T
    return (
        np.ascontiguousarray(y[:TP]).reshape(1, TP, D),
        np.ascontiguousarray(y[TP:]).reshape(SB, SQ, D),
        np.ascontiguousarray(o["npoolT_p"].reshape(1024, BUF).T).reshape(1, 1, BUF, 1024),
        o["nret_p"].reshape(1, 1, RH, RD, RD),
        np.ascontiguousarray(o["mkT"].reshape(D, MEM).T).reshape(1, 1, MEM, MH, MD),
        o["mv"].reshape(1, 1, MEM, MH, MD),
        np.ascontiguousarray(o["npoolT_s"].reshape(1024, SB, BUF).transpose(1, 2, 0)).reshape(1, SB, BUF, 1024),
        o["nret_s"].reshape(1, SB, RH, RD, RD),
    )
```

```python
from contextlib import ExitStack, contextmanager

import concourse.bass as bass
import numpy as np
from concourse import mybir

F32 = mybir.dt.float32
F32R = mybir.dt.float32r
U32 = mybir.dt.uint32
ACT = mybir.ActivationFunctionType
ALU = mybir.AluOpType
AX = mybir.AxisListType

P = 128
D = 2048
KB = D // P
TP = 512
SB, SQ = 8, 8
TS = SB * SQ
T = TP + TS
HALF = T // 2
PAST = 4096
MEM = 256
GROUPS = 4
BUF = 15
RH, RD = 4, 256
MH, MD = 4, 512
EH = 8
NK = 128
TOPK = 16
TILES = 5
EPS = 1e-6
LOWEST = -3.0e38
HW = 1024
PG = 32
NPG = T // PG

B_MK, B_MV, B_POOL, B_RET, B_OUT, B_MQ, B_MO, B_WQ = 0, 16, 20, 28, 60, 76, 92, 108
H_MV, H_POOL, H_RET, H_OUT, H_MQ, H_MO, H_WQ = 32, 64, 80, 144, 176, 208, 240
NP2 = NK // 2
LAG = EH + 1 + NPG // 2
H_TAIL = H_WQ + 8 * EH
H_P = H_TAIL + 4
H_UV = H_P + 2 * NPG
H_V = H_UV + 8 * (NP2 - LAG)
H_ALL = H_V + 4 * LAG
B_TAIL = B_WQ + 4 * EH
B_P = B_TAIL + 2
B_UV = B_P + NPG

G_MIX, G_MEM, G_SRC, G_FFN, G_FIN, G_POOLS, G_RET = 0, 16, 32, 48, 64, 80, 88
T_DEC, T_DECS, T_XI, T_ZETA, T_ZETAS, T_G8, T_END = 0, 512, 576, 640, 644, 652, 653


def used(n):
    return n + 4


def free(n):
    return n + 1


def split(n):
    return n + 3


class Steps:

    def __init__(self, eng, sem):
        self.eng, self.sem, self.base, self.count, self.i, self.per = eng, sem, 0, 0, None, 0

    def link(self, ins):
        ins.then_inc(self.sem, 1)
        self.count += 1
        at = self.base + self.count
        self.eng.wait_ge(self.sem, at if self.i is None else self.i * self.per + at)

    @contextmanager
    def loop(self, n, per):
        self.base, self.count, self.per = self.base + self.count, 0, per
        with self.eng.Fori(0, n) as i:
            self.i = i
            yield i
        assert self.count == per, (self.count, per)
        self.base, self.count, self.i = self.base + n * per, 0, None


def build(nc, xT, memT, w_lin, gains, consts, spoolT, sret, kcT, vc, pool_w, rot, tabs, subk, uT, vE,
          yT, npoolT_p, nret_p, mkT, mv, npoolT_s, nret_s):
    with ExitStack() as ctx:
        def sb(name, shape, dt=F32):
            return ctx.enter_context(nc.sbuf_tensor(name, shape, dt))

        def sem(name):
            return ctx.enter_context(nc.semaphore(name))

        def dram(name, shape):
            return nc.dram_tensor(name, shape, F32, kind="Internal").ap()

        mixT = dram("mixT", (KB, P, T))
        x2T = dram("x2T", (KB, P, T))
        omT = dram("omT", (KB, P, T))
        x3T = dram("x3T", (KB, P, T))
        pmap = dram("pmap", (NPG, P, NK * PG))
        gel = dram("gel", (NK, P, T))

        HL = sb("HL", [P, 2, KB, T], F32R)
        WS = sb("WS", [P, 4, 2, HW], F32R)
        WW = sb("WW", [P, 2, 2, 2, T], F32R)
        RAW = sb("RAW", [P, 2, HW])
        CS = sb("CS", [P, 2, T])
        CST = sb("CST", [P, 2, P])
        ONES = sb("ONES", [P, 2, P])
        GAINS = sb("GAINS", [P, 96])
        RC = sb("RC", [P, 16])
        AR = sb("AR", [P, 17440])
        PS = ctx.enter_context(nc.psum_tensor("PS", [P, 4096], F32))
        IDENT, IOTA = CST[:, 0, :], CST[:, 1, :]

        def ar(start, *dims, rows=P):
            n = int(np.prod(dims))
            v = AR[0:rows, start:start + n]
            if len(dims) == 1:
                return v
            names = "abcd"[:len(dims)]
            return v.rearrange(f"p ({' '.join(names)}) -> p {' '.join(names)}",
                               **{names[k]: dims[k] for k in range(1, len(dims))})

        def bank(b, n=512, rows=P, off=0):
            return PS[0:rows, 512 * b + off:512 * b + off + n]

        def pair(a):
            return PS[:, 1024 * a:1024 * a + 1024].rearrange("p (b n) -> p b n", b=2)[:, :, 0:HALF]

        def halves(v):
            return v.rearrange("p (b n) -> p b n", b=2)

        def wide(v, n):
            return v.unsqueeze(2).to_broadcast([v.shape[0], v.shape[1], n])

        X = ar(0, KB, T)
        N0 = KB * T
        NSQ, NACC, NVAR, NRS, NT = ar(N0, 2, T), ar(N0 + 1152, T), ar(N0 + 1728, T), ar(N0 + 2304, T), ar(N0 + 2880, 3, T)
        XM, KST, VST = ar(0, KB, MEM), ar(14000, 2, MEM), ar(14512, 2, 1024)
        PEX, PTA, PTB = ar(0, 2, BUF + TP), ar(1054, 2, BUF + TP), ar(2108, 2, BUF + TP)
        PSX, PSA, PSB = ar(3162, 2, SB, BUF + SQ), ar(3530, 2, SB, BUF + SQ), ar(3898, 2, SB, BUF + SQ)
        DT, AT, PW = ar(4266, 2, T), ar(5418, 2, T), ar(6570, 2, 256)
        RAWQ, RQ, RK = ar(0, 8, T), ar(4608, 2, T), ar(5760, 2, T)
        OT, SQD, RVAR, RSD = ar(0, 2, T), ar(5760, 2, T), ar(4608, T), ar(5184, T)
        INNER = [ar(1152 + o, TP - P * j) for j, o in enumerate((0, 512, 896, 1152))]
        VTOK, KTOK, KM = ar(6912, TILES, RD), ar(8192, TILES, RD), ar(9472, SB, RD, rows=TS)
        RT = ar(9472, 2, T)
        TAB, QX, SST = ar(11520, T_END), ar(12176, 2, TS), ar(12304, SB, 2, RD)
        SPR, INNERS = ar(16400, 2, RD), ar(16912, TS, rows=TS)
        QM, QZ, KT, VT = ar(0, 4, T), ar(2304, SB, 4, TS), ar(4352, 4, MEM), ar(5376, 2, MD)
        KS, VS = ar(6400, 4, 4, MEM), ar(10496, 2, 2, MD)
        PR, PT, OB = ar(12544, TILES, MEM), ar(13824, 2, T), ar(14976, 4, T)
        MX, NMX, SM, RSM = ar(17280, TILES), ar(17285, TILES), ar(17290, TILES), ar(17295, TILES)
        QP, SC, SV = ar(0, 2, T), ar(1152, 2, TILES, NK), ar(2432, 2, TILES, TOPK)
        SI, SIF = ar(2592, 2, TILES, TOPK).bitcast(U32), ar(2752, 2, TILES, TOPK)
        CAND, TV, TI = ar(2912, TILES, 256), ar(4192, TILES, TOPK), ar(4272, TILES, TOPK).bitcast(U32)
        TA, TAF = ar(4352, 2, TILES * TOPK).bitcast(U32), ar(4512, 2, TILES * TOPK)
        EQ, EQ2 = ar(4672, TILES * TOPK, TOPK), ar(5952, TILES * TOPK, TOPK)
        GS, IJ = ar(7232, TILES, P), ar(7872, 2, TILES, P)
        SMX = ar(4192, TILES * EH)
        SK = ar(13824, 2 * EH, NK)
        GIJ = ar(0, 3, T)
        AA, BB, STG = ar(1728, 2, 4, P), ar(2752, 2, 4, P), ar(3776, 2, NK, PG)
        GO, GI, PP = ar(12000, 2, T), ar(13824, 2, 2, T), ar(9216, 2, NPG, 2, PG)

        names = (
            "in_const in_x in_mem in_tab in_pw in_pool in_p0 in_p1 in_t0 in_t1 in_t2 raw0 raw1 "
            "ks_in0 ks_in1 ks_in2 ks_in3 vs_in0 vs_in1 in_kt in_st "
            "out_k0 out_k1 out_v0 out_v1 out_pool out_a out_spr out_sst out_b out_x out_om out_p0 out_p1 out_y0 out_y1 out_y2 out_g0 out_g1 "
            "consts_set waited_v dve_step used hi_done split_done lin_evac "
            "sq_ready sq_used sum_done var_ready sd_ready t_ready hi_ready lo_ready "
            "pool_d pool_mm pool_evac rot_done qx_done vt_done v_evac kt_done k_evac km_done qk_done inner_done "
            "o_done o_evac spr_evac mean_done sqd_ready rvar_done rvar_ready rsd_ready ks_mm sst_new b_done "
            "x_added qz_done mx_done p_exp p_done pt_done pt_evac om_evac ks_used vs_used "
            "sk_done sc_evac cand_done soft_in soft_exp soft_done gt_done gt_evac "
            "pa_ready p_mm pbank_free gelu_done w_done whi_done ww_ready v_done v_free"
        ).split()
        S = {n: sem(n) for n in names}

        block = ctx.enter_context(nc.Block())

        @block.sync
        def _(sp):
            def load(n, slot, src, loads=None):
                sp.wait_ge(S["split_done"], free(n))
                sp.dma_start(RAW[:, slot, :], src.rearrange("a p n -> p (a n)")).then_inc(S[f"raw{slot}"], 16)

            def load_lin(first, n_pairs):
                with sp.Fori(0, n_pairs) as i:
                    for s in range(2):
                        load(i * 2 + (first + s), s, w_lin[bass.ds(i * 2 + (first + s), 1)])

            for dst, src in ((CST[:, :, :], consts[:, 0:256].rearrange("p (a n) -> p a n", a=2)),
                             (RC[:, :], consts[:, 256:272]), (GAINS[:, :], gains), (CS[:, :, :], rot)):
                sp.dma_start(dst, src).then_inc(S["in_const"], 16)
            sp.dma_start(XM, memT.rearrange("k p m -> p k m")).then_inc(S["in_mem"], 16)
            load_lin(0, H_MQ // 2 + 2)

            sp.wait_ge(S["lo_ready"], 16 * 4)
            sp.wait_ge(S["out_x"], 16)
            with sp.Fori(0, MH) as h:
                sp.wait_ge(S["vs_used"], h * SB + 2)
                sp.dma_start(KT, mkT[bass.ts(h, 4)].rearrange("c p m -> p c m")).then_inc(S["in_kt"], 16)
                sp.dma_start(VT, mv.rearrange("(m p) n -> p m n", p=P)[:, :, bass.ts(h, MD)]).then_inc(S["in_kt"], 16)

                def load_k(b):
                    sp.wait_ge(S["ks_used"], h * SB + (b + 1))
                    sp.dma_start(KS[:, b % 4], kcT[b, bass.ds(h, 1)].rearrange("a (c p) m -> p (a c) m", p=P))\
                        .then_inc(S[f"ks_in{b % 4}"], 16)

                for b in range(4):
                    load_k(b)
                for n in range(8):
                    load(h * 8 + (H_MQ + 4 + n), n % 2, w_lin[bass.ds(h * 8 + (H_MQ + 4 + n), 1)])
                for b in range(4, SB):
                    load_k(b)
                for b in range(SB):
                    sp.wait_ge(S["vs_used"], h * SB + (b + 1))
                    sp.dma_start(VS[:, b % 2], vc[b].rearrange("(m p) n -> p m n", p=P)[:, :, bass.ts(h, MD)])\
                        .then_inc(S[f"vs_in{b % 2}"], 16)
            load_lin(H_MO + 4, (H_WQ - H_MO - 4) // 2)

            def load_u(pr, n):
                for k in range(4):
                    load(n + k, k % 2, uT[bass.ds(pr * 4 + k, 1)])

            def load_v(pr, n):
                for k in range(4):
                    load(n + k, k % 2, vE[bass.ds(pr * 2 + k % 2, 1), :, HW * (k // 2):HW * (k // 2 + 1)])

            with sp.Fori(0, EH) as h:
                for k in range(4):
                    load(h * 8 + (H_WQ + k), k % 2, w_lin[bass.ds(h * 4 + (H_WQ + k), 1)])
                load_u(h, h * 8 + (H_WQ + 4))
            with sp.Fori(0, 1 + NPG // 2) as i:
                load_u(i + EH, i * 4 + H_TAIL)
            with sp.Fori(0, NP2 - LAG) as i:
                load_u(i + LAG, i * 8 + H_UV)
                load_v(i, i * 8 + (H_UV + 4))
            with sp.Fori(0, LAG) as i:
                load_v(i + (NP2 - LAG), i * 4 + H_V)

        @block.gpsimd
        def _(pool):
            pool.memset(ONES[:, 0, :], 1.0 / D).then_inc(S["consts_set"], 1)
            pool.memset(ONES[:, 1, :], 1.0 / RD).then_inc(S["consts_set"], 1)
            pool.sem_inc(S["split_done"], 2)
            with pool.Fori(0, H_ALL // 4) as i:
                for k in range(4):
                    pool.wait_ge(S["hi_done"], i * 4 + (k + 1))
                    pool.tensor_tensor(WS[:, k, 1, :], RAW[:, k % 2, :], WS[:, k, 0, :].bitcast(F32), ALU.subtract)\
                        .then_inc(S["split_done"], 1)

        @block.tensor
        def _(pe):
            mm = pe.matmul
            pe.sem_inc(S["used"], 4)
            pe.sem_inc(S["p_mm"], 2)
            pe.sem_inc(S["ks_used"], 4)
            pe.sem_inc(S["vs_used"], 2)
            pe.sem_inc(S["sk_done"], 1)

            def projection(n, m, a, slot, cols=((0, HALF), (HALF, HALF)), ready=0, between=None):
                pe.wait_ge(S["lin_evac"], m + 1)
                for hf in range(2):
                    pe.wait_ge(S["split_done"], n + split(hf))
                    for k in range(KB // 2):
                        kb = hf * (KB // 2) + k
                        if ready:
                            pe.wait_ge(S["lo_ready"], ready + kb - 15)
                        first, last = kb == 0, kb == KB - 1
                        for wp, xp in ((0, 0), (0, 1), (1, 0)):
                            for c, (at, w) in enumerate(cols):
                                ins = mm(bank(2 * a + c, w), WS[:, slot + hf, wp, k * P:(k + 1) * P],
                                         HL[:, xp, kb, at:at + w], start=first and (wp, xp) == (0, 0),
                                         stop=last and wp == 1, skip_group_check=True)
                        if k == KB // 2 - 1:
                            ins.then_inc(S["used"], 1)
                        if between and k % 2:
                            between(kb // 2)

            def norm_sum(k, cols=((0, HALF), (HALF, HALF))):
                pe.wait_ge(S["sq_used"], 16 * (k + 1))
                for c, (at, w) in enumerate(cols):
                    ins = mm(bank(6 + c, w), ONES[:, 0, :], NACC[:, at:at + w], start=True, stop=True)
                ins.then_inc(S["sum_done"], 1)

            pe.wait_ge(S["consts_set"], 2)
            pe.wait_ge(S["in_const"], 64)
            norm_sum(0, ((0, MEM),))
            with pe.Fori(0, 8) as i:
                for s in range(2):
                    projection(i * 4 + 2 * s, i * 2 + (B_MK + s), s, 2 * s, ((0, MEM),), ready=16)
            with pe.Fori(0, 2) as i:
                for a in range(2):
                    pe.wait_ge(S["lin_evac"], i * 2 + (B_MV + a + 1))
                    for q in range(8):
                        n = i * 16 + (H_MV + 8 * a + q)
                        pe.wait_ge(S["split_done"], n + split(0))
                        for k in range(2):
                            kb = 2 * q + k
                            for xp, wp in ((0, 0), (0, 1), (1, 0)):
                                for t in range(2):
                                    ins = mm(bank(2 * a + t), HL[:, xp, kb, t * P:(t + 1) * P],
                                             WS[:, q % 4, wp, k * 512:(k + 1) * 512],
                                             start=kb == 0 and (xp, wp) == (0, 0), stop=kb == KB - 1 and xp == 1,
                                             skip_group_check=True)
                        ins.then_inc(S["used"], 1)

            norm_sum(1)
            with pe.Fori(0, GROUPS) as g:
                for s in range(2):
                    projection(g * 4 + (H_POOL + 2 * s), g * 2 + (B_POOL + s), s, 2 * s, ready=32)
                pe.wait_ge(S["pool_d"], g + 1)
                pe.wait_ge(S["in_pw"], g * 16 + 16)
                pe.wait_ge(S["pool_evac"], g + 1)
                for o in range(2):
                    for c in range(2):
                        for ch in range(2):
                            ins = mm(bank(4 + 2 * o + ch, HALF), PW[:, c, o * P:(o + 1) * P],
                                     DT[:, c, ch * HALF:(ch + 1) * HALF], start=c == 0, stop=c == 1,
                                     skip_group_check=True)
                ins.then_inc(S["pool_mm"], 1)

            with pe.Fori(0, RH) as h:
                for m in range(8):
                    projection(h * 16 + (H_RET + 2 * m), h * 8 + (B_RET + m), m % 2, 2 * (m % 2))
                pe.wait_ge(S["lin_evac"], h * 8 + (B_RET + 6 + 2))
                pe.wait_ge(S["b_done"], h + 1)
                pe.wait_ge(S["pool_evac"], GROUPS + 1)
                for t in range(TILES):
                    w = P if t < 4 else TS
                    for c in range(2):
                        ins = pe.transpose(PS[0:w, 2048 + RD * t + P * c:2048 + RD * t + P * c + P],
                                           RAWQ[:, 4 + c, P * t:P * t + w], IDENT)
                ins.then_inc(S["vt_done"], 1)
                pe.wait_ge(S["rot_done"], h + 1)
                pe.wait_ge(S["v_evac"], h + 1)
                for t in range(TILES):
                    w = P if t < 4 else TS
                    for c in range(2):
                        ins = pe.transpose(PS[0:w, 2048 + RD * t + P * c:2048 + RD * t + P * c + P],
                                           RK[:, c, P * t:P * t + w], IDENT)
                ins.then_inc(S["kt_done"], 1)
                pe.wait_ge(S["k_evac"], h + 1)
                for j in range(4):
                    for c in range(2):
                        mm(bank(4 + j, TP - P * j), RK[:, c, P * j:P * (j + 1)], RQ[:, c, P * j:TP],
                           start=c == 0, stop=c == 1)
                for c in range(2):
                    ins = mm(bank(7, TS, TS, 256), RK[:, c, TP:T], RQ[:, c, TP:T], start=c == 0, stop=c == 1)
                ins.then_inc(S["qk_done"], 1)
                pe.wait_ge(S["inner_done"], h + 1)
                pe.wait_ge(S["qx_done"], h + 1)
                pe.wait_ge(S["in_st"], h * 128 + 128)
                for c in range(2):
                    for j in range(4):
                        mm(bank(4 + c, TP - P * j, off=P * j), VTOK[:, j, P * c:P * (c + 1)], INNER[j],
                           start=j == 0, stop=j == 3, skip_group_check=True)
                    mm(bank(6, TS, off=TS * c), VTOK[0:TS, 4, P * c:P * (c + 1)], INNERS,
                       start=True, stop=False, skip_group_check=True)
                    for b in range(SB):
                        for k in range(2):
                            ins = mm(bank(6, SQ, off=TS * c + SQ * b), SST[:, b, k, P * c:P * (c + 1)],
                                     QX[:, k, SQ * b:SQ * (b + 1)], start=False, stop=k == 1, skip_group_check=True)
                ins.then_inc(S["o_done"], 1)
                for c in range(2):
                    for j in range(4):
                        ins = mm(bank(7, RD, off=RD * c), KTOK[:, j, P * c:P * (c + 1)], VTOK[:, j, :],
                                 start=j == 0, stop=j == 3, skip_group_check=True)
                ins.then_inc(S["o_done"], 1)
                pe.wait_ge(S["o_evac"], h + 1)
                pe.wait_ge(S["spr_evac"], h + 1)
                for ch in range(2):
                    for c in range(2):
                        ins = mm(bank(6 + ch, HALF), ONES[:, 1, :], OT[:, c, ch * HALF:(ch + 1) * HALF],
                                 start=c == 0, stop=c == 1)
                ins.then_inc(S["mean_done"], 1)
                pe.wait_ge(S["km_done"], h + 1)
                for b in range(SB):
                    if b >= 2:
                        pe.wait_ge(S["sst_new"], h * SB + (b - 1))
                    for c in range(2):
                        ins = mm(bank(4 + b % 2, RD, off=RD * c), KM[:, b, P * c:P * (c + 1)], VTOK[0:TS, 4, :],
                                 start=True, stop=True, skip_group_check=True)
                    ins.then_inc(S["ks_mm"], 1)
                pe.wait_ge(S["sqd_ready"], h + 1)
                for ch in range(2):
                    for c in range(2):
                        ins = mm(bank(6 + ch, HALF), ONES[:, 1, :], SQD[:, c, ch * HALF:(ch + 1) * HALF],
                                 start=c == 0, stop=c == 1)
                ins.then_inc(S["rvar_done"], 1)

            with pe.Fori(0, 8) as i:
                for s in range(2):
                    projection(i * 4 + (H_OUT + 2 * s), i * 2 + (B_OUT + s), s, 2 * s, ready=48)
            norm_sum(2)

            with pe.Fori(0, MH) as h:
                pe.wait_ge(S["om_evac"], h + 1)
                for m in range(4):
                    projection(h * 8 + (H_MQ + 2 * m), h * 4 + (B_MQ + m), m % 2, 2 * (m % 2), ready=64)
                pe.wait_ge(S["lin_evac"], h * 4 + (B_MQ + 4 + 2))
                pe.wait_ge(S["in_kt"], h * 32 + 32)
                for t in range(4):
                    for c in range(4):
                        mm(bank(4, MEM, off=MEM * t), QM[:, c, P * t:P * (t + 1)], KT[:, c, :],
                           start=c == 0, stop=c == 3, skip_group_check=True)
                pe.wait_ge(S["qz_done"], h + 1)
                for b in range(SB):
                    pe.wait_ge(S[f"ks_in{b % 4}"], h * 32 + 16 * (b // 4 + 1))
                    for c in range(4):
                        ins = mm(bank(6, MEM, TS), QZ[:, b, c, :], KS[:, b % 4, c, :],
                                 start=b == 0 and c == 0, stop=b == 7 and c == 3, skip_group_check=True)
                    ins.then_inc(S["ks_used"], 1)
                pe.wait_ge(S["p_done"], h + 1)
                for m in range(2):
                    for t in range(4):
                        pe.transpose(bank(4 + m, P, off=P * t), PR[:, t, P * m:P * (m + 1)], IDENT)
                    ins = pe.transpose(bank(6, TS, off=TS * m), PR[0:TS, 4, P * m:P * (m + 1)], CST[0:TS, 0, 0:TS])
                ins.then_inc(S["pt_done"], 1)
                pe.wait_ge(S["pt_evac"], h + 1)
                for c in range(4):
                    for m in range(2):
                        mm(bank(4 + c), VT[:, m, P * c:P * (c + 1)], PT[:, m, 0:TP], start=m == 0, stop=m == 1)
                for b in range(SB):
                    pe.wait_ge(S[f"vs_in{b % 2}"], h * 64 + 16 * (b // 2 + 1))
                    for c in range(4):
                        for m in range(2):
                            ins = mm(bank(0, SQ, off=TS * c + SQ * b), VS[:, b % 2, m, P * c:P * (c + 1)],
                                     PT[:, m, TP + SQ * b:TP + SQ * (b + 1)], start=m == 0, stop=m == 1,
                                     skip_group_check=True)
                    ins.then_inc(S["vs_used"], 1)

            pe.wait_ge(S["om_evac"], MH + 1)
            with pe.Fori(0, 8) as i:
                for s in range(2):
                    projection(i * 4 + (H_MO + 2 * s), i * 2 + (B_MO + s), s, 2 * s, ready=80)
            norm_sum(3)

            with pe.Fori(0, EH) as h:
                for s in range(2):
                    projection(h * 8 + (H_WQ + 2 * s), h * 4 + (B_WQ + s), s, 2 * s, ready=96)
                projection(h * 8 + (H_WQ + 4), h * 4 + (B_WQ + 2), 0, 0)
                pe.wait_ge(S["lin_evac"], h * 4 + (B_WQ + 2 + 2))
                pe.wait_ge(S["sc_evac"], h + 1)
                pe.wait_ge(S["out_g0"], 16)
                pe.wait_ge(S["out_g1"], 16)
                for c in range(2):
                    keys = SK[:, bass.ds(h * 2 + c, 1), :].rearrange("p a n -> p (a n)")
                    for t in range(TILES):
                        w = P if t < 4 else TS
                        ins = mm(PS[0:w, 512 * (4 + 2 * c) + P * t:512 * (4 + 2 * c) + P * (t + 1)],
                                 QP[:, c, P * t:P * t + w], keys, start=True, stop=True, skip_group_check=True)
                ins.then_inc(S["sk_done"], 1)
                projection(h * 8 + (H_WQ + 6), h * 4 + (B_WQ + 3), 1, 2)
            for s in range(2):
                projection(H_TAIL + 2 * s, B_TAIL + s, s, 2 * s)
            pe.wait_ge(S["soft_done"], 1)
            pe.wait_ge(S["sc_evac"], EH + 1)
            pe.wait_ge(S["lin_evac"], B_P + 2)
            for k, src in enumerate((GS, IJ[:, 0], IJ[:, 1])):
                for t in range(4):
                    pe.transpose(bank(2 * k, P, off=P * t), src[:, t, :], IDENT)
                ins = pe.transpose(bank(2 * k + 1, TS), src[0:TS, 4, :], CST[0:TS, 0, 0:TS])
            ins.then_inc(S["gt_done"], 1)
            pe.wait_ge(S["gt_evac"], 1)
            with pe.Fori(0, NPG // 2) as g:
                for par in range(2):
                    def quad(q):
                        n = g * (PG // 2) + (par * (PG // 4) + q)
                        pe.wait_ge(S["pa_ready"], n + 1)
                        pe.wait_ge(S["pbank_free"], n + 1)
                        for k in range(4):
                            ins = mm(bank(4 + q % 2, P, off=P * k), BB[:, q % 2, k, :], AA[:, q % 2, k, :],
                                     start=True, stop=True, skip_group_check=True)
                        ins.then_inc(S["p_mm"], 1)

                    projection(g * 4 + (H_P + 2 * par), g * 2 + (B_P + par), par, 2 * par, between=quad)

            def up(n, m):
                for e in range(2):
                    projection(n + 2 * e, m + e, e, 2 * e)

            def down(n, v, w, par):
                pe.wait_ge(S["ww_ready"], w)
                for dh in range(2):
                    for e in range(2):
                        pe.wait_ge(S["split_done"], n + split(2 * dh + e))
                    for d8 in range(8):
                        d = 8 * dh + d8
                        pe.wait_ge(S["v_free"], v + (d + 1))
                        for e in range(2):
                            for vp, wp in ((0, 0), (0, 1), (1, 0)):
                                for ch in range(2):
                                    ins = mm(bank(4 + 2 * (d % 2) + ch, HALF), WS[:, 2 * dh + e, vp, P * d8:P * (d8 + 1)],
                                             WW[:, par, e, wp, ch * HALF:(ch + 1) * HALF],
                                             start=e == 0 and (vp, wp) == (0, 0), stop=e == 1 and vp == 1,
                                             skip_group_check=True)
                        if d8 < 7:
                            ins.then_inc(S["v_done"], 1)
                    ins.then_inc(S["used"], 2)

            with pe.Fori(0, (NP2 - LAG) // 2) as i:
                for s in range(2):
                    up(i * 16 + (H_UV + 8 * s), i * 4 + (B_UV + 2 * s))
                    down(i * 16 + (H_UV + 4 + 8 * s), i * 32 + 16 * s, i * 4 + (2 * s + 2), s)
            with pe.Fori(0, LAG // 2) as i:
                for s in range(2):
                    pr = NP2 - LAG + s
                    down(i * 8 + (H_V + 4 * s), i * 32 + 16 * pr, i * 4 + 2 * (pr + 1), s)
            norm_sum(4)

        @block.scalar
        def _(act):
            copy = lambda out, in_, **kw: act.activation(out, in_, ACT.Identity, **kw)
            act.sem_inc(S["lin_evac"], 2)
            act.sem_inc(S["pbank_free"], 2)
            for name in ("pool_evac", "om_evac", "sc_evac"):
                act.sem_inc(S[name], 1)

            def high(n, slot, odd=0):
                act.wait_ge(S[f"raw{odd}"], n * 8 + 16)
                copy(WS[:, slot + odd, 0, :], RAW[:, odd, :]).then_inc(S["hi_done"], 1)

            def high2(n, slot):
                high(n, slot)
                high(n, slot, 1)

            high2(0, 0)
            high2(2, 2)
            act.wait_ge(S["in_const"], 64)

            def square(k, b, x, n=T):
                if k or b >= 2:
                    act.wait_ge(S["sq_used"], 16 * k + max(b - 1, 0))
                act.activation(NSQ[:, b % 2, 0:n], x[:, b, :], ACT.Square).then_inc(S["sq_ready"], 1)

            def squares(k, x, n=T):
                for b in range(KB):
                    square(k, b, x, n)

            def root(k, n=T):
                act.wait_ge(S["var_ready"], k + 1)
                act.activation(NRS[:, 0:n], NVAR[:, 0:n], ACT.Sqrt).then_inc(S["sd_ready"], 1)

            def highs(t, hi, n=T):
                for b in range(KB):
                    act.wait_ge(S["t_ready"], t + b + 1)
                    copy(HL[:, 0, b, 0:n], NT[:, b % 3, 0:n]).then_inc(S["hi_ready"], 1)

            def load_split(src, r, lo):
                def load(b):
                    if b >= 3:
                        act.wait_ge(S["lo_ready"], lo + b - 2)
                    act.dma_start(NT[:, b % 3, :], src[b]).then_inc(S[f"in_t{b % 3}"], 16)
                for b in range(3):
                    load(b)
                for b in range(KB):
                    act.wait_ge(S[f"in_t{b % 3}"], 16 * (r * (6 if b % 3 == 0 else 5) + b // 3 + 1))
                    copy(HL[:, 0, b, :], NT[:, b % 3, :]).then_inc(S["hi_ready"], 1)
                    if b >= 1 and b + 2 < KB:
                        load(b + 2)

            act.wait_ge(S["in_mem"], 16)
            squares(0, XM, MEM)
            root(0, MEM)
            highs(0, 0, MEM)
            act.wait_ge(S["lo_ready"], 16)
            act.dma_start(X, xT.rearrange("k p t -> p k t")).then_inc(S["in_x"], 16)
            act.wait_ge(S["in_x"], 16)
            squares(1, X)
            with act.Fori(0, 8) as i:
                for s in range(2):
                    act.wait_ge(S["used"], i * 4 + used(2 * s + 2))
                    copy(KST[:, s, :], bank(2 * s, MEM)).then_inc(S["lin_evac"], 1)
                    high2(i * 4 + (2 * s + 4), 2 * s)
                    act.wait_ge(S["lin_evac"], i * 2 + (B_MK + s + 3))
                    act.dma_start(mkT[bass.ds(i * 2 + s, 1)].rearrange("a p m -> p (a m)"), KST[:, s, :])\
                        .then_inc(S[f"out_k{s}"], 16)
                for s in range(2):
                    act.wait_ge(S[f"out_k{s}"], i * 16 + 16)
            with act.Fori(0, 2) as i:
                for s in range(2):
                    n = i * 16 + (H_MV + 8 * s)
                    for q in range(8):
                        act.wait_ge(S["used"], n + used(q + 1))
                        if q == 7:
                            copy(VST[:, s, :], PS[:, 1024 * s:1024 * s + 1024]).then_inc(S["lin_evac"], 1)
                        high(n + (q // 2 * 2 + 4), q % 4 // 2 * 2, q % 2)
                    act.wait_ge(S["lin_evac"], i * 2 + (B_MV + s + 3))
                    act.dma_start(mv.rearrange("(m p) n -> p m n", p=P)[:, :, bass.ts(i * 2 + s, 512)],
                                  VST[:, s, :].rearrange("p (m n) -> p m n", m=2)).then_inc(S[f"out_v{s}"], 16)
                for s in range(2):
                    act.wait_ge(S[f"out_v{s}"], i * 16 + 16)
            root(1)
            highs(16, 16)
            act.wait_ge(S["lo_ready"], 32)
            for g in range(GROUPS):
                if g:
                    act.wait_ge(S["pool_mm"], g)
                    act.wait_ge(S["pool_d"], g)
                    act.wait_ge(S["out_pool"], 64 * g)
                act.dma_start(PW, pool_w[g].rearrange("(c p) d -> p c d", p=P)).then_inc(S["in_pw"], 16)
                for c in range(2):
                    act.dma_start(PSX[:, c, :, 0:BUF], spoolT[2 * g + c]).then_inc(S["in_pool"], 16)
                if g == 0:
                    act.wait_ge(S["x_added"], 1)
                for c in range(2):
                    act.wait_ge(S["used"], used(H_POOL + 4 * g + 2 * c + 2))
                    copy(PEX[:, c, BUF:BUF + HALF], bank(2 * c, HALF))
                    copy(PEX[:, c, BUF + HALF:BUF + TP], bank(2 * c + 1, TP - HALF))
                    copy(PSX[:, c, :, BUF:BUF + SQ],
                         bank(2 * c + 1, TS, off=TP - HALF).rearrange("p (b q) -> p b q", b=SB)).then_inc(S["lin_evac"], 1)
                    high2(H_POOL + 4 * g + 2 * c + 4, 2 * c)
                act.wait_ge(S["lin_evac"], B_POOL + 2 * g + 4)
                act.wait_ge(S["in_pool"], 32 * (g + 1))
                for c in range(2):
                    act.dma_start(npoolT_p[2 * g + c], PEX[:, c, TP:TP + BUF]).then_inc(S["out_pool"], 16)
                    act.dma_start(npoolT_s[2 * g + c], PSX[:, c, :, SQ:SQ + BUF]).then_inc(S["out_pool"], 16)
                act.wait_ge(S["pool_mm"], g + 1)
                if g:
                    act.wait_ge(S["out_a"], 16 * g)
                for o in range(2):
                    ins = copy(halves(AT[:, o, :]), pair(2 + o), scale=GAINS[:, G_POOLS + 2 * g + o:G_POOLS + 2 * g + o + 1])
                ins.then_inc(S["pool_evac"], 1)
                act.wait_ge(S["pool_evac"], g + 2)
                act.dma_start(mixT[2 * g:2 * g + 2].rearrange("k p t -> p k t"), AT).then_inc(S["out_a"], 16)
            act.wait_ge(S["pool_d"], GROUPS)
            act.wait_ge(S["out_pool"], 64 * GROUPS)
            act.wait_ge(S["out_a"], 16 * GROUPS)
            with act.Fori(0, RH) as h:
                act.wait_ge(S["b_done"], h + 1)
                act.dma_start(TAB, tabs[bass.ds(h, 1)].rearrange("a p n -> p (a n)")).then_inc(S["in_tab"], 16)
                for b in range(SB):
                    act.dma_start(SST[:, b], sret[b, bass.ds(h, 1)].rearrange("a (c p) v -> p (a c) v", p=P))\
                        .then_inc(S["in_st"], 16)
                for m in range(8):
                    act.wait_ge(S["used"], h * 16 + used(H_RET + 2 * m + 2))
                    kw = {"scale": RD ** -0.5} if m in (2, 3) else {}
                    act.activation(halves(RAWQ[:, m, :]), pair(m % 2), ACT.Silu if m >= 6 else ACT.Identity, **kw)\
                        .then_inc(S["lin_evac"], 1)
                    high2(h * 16 + (H_RET + 2 * m + 4), 2 * (m % 2))
                act.wait_ge(S["vt_done"], h + 1)
                copy(VTOK[:, 0:4, :], PS[:, 2048:3072].rearrange("p (t n) -> p t n", t=4))
                copy(VTOK[0:TS, 4, :], bank(6, RD, TS)).then_inc(S["v_evac"], 1)
                act.wait_ge(S["kt_done"], h + 1)
                act.wait_ge(S["in_tab"], h * 16 + 16)
                for t in range(4):
                    copy(KTOK[:, t, :], PS[:, 2048 + RD * t:2048 + RD * (t + 1)], scale=TAB[:, T_ZETA + t:T_ZETA + t + 1])
                copy(KTOK[0:TS, 4, :], bank(6, RD, TS)).then_inc(S["k_evac"], 1)
                act.wait_ge(S["o_done"], h * 2 + 1)
                copy(OT[:, :, 0:TP], PS[:, 2048:3072].rearrange("p (c n) -> p c n", c=2))
                copy(OT[:, :, TP:T], bank(6, 2 * TS).rearrange("p (c n) -> p c n", c=2)).then_inc(S["o_evac"], 1)
                act.wait_ge(S["o_done"], h * 2 + 2)
                copy(SPR, bank(7).rearrange("p (c n) -> p c n", c=2)).then_inc(S["spr_evac"], 1)
                act.wait_ge(S["spr_evac"], h + 1)
                act.dma_start(nret_p[bass.ds(h, 1)].rearrange("a (c p) v -> p (a c) v", p=P), SPR).then_inc(S["out_spr"], 16)
                for b in range(SB):
                    act.wait_ge(S["sst_new"], h * SB + (b + 1))
                    act.dma_start(nret_s[b, bass.ds(h, 1)].rearrange("a (c p) v -> p (a c) v", p=P), SST[:, b])\
                        .then_inc(S["out_sst"], 16)
                act.wait_ge(S["rvar_ready"], h + 1)
                act.activation(RSD, RVAR, ACT.Sqrt).then_inc(S["rsd_ready"], 1)
                act.wait_ge(S["b_done"], h + 2)
                act.dma_start(mixT[bass.ds(h * 2 + 8, 2)].rearrange("k p t -> p k t"), OT).then_inc(S["out_b"], 16)
                act.wait_ge(S["out_sst"], h * 128 + 128)
                act.wait_ge(S["out_spr"], h * 16 + 16)
                act.wait_ge(S["out_b"], h * 16 + 16)

            def add_stage(k, first, m):
                for b in range(KB):
                    act.wait_ge(S["used"], used(first + 2 * b + 2))
                    high2(first + 2 * b + 4, 2 * (b % 2))
                    if b:
                        act.wait_ge(S["lin_evac"], m + b + 2)
                        square(k, b - 1, X)
                act.wait_ge(S["lin_evac"], m + KB + 2)
                square(k, KB - 1, X)

            act.dma_start(X, xT.rearrange("k p t -> p k t")).then_inc(S["in_x"], 16)
            load_split(mixT, 0, 32)
            add_stage(2, H_OUT, B_OUT)
            act.dma_start(x2T.rearrange("k p t -> p k t"), X).then_inc(S["out_x"], 16)
            root(2)
            highs(32, 48)
            act.wait_ge(S["lo_ready"], 64)
            act.wait_ge(S["out_x"], 16)

            with act.Fori(0, MH) as h:
                act.wait_ge(S["ks_used"], h * SB + 4)
                for m in range(4):
                    act.wait_ge(S["used"], h * 8 + used(H_MQ + 2 * m + 2))
                    copy(halves(QM[:, m, :]), pair(m % 2)).then_inc(S["lin_evac"], 1)
                    high2(h * 8 + (H_MQ + 2 * m + 4), 2 * (m % 2))
                act.wait_ge(S["mx_done"], h + 1)
                for t in range(TILES):
                    w = P if t < 4 else TS
                    ins = act.activation(PR[0:w, t, :], PS[0:w, 2048 + MEM * t:2048 + MEM * (t + 1)], ACT.Exp,
                                         bias=NMX[0:w, t:t + 1], scale=MD ** -0.5, accum_out=SM[0:w, t:t + 1])
                ins.then_inc(S["p_exp"], 1)
                act.wait_ge(S["pt_done"], h + 1)
                copy(PT[:, :, 0:TP], PS[:, 2048:3072].rearrange("p (m n) -> p m n", m=2))
                copy(PT[:, :, TP:T], bank(6, 2 * TS).rearrange("p (m n) -> p m n", m=2)).then_inc(S["pt_evac"], 1)
                act.wait_ge(S["vs_used"], h * SB + (SB + 2))
                copy(OB[:, :, 0:TP], PS[:, 2048:4096].rearrange("p (c n) -> p c n", c=4))
                copy(OB[:, :, TP:T], bank(0, 4 * TS).rearrange("p (c n) -> p c n", c=4)).then_inc(S["om_evac"], 1)
                act.wait_ge(S["om_evac"], h + 2)
                act.dma_start(omT[bass.ts(h, 4)].rearrange("k p t -> p k t"), OB).then_inc(S["out_om"], 16)
                act.wait_ge(S["out_om"], h * 16 + 16)
            act.dma_start(X, x2T.rearrange("k p t -> p k t")).then_inc(S["in_x"], 16)
            load_split(omT, 1, 64)
            add_stage(3, H_MO, B_MO)
            for s in range(2):
                act.dma_start(x3T[8 * s:8 * s + 8].rearrange("k p t -> p k t"), X[:, 8 * s:8 * s + 8, :])\
                    .then_inc(S[f"out_p{s}"], 16)
            root(3)
            for s in range(2):
                act.dma_start(SK[:, 8 * s:8 * s + 8, :], subk[:, 8 * s:8 * s + 8, :]).then_inc(S[f"out_g{s}"], 16)
            highs(48, 80)
            act.wait_ge(S["lo_ready"], 96)
            for s in range(2):
                act.wait_ge(S[f"out_p{s}"], 16)

            def gelu_out(r, n, e, slot):
                act.wait_ge(S["used"], n + used(2))
                act.wait_ge(S[f"out_g{e}"], r * 16 + 16)
                act.activation(halves(GO[:, e, :]), pair(e), ACT.Gelu).then_inc(S["lin_evac"], 1)
                high2(n + 4, slot)

            def store_gelu(r, m, e):
                act.wait_ge(S["lin_evac"], m + 3)
                act.dma_start(gel[bass.ds(r * 2 + e, 1)].rearrange("a p t -> p (a t)"), GO[:, e, :])\
                    .then_inc(S[f"out_g{e}"], 16)

            act.wait_ge(S["x_added"], 2)
            with act.Fori(0, EH) as h:
                act.wait_ge(S["sk_done"], h + 1)
                for c in range(2):
                    act.wait_ge(S["used"], h * 8 + used(H_WQ + 2 * c + 2))
                    copy(halves(QP[:, c, :]), pair(c)).then_inc(S["lin_evac"], 1)
                    high2(h * 8 + (H_WQ + 2 * c + 4), 2 * c)
                gelu_out(h, h * 8 + (H_WQ + 4), 0, 0)
                store_gelu(h, h * 4 + (B_WQ + 2), 0)
                act.wait_ge(S["sk_done"], h + 2)
                act.wait_ge(S["cand_done"], h + 1)
                copy(SC[:, :, 0:4, :].rearrange("p c t n -> p c (t n)"),
                     PS[:, 2048:4096].rearrange("p (c n) -> p c n", c=2)[:, :, 0:512])
                copy(SC[0:TS, :, 4, :], PS[0:TS, 2048:4096].rearrange("p (c n) -> p c n", c=2)[:, :, 512:512 + NK])\
                    .then_inc(S["sc_evac"], 1)
                gelu_out(h, h * 8 + (H_WQ + 6), 1, 2)
                store_gelu(h, h * 4 + (B_WQ + 3), 1)
            for e in range(2):
                gelu_out(EH, H_TAIL + 2 * e, e, 2 * e)
                store_gelu(EH, B_TAIL + e, e)
            act.wait_ge(S["soft_in"], 1)
            act.activation(CAND.rearrange("p t n -> p (t n)")[:, 0:640], EQ.rearrange("p a n -> p (a n)")[:, 0:640], ACT.Exp)\
                .then_inc(S["soft_exp"], 1)
            act.wait_ge(S["gt_done"], 1)
            for k in range(3):
                copy(GIJ[:, k, 0:TP], bank(2 * k))
                ins = copy(GIJ[:, k, TP:T], bank(2 * k + 1, TS))
            ins.then_inc(S["gt_evac"], 1)
            with act.Fori(0, NPG // 2) as g:
                for par in range(2):
                    act.wait_ge(S[f"out_p{par}"], g * 16 + 16)
                    for q in range(PG // 4):
                        n = g * (PG // 2) + (par * (PG // 4) + q)
                        act.wait_ge(S["p_mm"], n + 3)
                        copy(STG[:, par, :, 4 * q:4 * q + 4].rearrange("p i t -> p t i"),
                             bank(4 + q % 2).rearrange("p (t i) -> p t i", t=4)).then_inc(S["pbank_free"], 1)
                    gelu_out(g + (EH + 1), g * 4 + (H_P + 2 * par), par, 2 * par)
                    store_gelu(g + (EH + 1), g * 2 + (B_P + par), par)
                    act.wait_ge(S["pbank_free"], n + 3)
                    act.dma_start(pmap[bass.ds(g * 2 + par, 1)].rearrange("a p n -> p (a n)"),
                                  STG[:, par].rearrange("p i t -> p (i t)")).then_inc(S[f"out_p{par}"], 16)
            for par in range(2):
                act.wait_ge(S[f"out_p{par}"], 16 + 16 * (NPG // 2))
            act.dma_start(X, x3T.rearrange("k p t -> p k t")).then_inc(S["in_x"], 16)

            def load_pair(pr, par):
                for e in range(2):
                    act.wait_ge(S[f"out_g{e}"], pr * 16 + 32)
                act.dma_start(PP[:, par].rearrange("p g e t -> p g (e t)"),
                              pmap.rearrange("g p n -> p g n")[:, :, bass.ts(pr, 2 * PG)]).then_inc(S[f"in_p{par}"], 16)
                act.dma_start(GI[:, par], gel[bass.ts(pr, 2)].rearrange("e p t -> p e t")).then_inc(S[f"in_p{par}"], 16)

            def w_highs(pr, par):
                for e in range(2):
                    act.wait_ge(S["w_done"], pr * 2 + (e + 1))
                    copy(WW[:, par, e, 0, :], GI[:, par, e, :]).then_inc(S["whi_done"], 1)

            load_pair(0, 0)
            load_pair(1, 1)
            w_highs(0, 0)
            load_next = lambda pr, par: (act.wait_ge(S["ww_ready"], pr * 2 - 2), load_pair(pr, par))
            load_next(2, 0)
            with act.Fori(0, (NP2 - LAG) // 2) as i:
                for s in range(2):
                    n = i * 16 + (H_UV + 8 * s)
                    w_highs(i * 2 + (s + 1), 1 - s)
                    load_next(i * 2 + (s + 3), 1 - s)
                    for e in range(2):
                        gelu_out(i * 2 + (LAG + s), n + 2 * e, e, 2 * e)
                        store_gelu(i * 2 + (LAG + s), i * 4 + (B_UV + 2 * s + e), e)
                    for dh in range(2):
                        act.wait_ge(S["used"], n + used(6 + 2 * dh))
                        high2(n + (8 + 2 * dh), 2 * dh)

            def v_stage(pr, n, par, load=True, more=True):
                w_highs(pr + 1, 1 - par)
                if load:
                    load_next(pr + 3, 1 - par)
                for dh in range(2):
                    act.wait_ge(S["used"], n + used(2 + 2 * dh))
                    high2(n + (4 + 2 * dh), 2 * dh)

            looped = LAG // 2 - 2
            with act.Fori(0, looped) as i:
                for s in range(2):
                    v_stage(i * 2 + (NP2 - LAG + s), i * 8 + (H_V + 4 * s), s)
            for k in range(2 * looped, LAG - 1):
                v_stage(NP2 - LAG + k, H_V + 4 * k, k % 2, load=NP2 - LAG + k + 3 < NP2)

            for b in range(KB):
                act.wait_ge(S["v_free"], 2 + 16 * (NP2 - 1) + b + 1)
                square(4, b, X)
            root(4)
            for b in range(KB):
                act.wait_ge(S["t_ready"], 64 + b + 1)
                act.dma_start(yT[b], NT[:, b % 3, :]).then_inc(S[f"out_y{b % 3}"], 16)
            for k in range(3):
                act.wait_ge(S[f"out_y{k}"], 16 * (6 if k == 0 else 5))

        @block.vector
        def _(dve):
            step = Steps(dve, S["dve_step"])
            link = step.link
            tt, ts, stt = dve.tensor_tensor, dve.tensor_scalar, dve.scalar_tensor_tensor
            dve.sem_inc(S["v_free"], 2)
            dve.sem_inc(S["b_done"], 1)
            dve.sem_inc(S["cand_done"], 1)
            dve.wait_ge(S["in_const"], 64)

            def add_square(k, b, n=T):
                dve.wait_ge(S["sq_ready"], 16 * k + b + 1)
                if b:
                    dve.wait_ge(S["sq_used"], 16 * k + b)
                    tt(NACC[:, 0:n], NACC[:, 0:n], NSQ[:, b % 2, 0:n], ALU.add).then_inc(S["sq_used"], 1)
                else:
                    dve.tensor_copy(NACC[:, 0:n], NSQ[:, 0, 0:n]).then_inc(S["sq_used"], 1)

            def newton(r, v, t):
                link(tt(t, v, r, ALU.mult))
                link(tt(t, t, r, ALU.mult))
                link(ts(t, t, -0.5, 1.5, ALU.mult, ALU.add))
                link(tt(r, r, t, ALU.mult))

            def rstd(k, n=T, summed=False):
                if not summed:
                    for b in range(KB):
                        add_square(k, b, n)
                dve.wait_ge(S["sum_done"], k + 1)
                if n == T:
                    ts(halves(NVAR), pair(3), EPS, None, ALU.add).then_inc(S["var_ready"], 1)
                else:
                    ts(NVAR[:, 0:n], bank(6, n), EPS, None, ALU.add).then_inc(S["var_ready"], 1)
                dve.wait_ge(S["sd_ready"], k + 1)
                link(dve.reciprocal(NRS[:, 0:n], NRS[:, 0:n]))
                newton(NRS[:, 0:n], NVAR[:, 0:n], NACC[:, 0:n])

            def normed(k, x, gain, n=T, lo=None, free=None):
                def low(b):
                    dve.wait_ge(S["hi_ready"], lo + b + 1)
                    tt(HL[:, 1, b, 0:n], NT[:, b % 3, 0:n], HL[:, 0, b, 0:n].bitcast(F32), ALU.subtract)\
                        .then_inc(S["lo_ready"], 1)
                for b in range(KB):
                    if free and b >= 3:
                        dve.wait_ge(S[f"out_y{b % 3}"], 16 * (b // 3))
                    if lo is not None and b >= 3:
                        dve.wait_ge(S["lo_ready"], lo + b - 2)
                    stt(NT[:, b % 3, 0:n], x[:, b, :], GAINS[:, gain + b:gain + b + 1], NRS[:, 0:n], ALU.mult, ALU.mult)\
                        .then_inc(S["t_ready"], 1)
                    if lo is not None and b >= 1:
                        low(b - 1)
                if lo is not None:
                    low(KB - 1)

            def lows(lo):
                for b in range(KB):
                    dve.wait_ge(S["hi_ready"], lo + b + 1)
                    tt(HL[:, 1, b, :], NT[:, b % 3, :], HL[:, 0, b, :].bitcast(F32), ALU.subtract)\
                        .then_inc(S["lo_ready"], 1)

            rstd(0, MEM)
            normed(0, XM, G_SRC, MEM, lo=0)
            rstd(1)
            dve.wait_ge(S["used"], used(H_POOL))
            normed(1, X, G_MIX, lo=16)
            dve.wait_ge(S["lo_ready"], 32)
            dve.memset(PEX[:, :, 0:BUF], 0.0).then_inc(S["x_added"], 1)
            for g in range(GROUPS):
                w = 2 << g
                if g:
                    dve.wait_ge(S["pool_d"], g)
                dve.wait_ge(S["lin_evac"], B_POOL + 2 * g + 4)
                dve.wait_ge(S["in_pool"], 32 * (g + 1))
                src, ssrc, other = PEX, PSX, [(PTA, PSA), (PTB, PSB)]
                lo = 0
                for s in range(g + 1):
                    sh = 1 << s
                    lo += sh
                    dst, sdst = other[s % 2]
                    tt(dst[:, :, lo:], src[:, :, lo:], src[:, :, lo - sh:BUF + TP - sh], ALU.add)
                    link(tt(sdst[:, :, :, lo:], ssrc[:, :, :, lo:], ssrc[:, :, :, lo - sh:BUF + SQ - sh], ALU.add))
                    src, ssrc = dst, sdst
                if g:
                    dve.wait_ge(S["pool_mm"], g)
                link(stt(DT[:, :, 0:TP], src[:, :, BUF:], 1.0 / w, PEX[:, :, BUF:], ALU.mult, ALU.subtract))
                tmp = other[(g + 1) % 2][0][:, :, 0:w - 1]
                link(tt(tmp, src[:, :, BUF:BUF + w - 1], RC[:, 0:w - 1].unsqueeze(1).to_broadcast([P, 2, w - 1]), ALU.mult))
                tt(DT[:, :, 0:w - 1], tmp, PEX[:, :, BUF:BUF + w - 1], ALU.subtract)
                for c in range(2):
                    ins = stt(DT[:, c, TP:T].rearrange("p (b q) -> p b q", b=SB), ssrc[:, c, :, BUF:], 1.0 / w,
                              PSX[:, c, :, BUF:], ALU.mult, ALU.subtract)
                ins.then_inc(S["pool_d"], 1)
            dve.wait_ge(S["pool_d"], GROUPS)
            dve.wait_ge(S["pool_mm"], GROUPS)
            dve.wait_ge(S["out_a"], 16 * GROUPS)
            dve.wait_ge(S["out_pool"], 64 * GROUPS)
            cos, sin = CS[:, 0, :], CS[:, 1, :]
            with step.loop(RH, 15) as h:
                dve.wait_ge(S["lin_evac"], h * 8 + (B_RET + 4 + 2))
                for r, x1, x2 in ((RQ, RAWQ[:, 0], RAWQ[:, 1]), (RK, RAWQ[:, 2], RAWQ[:, 3])):
                    for o, a, b, op in ((0, cos, sin, ALU.subtract), (1, sin, cos, ALU.add)):
                        tt(r[:, o, :], x1, a, ALU.mult)
                        link(tt(RT[:, o, :], x2, b, ALU.mult))
                        ins = tt(r[:, o, :], r[:, o, :], RT[:, o, :], op)
                    link(ins)
                dve.sem_inc(S["rot_done"], 1)
                dve.wait_ge(S["in_tab"], h * 16 + 16)
                tt(QX, RQ[:, :, TP:T], TAB[:, T_XI:T_XI + TS].unsqueeze(1).to_broadcast([P, 2, TS]), ALU.mult)\
                    .then_inc(S["qx_done"], 1)
                dve.wait_ge(S["k_evac"], h + 1)
                for b in range(SB):
                    ins = ts(KM[:, b, :], KTOK[0:TS, 4, :], TAB[0:TS, T_ZETAS + b:T_ZETAS + b + 1], None, ALU.mult)
                ins.then_inc(S["km_done"], 1)
                dve.wait_ge(S["qk_done"], h + 1)
                for j in range(4):
                    tt(INNER[j], bank(4 + j, TP - P * j), TAB[:, T_DEC:T_DEC + TP - P * j], ALU.mult)
                tt(INNERS, bank(7, TS, TS, 256), TAB[0:TS, T_DECS:T_DECS + TS], ALU.mult).then_inc(S["inner_done"], 1)
                dve.wait_ge(S["o_evac"], h + 1)
                dve.wait_ge(S["mean_done"], h + 1)
                for c in range(2):
                    ins = tt(halves(OT[:, c, :]), halves(OT[:, c, :]), pair(3), ALU.subtract)
                link(ins)
                tt(SQD, OT, OT, ALU.mult).then_inc(S["sqd_ready"], 1)
                for b in range(SB):
                    dve.wait_ge(S["ks_mm"], h * SB + (b + 1))
                    stt(SST[:, b], SST[:, b], TAB[:, T_G8:T_G8 + 1], bank(4 + b % 2).rearrange("p (c n) -> p c n", c=2),
                        ALU.mult, ALU.add).then_inc(S["sst_new"], 1)
                dve.wait_ge(S["rvar_done"], h + 1)
                ts(halves(RVAR), pair(3), EPS, None, ALU.add).then_inc(S["rvar_ready"], 1)
                dve.wait_ge(S["rsd_ready"], h + 1)
                link(dve.reciprocal(RSD, RSD))
                newton(RSD, RVAR, RT[:, 0, :])
                gr = GAINS[:, bass.ds(h * 2 + G_RET, 2)]
                for c in range(2):
                    ins = tt(OT[:, c, :], OT[:, c, :], RSD, ALU.mult)
                link(ins)
                link(tt(OT, OT, wide(gr, T), ALU.mult))
                link(tt(OT, OT, RAWQ[:, 6:8, :], ALU.mult))
                dve.sem_inc(S["b_done"], 1)

            def add_residual(k, first):
                for n in range(KB):
                    dve.wait_ge(S["used"], used(first + 2 * n + 2))
                    tt(halves(X[:, n, :]), halves(X[:, n, :]), pair(n % 2), ALU.add).then_inc(S["lin_evac"], 1)
                    if n:
                        add_square(k, n - 1)
                add_square(k, KB - 1)

            lows(32)
            dve.wait_ge(S["in_x"], 32)
            add_residual(2, H_OUT)
            rstd(2, summed=True)
            normed(2, X, G_MEM, lo=48)
            dve.wait_ge(S["lo_ready"], 64)
            dve.wait_ge(S["out_x"], 16)
            dve.memset(AR[:, 17280:17300], 1.0)
            link(dve.memset(QZ, 0.0))
            with step.loop(MH, 3) as h:
                dve.wait_ge(S["lin_evac"], h * 4 + (B_MQ + 4 + 2))
                for b in range(SB):
                    ins = dve.tensor_copy(QZ[:, b, :, SQ * b:SQ * (b + 1)], QM[:, :, TP + SQ * b:TP + SQ * (b + 1)])
                ins.then_inc(S["qz_done"], 1)
                dve.wait_ge(S["ks_used"], h * SB + (SB + 4))
                dve.tensor_reduce(MX[:, 0:4], PS[:, 2048:3072].rearrange("p (t n) -> p t n", t=4), AX.X, ALU.max)
                link(dve.tensor_reduce(MX[0:TS, 4:5], bank(6, MEM, TS), AX.X, ALU.max))
                ts(NMX, MX, -(MD ** -0.5), None, ALU.mult).then_inc(S["mx_done"], 1)
                dve.wait_ge(S["p_exp"], h + 1)
                link(dve.reciprocal(RSM, SM))
                for t in range(TILES):
                    w = P if t < 4 else TS
                    ins = ts(PR[0:w, t, :], PR[0:w, t, :], RSM[0:w, t:t + 1], None, ALU.mult)
                link(ins)
                dve.sem_inc(S["p_done"], 1)
            lows(64)
            dve.wait_ge(S["in_x"], 48)
            add_residual(3, H_MO)
            rstd(3, summed=True)
            normed(3, X, G_FFN, lo=80)

            dve.wait_ge(S["lo_ready"], 96)
            for s in range(2):
                dve.wait_ge(S[f"out_p{s}"], 16)
            dve.memset(AR[:, 1152:2912], 0.0).then_inc(S["x_added"], 1)
            dve.wait_ge(S["x_added"], 2)

            def top16(items):
                def holds():
                    dve.sem_inc(S["waited_v"], 1)

                holds()
                for vals, sv, _ in items:
                    ins = dve.max(sv[:, 0:8], vals)
                link(ins)
                holds()
                for vals, sv, si in items:
                    ins = dve.max_index(si[:, 0:8], sv[:, 0:8], vals)
                link(ins)
                holds()
                for vals, sv, _ in items:
                    ins = dve.match_replace(vals, sv[:, 0:8], vals, LOWEST)
                link(ins)
                holds()
                for vals, sv, _ in items:
                    ins = dve.max(sv[:, 8:16], vals)
                link(ins)
                holds()
                for vals, sv, si in items:
                    ins = dve.max_index(si[:, 8:16], sv[:, 8:16], vals)
                link(ins)

            with step.loop(EH, 16) as h:
                dve.wait_ge(S["sc_evac"], h + 2)
                top16([(SC[:, c, t, :], SV[:, c, t, :], SI[:, c, t, :]) for c in range(2) for t in range(TILES)])
                dve.sem_inc(S["cand_done"], 1)
                dve.tensor_copy(SIF, SI)
                for t in range(TILES):
                    ins = tt(CAND[:, t, :].rearrange("p (a b) -> p a b", a=TOPK), wide(SV[:, 0, t, :], TOPK),
                             SV[:, 1, t, :].unsqueeze(1).to_broadcast([P, TOPK, TOPK]), ALU.add)
                link(ins)
                top16([(CAND[:, t, :], TV[:, t, :], TI[:, t, :]) for t in range(TILES)])
                ti = TI.rearrange("p t k -> p (t k)")
                ts(TA[:, 0, :], ti, 4, None, ALU.logical_shift_right)
                link(ts(TA[:, 1, :], ti, 15, None, ALU.bitwise_and))
                link(dve.tensor_copy(TAF, TA))
                dve.tensor_copy(GS[:, :, bass.ts(h, TOPK)], TV)
                iota16 = IOTA[:, 0:TOPK].unsqueeze(1).to_broadcast([P, TILES * TOPK, TOPK])
                for c, eq in ((0, EQ), (1, EQ2)):
                    ins = tt(eq, wide(TAF[:, c, :], TOPK), iota16, ALU.is_equal)
                link(ins)
                for c, eq in ((0, EQ), (1, EQ2)):
                    for t in range(TILES):
                        v = eq[:, TOPK * t:TOPK * (t + 1), :]
                        ins = tt(v, v, SIF[:, c, t, :].unsqueeze(1).to_broadcast([P, TOPK, TOPK]), ALU.mult)
                link(ins)
                for c, eq in ((0, EQ), (1, EQ2)):
                    ins = dve.tensor_reduce(IJ[:, c, :, bass.ts(h, TOPK)], eq.rearrange("p (t k) a -> p t k a", t=TILES),
                                            AX.X, ALU.add)
                link(ins)
            gs3 = GS.rearrange("p t (h k) -> p (t h) k", k=TOPK)
            eq3 = EQ[:, 0:TILES * EH, :]
            ex3 = CAND.rearrange("p t n -> p (t n)")[:, 0:640].rearrange("p (a k) -> p a k", k=TOPK)
            tt(eq3, gs3, gs3[:, :, 0:1].to_broadcast([P, TILES * EH, TOPK]), ALU.subtract).then_inc(S["soft_in"], 1)
            dve.wait_ge(S["soft_exp"], 1)
            link(dve.tensor_reduce(SMX, ex3, AX.X, ALU.add))
            link(dve.reciprocal(SMX, SMX))
            tt(gs3, ex3, wide(SMX, TOPK), ALU.mult).then_inc(S["soft_done"], 1)
            dve.wait_ge(S["gt_evac"], 1)
            with dve.Fori(0, NPG) as g:
                for q in range(PG // 4):
                    dve.wait_ge(S["p_mm"], g * (PG // 4) + (q + 1))
                    for k in range(4):
                        t = g * PG + (4 * q + k)
                        ins = ts(AA[:, q % 2, k, :], IOTA, GIJ[:, 1, bass.ds(t, 1)], GIJ[:, 0, bass.ds(t, 1)],
                                 ALU.is_equal, ALU.mult)
                    tt(BB[:, q % 2], IOTA.unsqueeze(1).to_broadcast([P, 4, P]),
                       wide(GIJ[:, 2, bass.ds(g * PG + 4 * q, 4)], P), ALU.is_equal).then_inc(S["pa_ready"], 1)

            def weigh(pr, par, loads):
                dve.wait_ge(S[f"in_p{par}"], loads)
                for e in range(2):
                    gi = GI[:, par, e, :].rearrange("p (g t) -> p g t", t=PG)
                    tt(gi, gi, PP[:, par, :, e, :], ALU.mult).then_inc(S["w_done"], 1)
                for e in range(2):
                    dve.wait_ge(S["whi_done"], pr * 2 + (e + 1))
                    tt(WW[:, par, e, 1, :], GI[:, par, e, :], WW[:, par, e, 0, :].bitcast(F32), ALU.subtract)\
                        .then_inc(S["ww_ready"], 1)

            def accumulate(pr, n, last=False):
                for d in range(KB):
                    if d % 8 < 7:
                        dve.wait_ge(S["v_done"], pr * 14 + (d + 1 - d // 8))
                    else:
                        dve.wait_ge(S["used"], n + used(2 * (d // 8) + 2))
                    tt(halves(X[:, d, :]), halves(X[:, d, :]), pair(2 + d % 2), ALU.add).then_inc(S["v_free"], 1)
                    if last and d:
                        add_square(4, d - 1)

            weigh(0, 0, 32)
            dve.wait_ge(S["in_x"], 64)
            with dve.Fori(0, (NP2 - LAG) // 2) as i:
                for s in range(2):
                    weigh(i * 2 + (s + 1), 1 - s, i * 32 + 32 * (s + 1))
                    accumulate(i * 2 + s, i * 16 + (H_UV + 4 + 8 * s))
            with dve.Fori(0, LAG // 2 - 1) as i:
                for s in range(2):
                    pr = NP2 - LAG + s
                    weigh(i * 2 + (pr + 1), 1 - s, i * 32 + 32 * ((pr + 1) // 2 + 1))
                    accumulate(i * 2 + pr, i * 8 + (H_V + 4 * s))
            weigh(NP2 - 1, 1, 32 * (NP2 // 2))
            accumulate(NP2 - 2, H_ALL - 8)
            accumulate(NP2 - 1, H_ALL - 4, last=True)
            add_square(4, KB - 1)
            rstd(4, summed=True)
            normed(4, X, G_FIN, free=True)


def rotary_tables():
    half = RD // 2
    inv = (np.float32(1.0) / (np.float32(10000.0) ** (np.arange(half, dtype=np.float32) / np.float32(half)))).astype(np.float32)
    pos = np.concatenate([np.arange(TP), np.tile(PAST + np.arange(SQ), SB)]).astype(np.float32)
    ang = (inv[:, None] * pos[None, :]).astype(np.float32).astype(np.float64)
    return np.ascontiguousarray(np.stack([np.cos(ang), np.sin(ang)], 1).astype(np.float32))


def retention_tables():
    tab = np.zeros((RH, P, T_END), np.float32)
    lgs = np.log((1.0 - 2.0 ** (-5.0 - np.arange(RH))).astype(np.float32)).astype(np.float32)
    power = lambda lg, n: np.exp(np.float64(lg) * n).astype(np.float32)
    p, i = np.arange(P)[:, None], np.arange(TP)[None, :]
    s, q = np.arange(TS)[:, None], np.arange(TS)[None, :]
    for h in range(RH):
        lg = lgs[h]
        tab[h, :, T_DEC:T_DEC + TP] = np.where(i >= p, power(lg, np.maximum(i - p, 0)), 0.0)
        same = (s // SQ == q // SQ) & (q >= s)
        tab[h, :TS, T_DECS:T_DECS + TS] = np.where(same, power(lg, np.maximum(q - s, 0)), 0.0)
        tab[h, :, T_XI:T_XI + TS] = power(lg, np.arange(TS) % SQ + 1.0)[None]
        tab[h, :, T_ZETA:T_ZETA + 4] = power(lg, TP - 1.0 - (np.arange(4)[None] * P + p))
        tab[h, :TS, T_ZETAS:T_ZETAS + SB] = np.where(s // SQ == np.arange(SB)[None], power(lg, SQ - 1.0 - s % SQ), 0.0)
        tab[h, :, T_G8] = power(lg, float(SQ))
    return tab


def constants():
    c = np.zeros((P, 272), np.float32)
    c[:, 0:128] = np.eye(P)
    c[:, 128:256] = np.arange(P)[None]
    c[:, 256:272] = 1.0 / (np.arange(16) + 1.0)
    return c


def kernel(**inputs):
    import concourse.bacc as bacc
    from concourse.bass_utils import run_bass_kernel_spmd as run

    a = {k: np.asarray(v) for k, v in inputs.items()}

    def blocks(w):
        n = w.shape[1] // P
        return w.reshape(2, KB // 2, P, n, P).transpose(3, 0, 2, 1, 4).reshape(2 * n, P, HW)

    def blocks_wide(w):
        n = w.shape[1] // 512
        return w.reshape(KB // 2, 2, P, n, 512).transpose(3, 0, 2, 1, 4).reshape(8 * n, P, HW)

    w_in = blocks(a["w_in"][0])
    heads = [w_in[16:].reshape(4, RH, 4, P, HW)[:, h].reshape(16, P, HW) for h in range(RH)]
    w_lin = np.concatenate([blocks(a["w_mk"][0]), blocks_wide(a["w_mv"][0]), w_in[:16], *heads,
                            blocks(a["w_out"][0]), blocks(a["w_mq"][0]), blocks(a["w_mo"][0]), blocks(a["peer_wq"][0])])
    xs = np.concatenate([a["x_prompt"][0], a["x_sample"].reshape(TS, D)], 0)
    gains = np.concatenate([a[n].reshape(-1, P).T for n in
                            ("norm_mix_g", "norm_mem_g", "norm_memsrc_g", "norm_ffn_g", "norm_final_g",
                             "pool_scale", "ret_norm_g")], 1)
    arrays = {
        "xT": xs.T.reshape(KB, P, T),
        "memT": a["mem_prompt"][0].T.reshape(KB, P, MEM),
        "w_lin": w_lin,
        "gains": gains,
        "consts": constants(),
        "spoolT": a["state_pool"][0].transpose(2, 0, 1).reshape(8, P, SB, BUF),
        "sret": a["state_ret"][0],
        "kcT": a["cache_mem_k"][0].transpose(0, 2, 3, 1),
        "vc": a["cache_mem_v"][0].reshape(SB, MEM, D),
        "pool_w": a["pool_w"][0],
        "rot": rotary_tables(),
        "tabs": retention_tables(),
        "subk": a["peer_subkeys"][0].reshape(2 * EH, NK, P).transpose(2, 0, 1),
        "uT": a["peer_u"][0].reshape(NK, P, 2, KB // 2, P).transpose(0, 2, 4, 3, 1).reshape(2 * NK, P, HW),
        "vE": a["peer_v"][0].reshape(NK, P, D),
    }
    outs = {
        "yT": (KB, P, T), "npoolT_p": (8, P, BUF), "nret_p": (RH, RD, RD), "mkT": (KB, P, MEM), "mv": (MEM, D),
        "npoolT_s": (8, P, SB, BUF), "nret_s": (SB, RH, RD, RD),
    }
    nc = bacc.Bacc("TRN2", target_bir_lowering=False, num_devices=1)
    ins, args = {}, []
    for name, v in arrays.items():
        v = np.ascontiguousarray(v)
        ins[f"in_{name}"] = v
        args.append(nc.dram_tensor(f"in_{name}", v.shape, mybir.dt.from_np(v.dtype), kind="ExternalInput").ap())
    for name, shape in outs.items():
        args.append(nc.dram_tensor(f"out_{name}", shape, F32, kind="ExternalOutput").ap())
    build(nc, *args)
    r = run(nc, [ins], core_ids=[0]).results[0]
    o = {name: r[f"out_{name}"] for name in outs}
    y = o["yT"].reshape(D, T).T
    return (
        np.ascontiguousarray(y[:TP]).reshape(1, TP, D),
        np.ascontiguousarray(y[TP:]).reshape(SB, SQ, D),
        np.ascontiguousarray(o["npoolT_p"].reshape(1024, BUF).T).reshape(1, 1, BUF, 1024),
        o["nret_p"].reshape(1, 1, RH, RD, RD),
        np.ascontiguousarray(o["mkT"].reshape(D, MEM).T).reshape(1, 1, MEM, MH, MD),
        o["mv"].reshape(1, 1, MEM, MH, MD),
        np.ascontiguousarray(o["npoolT_s"].reshape(1024, SB, BUF).transpose(1, 2, 0)).reshape(1, SB, BUF, 1024),
        o["nret_s"].reshape(1, SB, RH, RD, RD),
    )
```

```python
from contextlib import ExitStack, contextmanager

import concourse.bass as bass
import numpy as np
from concourse import mybir

F32 = mybir.dt.float32
F32R = mybir.dt.float32r
U32 = mybir.dt.uint32
ACT = mybir.ActivationFunctionType
ALU = mybir.AluOpType
AX = mybir.AxisListType

P = 128
D = 2048
KB = D // P
TP = 512
SB, SQ = 8, 8
TS = SB * SQ
T = TP + TS
HALF = T // 2
PAST = 4096
MEM = 256
GROUPS = 4
BUF = 15
RH, RD = 4, 256
MH, MD = 4, 512
EH = 8
NK = 128
TOPK = 16
TILES = 5
EPS = 1e-6
LOWEST = -3.0e38
HW = 1024
PG = 32
NPG = T // PG

B_MK, B_MV, B_POOL, B_RET, B_OUT, B_MQ, B_MO, B_WQ = 0, 16, 20, 28, 60, 76, 92, 108
H_MV, H_POOL, H_RET, H_OUT, H_MQ, H_MO, H_WQ = 32, 64, 80, 144, 176, 208, 240
NP2 = NK // 2
LAG = EH + 1 + NPG // 2
H_TAIL = H_WQ + 8 * EH
H_P = H_TAIL + 4
H_UV = H_P + 2 * NPG
H_V = H_UV + 8 * (NP2 - LAG)
H_ALL = H_V + 4 * LAG
B_TAIL = B_WQ + 4 * EH
B_P = B_TAIL + 2
B_UV = B_P + NPG

H_HEAD, B_HEAD = H_RET + 4, B_RET + 2
HEAD = (0, 1, 2, 3, 6, 7, 4, 5)
OUT_EARLY, MO_EARLY = KB - RD // P, KB - MD // P
LO_MEM, LO_MIX, LO_OUT, LO_MQ, LO_MO, LO_FFN = 0, 16, 48, 64, 80, 96

G_MIX, G_MEM, G_SRC, G_FFN, G_FIN, G_POOLS, G_RET = 0, 16, 32, 48, 64, 80, 88
T_DEC, T_DECS, T_XI, T_ZETA, T_ZETAS, T_G8, T_END = 0, 512, 576, 640, 644, 652, 653


def used(n):
    return n + 4


def free(n, slots=2):
    return n + 5 - slots


def split(n):
    return n + 5


def v_slot(b):
    return 4 + b if b < 2 else b - 2


class Steps:

    def __init__(self, eng, sem):
        self.eng, self.sem, self.base, self.count, self.i, self.per = eng, sem, 0, 0, None, 0

    def link(self, ins):
        ins.then_inc(self.sem, 1)
        self.count += 1
        at = self.base + self.count
        self.eng.wait_ge(self.sem, at if self.i is None else self.i * self.per + at)

    @contextmanager
    def loop(self, n, per):
        self.base, self.count, self.per = self.base + self.count, 0, per
        with self.eng.Fori(0, n) as i:
            self.i = i
            yield i
        assert self.count == per, (self.count, per)
        self.base, self.count, self.i = self.base + n * per, 0, None


def build(nc, xT, memT, w_lin, gains, consts, spoolT, sret, kcT, vc, pool_w, rot, tabs, subk, uT, vE,
          yT, npoolT_p, nret_p, mkT, mv, npoolT_s, nret_s):
    with ExitStack() as ctx:
        def sb(name, shape, dt=F32):
            return ctx.enter_context(nc.sbuf_tensor(name, shape, dt))

        def sem(name):
            return ctx.enter_context(nc.semaphore(name))

        def dram(name, shape):
            return nc.dram_tensor(name, shape, F32, kind="Internal").ap()

        mixT = dram("mixT", (KB, P, T))
        x2T = dram("x2T", (KB, P, T))
        omT = dram("omT", (KB, P, T))
        x3T = dram("x3T", (KB, P, T))
        pmap = dram("pmap", (NPG, P, NK * PG))
        gel = dram("gel", (NK, P, T))

        HL = sb("HL", [P, 2, KB, T], F32R)
        WS = sb("WS", [P, 4, 2, HW], F32R)
        WW = sb("WW", [P, 2, 2, 2, T], F32R)
        RAW = sb("RAW", [P, 2, HW])
        CS = sb("CS", [P, 2, T])
        CST = sb("CST", [P, 2, P])
        ONES = sb("ONES", [P, 2, P])
        GAINS = sb("GAINS", [P, 96])
        RC = sb("RC", [P, 16])
        AR = sb("AR", [P, 18128])
        PS = ctx.enter_context(nc.psum_tensor("PS", [P, 4096], F32))
        IDENT, IOTA = CST[:, 0, :], CST[:, 1, :]

        def ar(start, *dims, rows=P):
            n = int(np.prod(dims))
            v = AR[0:rows, start:start + n]
            if len(dims) == 1:
                return v
            names = "abcd"[:len(dims)]
            return v.rearrange(f"p ({' '.join(names)}) -> p {' '.join(names)}",
                               **{names[k]: dims[k] for k in range(1, len(dims))})

        def raw(k, many):
            return RAW[:, k, :] if k < 2 else RAWX[:, k - 2, :] if many else RAW[:, k - 2, :]

        def bank(b, n=512, rows=P, off=0):
            return PS[0:rows, 512 * b + off:512 * b + off + n]

        def pair(a):
            return PS[:, 1024 * a:1024 * a + 1024].rearrange("p (b n) -> p b n", b=2)[:, :, 0:HALF]

        def halves(v):
            return v.rearrange("p (b n) -> p b n", b=2)

        def wide(v, n):
            return v.unsqueeze(2).to_broadcast([v.shape[0], v.shape[1], n])

        X = ar(0, KB, T)
        N0 = KB * T
        NSQ, NACC, NVAR, NRS, NT = ar(N0, 2, T), ar(N0 + 1152, T), ar(N0 + 1728, T), ar(N0 + 2304, T), ar(N0 + 2880, 3, T)
        XM, KST, VST = ar(13824, KB, MEM), ar(13824, 2, MEM), ar(13824, 2, 1024)
        RAWX = ar(15872, 2, HW)
        PEX, PTA, PTB = ar(0, 2, BUF + TP), ar(1054, 2, BUF + TP), ar(2108, 2, BUF + TP)
        PSX, PSA, PSB = ar(3162, 2, SB, BUF + SQ), ar(3530, 2, SB, BUF + SQ), ar(3898, 2, SB, BUF + SQ)
        DT, AT, PW = ar(4266, 2, T), ar(5418, 2, T), ar(6570, 2, 256)
        RAWQ, RQ, RK = ar(0, 8, T), ar(4608, 2, T), ar(5760, 2, T)
        OT, SQD, RVAR, RSD = ar(16976, 2, T), ar(5760, 2, T), ar(4608, T), ar(5184, T)
        INNER = [ar(o, TP - P * j) for j, o in enumerate((0, 512, 896, 1152))]
        VTOK, KTOK, KM = ar(6912, TILES, RD), ar(8192, TILES, RD), ar(9472, SB, RD, rows=TS)
        RT = ar(9472, 2, T)
        TAB, QX, SST = ar(11520, T_END), ar(12176, 2, TS), ar(12304, SB, 2, RD)
        SPR, INNERS = ar(16400, 2, RD), ar(16912, TS, rows=TS)
        QM, QZ, KT, VT = ar(0, 4, T), ar(2304, SB, 4, TS), ar(4352, 4, MEM), ar(5376, 2, MD)
        KVS = ar(6400, 6, 2 * MD)
        PR, PT, OB = ar(12544, TILES, MEM), ar(13824, 2, T), ar(14976, 4, T)
        MX, NMX, SM, RSM = ar(17280, TILES), ar(17285, TILES), ar(17290, TILES), ar(17295, TILES)
        Z_OUT = (CS[:, 0, :], CS[:, 1, :], RAWQ[:, 4, :])
        Z_MO = (CS[:, 0, :], CS[:, 1, :], ar(17300, T))
        QP, SC, SV = ar(0, 2, T), ar(1152, 2, TILES, NK), ar(2432, 2, TILES, TOPK)
        SI, SIF = ar(2592, 2, TILES, TOPK).bitcast(U32), ar(2752, 2, TILES, TOPK)
        CAND, TV, TI = ar(2912, TILES, 256), ar(4192, TILES, TOPK), ar(4272, TILES, TOPK).bitcast(U32)
        TA, TAF = ar(4352, 2, TILES * TOPK).bitcast(U32), ar(4512, 2, TILES * TOPK)
        EQ, EQ2 = ar(4672, TILES * TOPK, TOPK), ar(5952, TILES * TOPK, TOPK)
        GS, IJ = ar(7232, TILES, P), ar(7872, 2, TILES, P)
        SMX = ar(4192, TILES * EH)
        SK = ar(13824, 2 * EH, NK)
        GIJ = ar(0, 3, T)
        AA, BB, STG = ar(1728, 2, 4, P), ar(2752, 2, 4, P), ar(3776, 2, NK, PG)
        GO, GI, PP = ar(12000, 2, T), ar(13824, 2, 2, T), ar(9216, 2, NPG, 2, PG)

        names = (
            "in_const in_rot in_x0 in_x1 in_x2 in_x3 in_mem in_tab in_pw in_pool in_p0 in_p1 in_z0 in_z1 in_z2 raw0 raw1 raw2 raw3 "
            "kv_in0 kv_in1 kv_in2 kv_in3 kv_in4 kv_in5 in_kt in_vt in_st "
            "out_k0 out_k1 out_v0 out_v1 out_pool out_a out_spr out_sst out_b out_x out_om out_p0 out_p1 out_y out_g0 out_g1 "
            "consts_set waited_v dve_step used hi_done split_done lin_evac "
            "sq_ready sq_used sum_done var_ready sd_ready t_ready hi_ready lo_ready "
            "pool_d pool_mm pool_evac rot_done qx_done vt_done v_evac kt_done k_evac km_done qk_done inner_done "
            "o_done o_evac spr_evac mean_done sqd_ready rvar_done rvar_ready rsd_ready ks_mm sst_new b_done "
            "x_added qz_done mx_done p_exp p_done pt_done pt_evac om_evac om_done os_evac ks_used vs_used "
            "sk_done sc_evac cand_done soft_in soft_exp soft_done gt_done gt_evac "
            "pa_ready p_mm pbank_free gelu_done w_done whi_done ww_ready v_done v_free"
        ).split()
        S = {n: sem(n) for n in names}

        block = ctx.enter_context(nc.Block())

        def load_x(eng, src):
            for q in range(4):
                eng.dma_start(X[:, 4 * q:4 * q + 4, :], src[4 * q:4 * q + 4].rearrange("k p t -> p k t"))\
                    .then_inc(S[f"in_x{q}"], 16)

        @block.sync
        def _(sp):
            def load(n, k, src, many=False):
                sp.wait_ge(S["split_done"], free(n, 4 if many else 2))
                sp.dma_start(raw(k, many), src.rearrange("a p n -> p (a n)")).then_inc(S[f"raw{k}"], 16)

            def load_lin(first, end, many=False):
                with sp.Fori(0, (end - first) // 4) as i:
                    for k in range(4):
                        load(i * 4 + (first + k), k, w_lin[bass.ds(i * 4 + (first + k), 1)], many)

            sp.dma_start(XM, memT.rearrange("k p m -> p k m")).then_inc(S["in_mem"], 16)
            for dst, src in ((CST[:, :, :], consts[:, 0:256].rearrange("p (a n) -> p a n", a=2)),
                             (RC[:, :], consts[:, 256:272]), (GAINS[:, :], gains)):
                sp.dma_start(dst, src).then_inc(S["in_const"], 16)
            for n in range(8):
                if n == 2:
                    load_x(sp, xT)
                    sp.dma_start(CS[:, :, :], rot).then_inc(S["in_rot"], 16)
                if n == 6:
                    sp.wait_ge(S["t_ready"], KB)
                load(n, n % 4, w_lin[n:n + 1], many=n >= 6)
            load_lin(8, H_RET, many=True)
            load_lin(H_RET, H_MQ + 12)

            sp.wait_ge(S["lo_ready"], LO_MQ + 16)
            sp.wait_ge(S["out_x"], 16)
            cache_v = mv.rearrange("(m p) n -> p m n", p=P)

            def load_k(h, b):
                if b < 4:
                    sp.wait_ge(S["vs_used"], h * SB + (b + 3))
                else:
                    sp.wait_ge(S["ks_used"], h * SB + (b + 1))
                sp.dma_start(KVS[:, b % 4].rearrange("p (c m) -> p c m", c=4),
                             kcT[b, bass.ds(h, 1)].rearrange("a (c p) m -> p (a c) m", p=P))\
                    .then_inc(S[f"kv_in{b % 4}"], 16)

            def load_v(h, b):
                if b < 2:
                    sp.wait_ge(S["vs_used"], h * SB + (b + 7))
                elif b < 6:
                    sp.wait_ge(S["ks_used"], h * SB + (b + 7))
                else:
                    sp.wait_ge(S["vs_used"], h * SB + (b + 3))
                sp.dma_start(KVS[:, v_slot(b)].rearrange("p (m n) -> p m n", m=2),
                             vc[b].rearrange("(m p) n -> p m n", p=P)[:, :, bass.ts(h, MD)])\
                    .then_inc(S[f"kv_in{v_slot(b)}"], 16)

            def first_keys(h):
                for b in range(4):
                    load_k(h, b)
                sp.wait_ge(S["ks_used"], h * SB + 4)
                sp.dma_start(KT, mkT[bass.ts(h, 4)].rearrange("c p m -> p c m")).then_inc(S["in_kt"], 16)

            def caches(h, more):
                def weights(*at):
                    for n in at if more else ():
                        load(h * 8 + (H_MQ + 12 + n), n % 4, w_lin[bass.ds(h * 8 + (H_MQ + 12 + n), 1)])
                for b in range(4, SB):
                    load_k(h, b)
                sp.wait_ge(S["om_done"], h + 1)
                sp.dma_start(VT, cache_v[:, :, bass.ts(h, MD)]).then_inc(S["in_vt"], 16)
                for b in range(6):
                    load_v(h, b)
                weights(0, 1, 2, 3, 4, 5)
                load_v(h, 6)
                load_v(h, 7)
                if more:
                    first_keys(h + 1)
                weights(6, 7)

            first_keys(0)
            with sp.Fori(0, MH - 1) as h:
                caches(h, True)
            caches(MH - 1, False)
            load_lin(H_MO + 4, H_WQ)

            def load_u(pr, n):
                for k in range(4):
                    load(n + k, k, uT[bass.ds(pr * 4 + k, 1)])

            def load_ve(pr, n):
                for k in range(4):
                    load(n + k, k, vE[bass.ds(pr * 2 + k % 2, 1), :, HW * (k // 2):HW * (k // 2 + 1)])

            with sp.Fori(0, EH) as h:
                for k in range(4):
                    load(h * 8 + (H_WQ + k), k, w_lin[bass.ds(h * 4 + (H_WQ + k), 1)])
                load_u(h, h * 8 + (H_WQ + 4))
            with sp.Fori(0, 1 + NPG // 2) as i:
                load_u(i + EH, i * 4 + H_TAIL)
            with sp.Fori(0, NP2 - LAG) as i:
                load_u(i + LAG, i * 8 + H_UV)
                load_ve(i, i * 8 + (H_UV + 4))
            with sp.Fori(0, LAG) as i:
                load_ve(i + (NP2 - LAG), i * 4 + H_V)

        @block.gpsimd
        def _(pool):
            pool.memset(ONES[:, 0, :], 1.0 / D).then_inc(S["consts_set"], 1)
            pool.memset(ONES[:, 1, :], 1.0 / RD).then_inc(S["consts_set"], 1)
            pool.sem_inc(S["split_done"], 4)

            def low_parts(n, many=False):
                for k in range(4):
                    pool.wait_ge(S["hi_done"], n + (k + 1))
                    pool.tensor_tensor(WS[:, k, 1, :], raw(k, many), WS[:, k, 0, :].bitcast(F32), ALU.subtract)\
                        .then_inc(S["split_done"], 1)

            low_parts(0)
            with pool.Fori(0, (H_RET - 4) // 4) as i:
                low_parts(i * 4 + 4, many=True)
            with pool.Fori(0, (H_ALL - H_RET) // 4) as i:
                low_parts(i * 4 + H_RET)

        @block.tensor
        def _(pe):
            mm = pe.matmul
            pe.sem_inc(S["used"], 4)
            pe.sem_inc(S["p_mm"], 2)
            pe.sem_inc(S["ks_used"], 4)
            pe.sem_inc(S["vs_used"], SB)
            pe.sem_inc(S["sk_done"], 1)
            pe.sem_inc(S["om_done"], 1)

            def projection(n, m, a, slot, cols=((0, HALF), (HALF, HALF)), ready=None, between=None,
                           part=(0, KB), marks=(KB // 2 - 1, KB - 1)):
                if part[0] == 0:
                    pe.wait_ge(S["lin_evac"], m + 1)
                for hf in range(2):
                    if hf * (KB // 2) < part[1]:
                        pe.wait_ge(S["split_done"], n + split(hf))
                    for k in range(KB // 2):
                        kb = hf * (KB // 2) + k
                        if not part[0] <= kb < part[1]:
                            continue
                        if ready is not None:
                            pe.wait_ge(S["lo_ready"], ready + kb + 1)
                        first, last = kb == 0, kb == KB - 1
                        for wp, xp in ((0, 0), (0, 1), (1, 0)):
                            for c, (at, w) in enumerate(cols):
                                ins = mm(bank(2 * a + c, w), WS[:, slot + hf, wp, k * P:(k + 1) * P],
                                         HL[:, xp, kb, at:at + w], start=first and (wp, xp) == (0, 0),
                                         stop=last and wp == 1, skip_group_check=True)
                        if kb in marks:
                            ins.then_inc(S["used"], 1)
                        if between and k % 2:
                            between(kb // 2)

            def norm_sum(k, cols=((0, HALF), (HALF, HALF))):
                pe.wait_ge(S["sq_used"], 16 * (k + 1))
                for c, (at, w) in enumerate(cols):
                    ins = mm(bank(6 + c, w), ONES[:, 0, :], NACC[:, at:at + w], start=True, stop=True)
                ins.then_inc(S["sum_done"], 1)

            pe.wait_ge(S["consts_set"], 2)
            pe.wait_ge(S["in_const"], 48)
            norm_sum(0, ((0, MEM),))
            with pe.Fori(0, 8) as i:
                for s in range(2):
                    projection(i * 4 + 2 * s, i * 2 + (B_MK + s), s, 2 * s, ((0, MEM),), ready=LO_MEM)
            norm_sum(1)
            with pe.Fori(0, 2) as i:
                for a in range(2):
                    pe.wait_ge(S["lin_evac"], i * 2 + (B_MV + a + 1))
                    for q in range(8):
                        n = i * 16 + (H_MV + 8 * a + q)
                        pe.wait_ge(S["split_done"], n + split(0))
                        for k in range(2):
                            kb = 2 * q + k
                            for xp, wp in ((0, 0), (0, 1), (1, 0)):
                                for t in range(2):
                                    ins = mm(bank(2 * a + t), HL[:, xp, kb, t * P:(t + 1) * P],
                                             WS[:, q % 4, wp, k * 512:(k + 1) * 512],
                                             start=kb == 0 and (xp, wp) == (0, 0), stop=kb == KB - 1 and xp == 1,
                                             skip_group_check=True)
                        ins.then_inc(S["used"], 1)

            with pe.Fori(0, GROUPS) as g:
                for s in range(2):
                    projection(g * 4 + (H_POOL + 2 * s), g * 2 + (B_POOL + s), s, 2 * s, ready=LO_MIX + 16)
                pe.wait_ge(S["pool_d"], g + 1)
                pe.wait_ge(S["in_pw"], g * 16 + 16)
                pe.wait_ge(S["pool_evac"], g + 1)
                for o in range(2):
                    for c in range(2):
                        for ch in range(2):
                            ins = mm(bank(4 + 2 * o + ch, HALF), PW[:, c, o * P:(o + 1) * P],
                                     DT[:, c, ch * HALF:(ch + 1) * HALF], start=c == 0, stop=c == 1,
                                     skip_group_check=True)
                ins.then_inc(S["pool_mm"], 1)

            def out_early(first, block, m, early, lo):
                projection(first + 2 * m, block + m, m, 2 * m, ready=lo, part=(0, early),
                           marks=(KB // 2 - 1,) if m == 0 else ())

            def out_rest(first, block, early, lo):
                for m, marks in ((0, (KB - 1,)), (1, (KB - 2, KB - 1))):
                    projection(first + 2 * m, block + m, m, 2 * m, ready=lo, part=(early, KB), marks=marks)
                with pe.Fori(0, 7) as i:
                    for s in range(2):
                        projection(i * 4 + (first + 4 + 2 * s), i * 2 + (block + 2 + s), s, 2 * s)

            def head_block(h, m):
                projection(h * 16 + (H_HEAD + 2 * m), h * 8 + (B_HEAD + m), m % 2, 2 * (m % 2))

            def to_rows(src, at):
                for t in range(TILES):
                    w = P if t < 4 else TS
                    for c in range(2):
                        ins = pe.transpose(PS[0:w, 2048 + RD * t + P * c:2048 + RD * t + P * c + P],
                                           src[:, at + c, P * t:P * t + w], IDENT)
                return ins

            def retention(h, more):
                pe.wait_ge(S["lin_evac"], h * 8 + (B_HEAD + 2))
                pe.wait_ge(S["rvar_ready"], h + 1)
                to_rows(RAWQ, 4).then_inc(S["vt_done"], 1)
                for m in range(6):
                    head_block(h, m)
                pe.wait_ge(S["rot_done"], h + 1)
                pe.wait_ge(S["v_evac"], h + 1)
                to_rows(RK, 0).then_inc(S["kt_done"], 1)
                pe.wait_ge(S["k_evac"], h + 1)
                for j in range(4):
                    for c in range(2):
                        mm(bank(4 + j, TP - P * j), RK[:, c, P * j:P * (j + 1)], RQ[:, c, P * j:TP],
                           start=c == 0, stop=c == 1)
                for c in range(2):
                    ins = mm(bank(7, TS, TS, 256), RK[:, c, TP:T], RQ[:, c, TP:T], start=c == 0, stop=c == 1)
                ins.then_inc(S["qk_done"], 1)
                if more:
                    head_block(h, 6)
                pe.wait_ge(S["inner_done"], h + 1)
                pe.wait_ge(S["qx_done"], h + 1)
                pe.wait_ge(S["in_st"], h * 128 + 128)
                for c in range(2):
                    for j in range(4):
                        mm(bank(4 + c, TP - P * j, off=P * j), VTOK[:, j, P * c:P * (c + 1)], INNER[j],
                           start=j == 0, stop=j == 3, skip_group_check=True)
                    mm(bank(6, TS, off=TS * c), VTOK[0:TS, 4, P * c:P * (c + 1)], INNERS,
                       start=True, stop=False, skip_group_check=True)
                    for b in range(SB):
                        for k in range(2):
                            ins = mm(bank(6, SQ, off=TS * c + SQ * b), SST[:, b, k, P * c:P * (c + 1)],
                                     QX[:, k, SQ * b:SQ * (b + 1)], start=False, stop=k == 1, skip_group_check=True)
                ins.then_inc(S["o_done"], 1)
                for c in range(2):
                    for j in range(4):
                        ins = mm(bank(7, RD, off=RD * c), KTOK[:, j, P * c:P * (c + 1)], VTOK[:, j, :],
                                 start=j == 0, stop=j == 3, skip_group_check=True)
                ins.then_inc(S["o_done"], 1)
                if more:
                    head_block(h, 7)
                else:
                    out_early(H_OUT, B_OUT, 0, OUT_EARLY, LO_OUT)
                pe.wait_ge(S["o_evac"], h + 1)
                pe.wait_ge(S["spr_evac"], h + 1)
                for ch in range(2):
                    for c in range(2):
                        ins = mm(bank(6 + ch, HALF), ONES[:, 1, :], OT[:, c, ch * HALF:(ch + 1) * HALF],
                                 start=c == 0, stop=c == 1)
                ins.then_inc(S["mean_done"], 1)
                pe.wait_ge(S["km_done"], h + 1)
                for b in range(SB):
                    if b >= 2:
                        pe.wait_ge(S["sst_new"], h * SB + (b - 1))
                    for c in range(2):
                        ins = mm(bank(4 + b % 2, RD, off=RD * c), KM[:, b, P * c:P * (c + 1)], VTOK[0:TS, 4, :],
                                 start=True, stop=True, skip_group_check=True)
                    ins.then_inc(S["ks_mm"], 1)
                pe.wait_ge(S["sqd_ready"], h + 1)
                for ch in range(2):
                    for c in range(2):
                        ins = mm(bank(6 + ch, HALF), ONES[:, 1, :], SQD[:, c, ch * HALF:(ch + 1) * HALF],
                                 start=c == 0, stop=c == 1)
                ins.then_inc(S["rvar_done"], 1)

            for s in range(2):
                projection(H_RET + 2 * s, B_RET + s, s, 2 * s)
            pe.wait_ge(S["pool_evac"], GROUPS + 1)
            with pe.Fori(0, RH - 1) as h:
                retention(h, True)
            retention(RH - 1, False)
            out_early(H_OUT, B_OUT, 1, OUT_EARLY, LO_OUT)

            out_rest(H_OUT, B_OUT, OUT_EARLY, LO_OUT)
            norm_sum(2)

            def query(h, m):
                projection(h * 8 + (H_MQ + 2 * m), h * 4 + (B_MQ + m), m % 2, 2 * (m % 2), ready=LO_MQ)

            def attention(h, more):
                pe.wait_ge(S["om_evac"], h + 1)
                pe.wait_ge(S["lin_evac"], h * 4 + (B_MQ + 4 + 2))
                pe.wait_ge(S["in_kt"], h * 16 + 16)
                for t in range(4):
                    for c in range(4):
                        mm(bank(4, MEM, off=MEM * t), QM[:, c, P * t:P * (t + 1)], KT[:, c, :],
                           start=c == 0, stop=c == 3, skip_group_check=True)
                pe.wait_ge(S["qz_done"], h + 1)
                for b in range(SB):
                    pe.wait_ge(S[f"kv_in{b % 4}"], h * 48 + 16 * (b // 4 + 1))
                    keys = KVS[:, b % 4].rearrange("p (c m) -> p c m", c=4)
                    for c in range(4):
                        ins = mm(bank(6, MEM, TS), QZ[:, b, c, :], keys[:, c, :],
                                 start=b == 0 and c == 0, stop=b == 7 and c == 3, skip_group_check=True)
                    ins.then_inc(S["ks_used"], 1)
                if more:
                    query(h + 1, 0)
                    query(h + 1, 1)
                else:
                    out_early(H_MO, B_MO, 0, MO_EARLY, LO_MO)
                pe.wait_ge(S["p_done"], h + 1)
                for m in range(2):
                    for t in range(4):
                        pe.transpose(bank(4 + m, P, off=P * t), PR[:, t, P * m:P * (m + 1)], IDENT)
                    ins = pe.transpose(bank(6, TS, off=TS * m), PR[0:TS, 4, P * m:P * (m + 1)], CST[0:TS, 0, 0:TS])
                ins.then_inc(S["pt_done"], 1)
                if more:
                    query(h + 1, 2)
                else:
                    out_early(H_MO, B_MO, 1, MO_EARLY, LO_MO)
                pe.wait_ge(S["pt_evac"], h + 1)
                for b in range(SB):
                    slot = v_slot(b)
                    values = KVS[:, slot].rearrange("p (m n) -> p m n", m=2)
                    pe.wait_ge(S[f"kv_in{slot}"], h * 48 + 48 if slot < 4 else h * 32 + (16 if b < 2 else 32))
                    for c in range(4):
                        for m in range(2):
                            ins = mm(bank(7, SQ, off=TS * c + SQ * b), values[:, m, P * c:P * (c + 1)],
                                     PT[:, m, TP + SQ * b:TP + SQ * (b + 1)], start=m == 0, stop=m == 1,
                                     skip_group_check=True)
                    ins.then_inc(S["vs_used"], 1)
                pe.wait_ge(S["in_vt"], h * 16 + 16)
                for c in range(4):
                    if c == 3:
                        pe.wait_ge(S["os_evac"], h + 1)
                    for m in range(2):
                        ins = mm(bank(4 + c), VT[:, m, P * c:P * (c + 1)], PT[:, m, 0:TP], start=m == 0, stop=m == 1)
                ins.then_inc(S["om_done"], 1)
                if more:
                    query(h + 1, 3)

            for m in range(4):
                query(0, m)
            with pe.Fori(0, MH - 1) as h:
                attention(h, True)
            attention(MH - 1, False)

            out_rest(H_MO, B_MO, MO_EARLY, LO_MO)
            norm_sum(3)

            with pe.Fori(0, EH) as h:
                for s in range(2):
                    projection(h * 8 + (H_WQ + 2 * s), h * 4 + (B_WQ + s), s, 2 * s, ready=LO_FFN)
                projection(h * 8 + (H_WQ + 4), h * 4 + (B_WQ + 2), 0, 0)
                pe.wait_ge(S["lin_evac"], h * 4 + (B_WQ + 2 + 2))
                pe.wait_ge(S["sc_evac"], h + 1)
                pe.wait_ge(S["out_g0"], 16)
                pe.wait_ge(S["out_g1"], 16)
                for c in range(2):
                    keys = SK[:, bass.ds(h * 2 + c, 1), :].rearrange("p a n -> p (a n)")
                    for t in range(TILES):
                        w = P if t < 4 else TS
                        ins = mm(PS[0:w, 512 * (4 + 2 * c) + P * t:512 * (4 + 2 * c) + P * (t + 1)],
                                 QP[:, c, P * t:P * t + w], keys, start=True, stop=True, skip_group_check=True)
                ins.then_inc(S["sk_done"], 1)
                projection(h * 8 + (H_WQ + 6), h * 4 + (B_WQ + 3), 1, 2)
            for s in range(2):
                projection(H_TAIL + 2 * s, B_TAIL + s, s, 2 * s)
            pe.wait_ge(S["soft_done"], 1)
            pe.wait_ge(S["sc_evac"], EH + 1)
            pe.wait_ge(S["lin_evac"], B_P + 2)
            for k, src in enumerate((GS, IJ[:, 0], IJ[:, 1])):
                for t in range(4):
                    pe.transpose(bank(2 * k, P, off=P * t), src[:, t, :], IDENT)
                ins = pe.transpose(bank(2 * k + 1, TS), src[0:TS, 4, :], CST[0:TS, 0, 0:TS])
            ins.then_inc(S["gt_done"], 1)
            pe.wait_ge(S["gt_evac"], 1)
            with pe.Fori(0, NPG // 2) as g:
                for par in range(2):
                    def quad(q):
                        n = g * (PG // 2) + (par * (PG // 4) + q)
                        pe.wait_ge(S["pa_ready"], n + 1)
                        pe.wait_ge(S["pbank_free"], n + 1)
                        for k in range(4):
                            ins = mm(bank(4 + q % 2, P, off=P * k), BB[:, q % 2, k, :], AA[:, q % 2, k, :],
                                     start=True, stop=True, skip_group_check=True)
                        ins.then_inc(S["p_mm"], 1)

                    projection(g * 4 + (H_P + 2 * par), g * 2 + (B_P + par), par, 2 * par, between=quad)

            def up(n, m):
                for e in range(2):
                    projection(n + 2 * e, m + e, e, 2 * e)

            def down(n, v, w, par):
                pe.wait_ge(S["ww_ready"], w)
                for dh in range(2):
                    for e in range(2):
                        pe.wait_ge(S["split_done"], n + split(2 * dh + e))
                    for d8 in range(8):
                        d = 8 * dh + d8
                        pe.wait_ge(S["v_free"], v + (d + 1))
                        for e in range(2):
                            for vp, wp in ((0, 0), (0, 1), (1, 0)):
                                for ch in range(2):
                                    ins = mm(bank(4 + 2 * (d % 2) + ch, HALF), WS[:, 2 * dh + e, vp, P * d8:P * (d8 + 1)],
                                             WW[:, par, e, wp, ch * HALF:(ch + 1) * HALF],
                                             start=e == 0 and (vp, wp) == (0, 0), stop=e == 1 and vp == 1,
                                             skip_group_check=True)
                        if d8 < 7:
                            ins.then_inc(S["v_done"], 1)
                    ins.then_inc(S["used"], 2)

            with pe.Fori(0, (NP2 - LAG) // 2) as i:
                for s in range(2):
                    up(i * 16 + (H_UV + 8 * s), i * 4 + (B_UV + 2 * s))
                    down(i * 16 + (H_UV + 4 + 8 * s), i * 32 + 16 * s, i * 4 + (2 * s + 2), s)
            with pe.Fori(0, LAG // 2) as i:
                for s in range(2):
                    pr = NP2 - LAG + s
                    down(i * 8 + (H_V + 4 * s), i * 32 + 16 * pr, i * 4 + 2 * (pr + 1), s)
            norm_sum(4)

        @block.scalar
        def _(act):
            copy = lambda out, in_, **kw: act.activation(out, in_, ACT.Identity, **kw)
            act.sem_inc(S["lin_evac"], 2)
            act.sem_inc(S["pbank_free"], 2)
            for name in ("pool_evac", "om_evac", "sc_evac"):
                act.sem_inc(S[name], 1)

            def high(n, slot, odd=0):
                k = slot + odd
                many = isinstance(n, int) and 4 <= n < H_RET
                act.wait_ge(S[f"raw{k}"], n * 4 + (16 - 4 * slot))
                copy(WS[:, k, 0, :], raw(k, many)).then_inc(S["hi_done"], 1)

            def high2(n, slot):
                high(n, slot)
                high(n, slot, 1)

            def square(k, b, x, n=T):
                if k or b >= 2:
                    act.wait_ge(S["sq_used"], 16 * k + max(b - 1, 0))
                act.activation(NSQ[:, b % 2, 0:n], x[:, b, :], ACT.Square).then_inc(S["sq_ready"], 1)

            def squares(k, x, n=T):
                for b in range(KB):
                    square(k, b, x, n)

            def root(k, n=T):
                act.wait_ge(S["var_ready"], k + 1)
                act.activation(NRS[:, 0:n], NVAR[:, 0:n], ACT.Sqrt).then_inc(S["sd_ready"], 1)

            def high_part(t, b, at=0, n=T):
                act.wait_ge(S["t_ready"], t + b + 1)
                copy(HL[:, 0, b, at:at + n], NT[:, b % 3, at:at + n]).then_inc(S["hi_ready"], 1)

            def split_early(src, slots, count, before, lo):
                def load(b):
                    if b >= 3:
                        act.wait_ge(S["lo_ready"], lo + b - 2)
                    act.dma_start(slots[b % 3], src[b]).then_inc(S[f"in_z{b % 3}"], 16)
                for b in range(3):
                    load(b)
                for b in range(count):
                    act.wait_ge(S[f"in_z{b % 3}"], 16 * (before[b % 3] + b // 3 + 1))
                    copy(HL[:, 0, b, :], slots[b % 3]).then_inc(S["hi_ready"], 1)
                    if b >= 1 and b + 2 < count:
                        load(b + 2)

            def split_last(src, early):
                for b in range(early, KB):
                    copy(HL[:, 0, b, :], src[:, b - early, :]).then_inc(S["hi_ready"], 1)

            act.wait_ge(S["in_mem"], 16)
            squares(0, XM, MEM)
            root(0, MEM)
            high2(0, 0)
            for b in range(KB):
                high_part(0, b, 0, MEM)
                if b == 11:
                    high2(2, 2)
            for m in range(B_MV):
                s = m % 2
                act.wait_ge(S["used"], used(2 * m + 2))
                high2(2 * m + 4, 2 * s)
                if m >= 2:
                    act.wait_ge(S[f"out_k{s}"], 16 * (m // 2))
                copy(KST[:, s, :], bank(2 * s, MEM)).then_inc(S["lin_evac"], 1)
                act.wait_ge(S["lin_evac"], m + 3)
                act.dma_start(mkT[m], KST[:, s, :]).then_inc(S[f"out_k{s}"], 16)
                if m % 4 == 0:
                    act.wait_ge(S[f"in_x{m // 4}"], 16)
                square(1, m, X)
            root(1)
            for s in range(2):
                act.wait_ge(S[f"out_k{s}"], 128)
            for m in range(4):
                s = m % 2
                for q in range(8):
                    n = H_MV + 8 * m + q
                    act.wait_ge(S["used"], used(n + 1))
                    high(n - q % 2 + 4, q % 4 // 2 * 2, q % 2)
                    if q % 2:
                        high_part(16, 4 * m + q // 2, MEM, T - MEM)
                if m >= 2:
                    act.wait_ge(S[f"out_v{s}"], 16)
                copy(VST[:, s, :], PS[:, 1024 * s:1024 * s + 1024]).then_inc(S["lin_evac"], 1)
                act.wait_ge(S["lin_evac"], B_MV + m + 3)
                act.dma_start(mv.rearrange("(m p) n -> p m n", p=P)[:, :, 512 * m:512 * (m + 1)],
                              VST[:, s, :].rearrange("p (m n) -> p m n", m=2)).then_inc(S[f"out_v{s}"], 16)
            for b in range(KB):
                high_part(32, b, 0, MEM)
            for s in range(2):
                act.wait_ge(S[f"out_v{s}"], 32)
            act.wait_ge(S["lo_ready"], LO_MIX + 32)
            for g in range(GROUPS):
                if g:
                    act.wait_ge(S["pool_mm"], g)
                    act.wait_ge(S["pool_d"], g)
                    act.wait_ge(S["out_pool"], 64 * g)
                act.dma_start(PW, pool_w[g].rearrange("(c p) d -> p c d", p=P)).then_inc(S["in_pw"], 16)
                for c in range(2):
                    act.dma_start(PSX[:, c, :, 0:BUF], spoolT[2 * g + c]).then_inc(S["in_pool"], 16)
                if g == 0:
                    act.wait_ge(S["x_added"], 1)
                for c in range(2):
                    act.wait_ge(S["used"], used(H_POOL + 4 * g + 2 * c + 2))
                    copy(PEX[:, c, BUF:BUF + HALF], bank(2 * c, HALF))
                    copy(PEX[:, c, BUF + HALF:BUF + TP], bank(2 * c + 1, TP - HALF))
                    copy(PSX[:, c, :, BUF:BUF + SQ],
                         bank(2 * c + 1, TS, off=TP - HALF).rearrange("p (b q) -> p b q", b=SB)).then_inc(S["lin_evac"], 1)
                    high2(H_POOL + 4 * g + 2 * c + 4, 2 * c)
                act.wait_ge(S["lin_evac"], B_POOL + 2 * g + 4)
                act.wait_ge(S["in_pool"], 32 * (g + 1))
                for c in range(2):
                    act.dma_start(npoolT_p[2 * g + c], PEX[:, c, TP:TP + BUF]).then_inc(S["out_pool"], 16)
                    act.dma_start(npoolT_s[2 * g + c], PSX[:, c, :, SQ:SQ + BUF]).then_inc(S["out_pool"], 16)
                act.wait_ge(S["pool_mm"], g + 1)
                if g:
                    act.wait_ge(S["out_a"], 16 * g)
                for o in range(2):
                    ins = copy(halves(AT[:, o, :]), pair(2 + o), scale=GAINS[:, G_POOLS + 2 * g + o:G_POOLS + 2 * g + o + 1])
                ins.then_inc(S["pool_evac"], 1)
                act.wait_ge(S["pool_evac"], g + 2)
                act.dma_start(mixT[2 * g:2 * g + 2].rearrange("k p t -> p k t"), AT).then_inc(S["out_a"], 16)
            act.wait_ge(S["pool_d"], GROUPS)
            act.wait_ge(S["out_pool"], 64 * GROUPS)
            act.wait_ge(S["out_a"], 16 * GROUPS)
            def evac_head(h, m):
                act.wait_ge(S["used"], h * 16 + used(H_HEAD + 2 * m + 2))
                kw = {"scale": RD ** -0.5} if m in (2, 3) else {}
                act.activation(halves(RAWQ[:, HEAD[m], :]), pair(m % 2), ACT.Silu if m in (4, 5) else ACT.Identity, **kw)\
                    .then_inc(S["lin_evac"], 1)
                high2(h * 16 + (H_HEAD + 2 * m + 4), 2 * (m % 2))

            def retention(h, more):
                act.dma_start(TAB, tabs[bass.ds(h, 1)].rearrange("a p n -> p (a n)")).then_inc(S["in_tab"], 16)
                for b in range(SB):
                    act.dma_start(SST[:, b], sret[b, bass.ds(h, 1)].rearrange("a (c p) v -> p (a c) v", p=P))\
                        .then_inc(S["in_st"], 16)
                act.wait_ge(S["vt_done"], h + 1)
                copy(VTOK[:, 0:4, :], PS[:, 2048:3072].rearrange("p (t n) -> p t n", t=4))
                copy(VTOK[0:TS, 4, :], bank(6, RD, TS)).then_inc(S["v_evac"], 1)
                for m in range(6):
                    if m == 4:
                        act.wait_ge(S["b_done"], h + 1)
                    evac_head(h, m)
                act.wait_ge(S["kt_done"], h + 1)
                act.wait_ge(S["in_tab"], h * 16 + 16)
                for t in range(4):
                    copy(KTOK[:, t, :], PS[:, 2048 + RD * t:2048 + RD * (t + 1)], scale=TAB[:, T_ZETA + t:T_ZETA + t + 1])
                copy(KTOK[0:TS, 4, :], bank(6, RD, TS)).then_inc(S["k_evac"], 1)
                if more:
                    evac_head(h, 6)
                else:
                    act.wait_ge(S["rot_done"], RH)
                    act.wait_ge(S["used"], used(H_OUT))
                    split_early(mixT, Z_OUT, OUT_EARLY, (0, 0, 0), LO_OUT)
                act.wait_ge(S["o_done"], h * 2 + 1)
                copy(OT[:, :, 0:TP], PS[:, 2048:3072].rearrange("p (c n) -> p c n", c=2))
                copy(OT[:, :, TP:T], bank(6, 2 * TS).rearrange("p (c n) -> p c n", c=2)).then_inc(S["o_evac"], 1)
                act.wait_ge(S["o_done"], h * 2 + 2)
                copy(SPR, bank(7).rearrange("p (c n) -> p c n", c=2)).then_inc(S["spr_evac"], 1)
                act.wait_ge(S["spr_evac"], h + 1)
                act.dma_start(nret_p[bass.ds(h, 1)].rearrange("a (c p) v -> p (a c) v", p=P), SPR).then_inc(S["out_spr"], 16)
                if more:
                    evac_head(h, 7)
                for b in range(SB):
                    act.wait_ge(S["sst_new"], h * SB + (b + 1))
                    act.dma_start(nret_s[b, bass.ds(h, 1)].rearrange("a (c p) v -> p (a c) v", p=P), SST[:, b])\
                        .then_inc(S["out_sst"], 16)
                act.wait_ge(S["rvar_ready"], h + 2)
                act.activation(RSD, RVAR, ACT.Sqrt).then_inc(S["rsd_ready"], 1)
                act.wait_ge(S["b_done"], h + 2)
                if more:
                    act.dma_start(mixT[bass.ds(h * 2 + 8, 2)].rearrange("k p t -> p k t"), OT).then_inc(S["out_b"], 16)
                else:
                    load_x(act, xT)
                    split_last(OT, OUT_EARLY)
                act.wait_ge(S["out_sst"], h * 128 + 128)
                act.wait_ge(S["out_spr"], h * 16 + 16)
                if more:
                    act.wait_ge(S["out_b"], h * 16 + 16)

            for s in range(2):
                act.wait_ge(S["used"], used(H_RET + 2 * s + 2))
                copy(halves(RAWQ[:, 4 + s, :]), pair(s)).then_inc(S["lin_evac"], 1)
                high2(H_RET + 2 * s + 4, 2 * s)
            with act.Fori(0, RH - 1) as h:
                retention(h, True)
            retention(RH - 1, False)

            def add_stage(k, first, m):
                for b in range(KB):
                    act.wait_ge(S["used"], used(first + 2 * b + 2))
                    high2(first + 2 * b + 4, 2 * (b % 2))
                    if b:
                        act.wait_ge(S["lin_evac"], m + b + 2)
                        square(k, b - 1, X)
                act.wait_ge(S["lin_evac"], m + KB + 2)
                square(k, KB - 1, X)

            add_stage(2, H_OUT, B_OUT)
            act.dma_start(x2T.rearrange("k p t -> p k t"), X).then_inc(S["out_x"], 16)
            root(2)
            for b in range(KB):
                high_part(48, b)
            act.wait_ge(S["lo_ready"], LO_MQ + 16)
            act.wait_ge(S["out_x"], 16)

            def evac_query(h, m):
                act.wait_ge(S["used"], h * 8 + used(H_MQ + 2 * m + 2))
                copy(halves(QM[:, m, :]), pair(m % 2)).then_inc(S["lin_evac"], 1)
                high2(h * 8 + (H_MQ + 2 * m + 4), 2 * (m % 2))

            def attention(h, more):
                if not more:
                    act.wait_ge(S["used"], used(H_MO))
                    split_early(omT, Z_MO, MO_EARLY, (5, 5, 4), LO_MO)
                act.wait_ge(S["mx_done"], h + 1)
                for t in range(TILES):
                    w = P if t < 4 else TS
                    ins = act.activation(PR[0:w, t, :], PS[0:w, 2048 + MEM * t:2048 + MEM * (t + 1)], ACT.Exp,
                                         bias=NMX[0:w, t:t + 1], scale=MD ** -0.5, accum_out=SM[0:w, t:t + 1])
                ins.then_inc(S["p_exp"], 1)
                if more:
                    evac_query(h + 1, 0)
                    evac_query(h + 1, 1)
                act.wait_ge(S["pt_done"], h + 1)
                copy(PT[:, :, 0:TP], PS[:, 2048:3072].rearrange("p (m n) -> p m n", m=2))
                copy(PT[:, :, TP:T], bank(6, 2 * TS).rearrange("p (m n) -> p m n", m=2)).then_inc(S["pt_evac"], 1)
                if more:
                    evac_query(h + 1, 2)
                act.wait_ge(S["vs_used"], h * SB + 2 * SB)
                copy(OB[:, :, TP:T], bank(7, 4 * TS).rearrange("p (c n) -> p c n", c=4)).then_inc(S["os_evac"], 1)
                act.wait_ge(S["om_done"], h + 2)
                if not more:
                    load_x(act, x2T)
                copy(OB[:, :, 0:TP], PS[:, 2048:4096].rearrange("p (c n) -> p c n", c=4)).then_inc(S["om_evac"], 1)
                act.wait_ge(S["om_evac"], h + 2)
                if more:
                    act.dma_start(omT[bass.ts(h, 4)].rearrange("k p t -> p k t"), OB).then_inc(S["out_om"], 16)
                    evac_query(h + 1, 3)
                    act.wait_ge(S["out_om"], h * 16 + 16)
                else:
                    split_last(OB, MO_EARLY)

            for m in range(4):
                evac_query(0, m)
            with act.Fori(0, MH - 1) as h:
                attention(h, True)
            attention(MH - 1, False)
            add_stage(3, H_MO, B_MO)
            for s in range(2):
                act.dma_start(x3T[8 * s:8 * s + 8].rearrange("k p t -> p k t"), X[:, 8 * s:8 * s + 8, :])\
                    .then_inc(S[f"out_p{s}"], 16)
            root(3)
            for s in range(2):
                act.dma_start(SK[:, 8 * s:8 * s + 8, :], subk[:, 8 * s:8 * s + 8, :]).then_inc(S[f"out_g{s}"], 16)
            for b in range(KB):
                high_part(64, b)
            act.wait_ge(S["lo_ready"], LO_FFN + 16)
            for s in range(2):
                act.wait_ge(S[f"out_p{s}"], 16)

            def gelu_out(r, n, e, slot):
                act.wait_ge(S["used"], n + used(2))
                act.wait_ge(S[f"out_g{e}"], r * 16 + 16)
                act.activation(halves(GO[:, e, :]), pair(e), ACT.Gelu).then_inc(S["lin_evac"], 1)
                high2(n + 4, slot)

            def store_gelu(r, m, e):
                act.wait_ge(S["lin_evac"], m + 3)
                act.dma_start(gel[bass.ds(r * 2 + e, 1)].rearrange("a p t -> p (a t)"), GO[:, e, :])\
                    .then_inc(S[f"out_g{e}"], 16)

            act.wait_ge(S["x_added"], 2)
            with act.Fori(0, EH) as h:
                act.wait_ge(S["sk_done"], h + 1)
                for c in range(2):
                    act.wait_ge(S["used"], h * 8 + used(H_WQ + 2 * c + 2))
                    copy(halves(QP[:, c, :]), pair(c)).then_inc(S["lin_evac"], 1)
                    high2(h * 8 + (H_WQ + 2 * c + 4), 2 * c)
                gelu_out(h, h * 8 + (H_WQ + 4), 0, 0)
                store_gelu(h, h * 4 + (B_WQ + 2), 0)
                act.wait_ge(S["sk_done"], h + 2)
                act.wait_ge(S["cand_done"], h + 1)
                copy(SC[:, :, 0:4, :].rearrange("p c t n -> p c (t n)"),
                     PS[:, 2048:4096].rearrange("p (c n) -> p c n", c=2)[:, :, 0:512])
                copy(SC[0:TS, :, 4, :], PS[0:TS, 2048:4096].rearrange("p (c n) -> p c n", c=2)[:, :, 512:512 + NK])\
                    .then_inc(S["sc_evac"], 1)
                gelu_out(h, h * 8 + (H_WQ + 6), 1, 2)
                store_gelu(h, h * 4 + (B_WQ + 3), 1)
            for e in range(2):
                gelu_out(EH, H_TAIL + 2 * e, e, 2 * e)
                store_gelu(EH, B_TAIL + e, e)
            act.wait_ge(S["soft_in"], 1)
            act.activation(CAND.rearrange("p t n -> p (t n)")[:, 0:640], EQ.rearrange("p a n -> p (a n)")[:, 0:640], ACT.Exp)\
                .then_inc(S["soft_exp"], 1)
            act.wait_ge(S["gt_done"], 1)
            for k in range(3):
                copy(GIJ[:, k, 0:TP], bank(2 * k))
                ins = copy(GIJ[:, k, TP:T], bank(2 * k + 1, TS))
            ins.then_inc(S["gt_evac"], 1)
            with act.Fori(0, NPG // 2) as g:
                for par in range(2):
                    act.wait_ge(S[f"out_p{par}"], g * 16 + 16)
                    for q in range(PG // 4):
                        n = g * (PG // 2) + (par * (PG // 4) + q)
                        act.wait_ge(S["p_mm"], n + 3)
                        copy(STG[:, par, :, 4 * q:4 * q + 4].rearrange("p i t -> p t i"),
                             bank(4 + q % 2).rearrange("p (t i) -> p t i", t=4)).then_inc(S["pbank_free"], 1)
                    gelu_out(g + (EH + 1), g * 4 + (H_P + 2 * par), par, 2 * par)
                    store_gelu(g + (EH + 1), g * 2 + (B_P + par), par)
                    act.wait_ge(S["pbank_free"], n + 3)
                    act.dma_start(pmap[bass.ds(g * 2 + par, 1)].rearrange("a p n -> p (a n)"),
                                  STG[:, par].rearrange("p i t -> p (i t)")).then_inc(S[f"out_p{par}"], 16)
            for par in range(2):
                act.wait_ge(S[f"out_p{par}"], 16 + 16 * (NPG // 2))

            def load_pair(pr, par):
                for e in range(2):
                    act.wait_ge(S[f"out_g{e}"], pr * 16 + 32)
                act.dma_start(PP[:, par].rearrange("p g e t -> p g (e t)"),
                              pmap.rearrange("g p n -> p g n")[:, :, bass.ts(pr, 2 * PG)]).then_inc(S[f"in_p{par}"], 16)
                act.dma_start(GI[:, par], gel[bass.ts(pr, 2)].rearrange("e p t -> p e t")).then_inc(S[f"in_p{par}"], 16)

            def w_highs(pr, par):
                for e in range(2):
                    act.wait_ge(S["w_done"], pr * 2 + (e + 1))
                    copy(WW[:, par, e, 0, :], GI[:, par, e, :]).then_inc(S["whi_done"], 1)

            load_pair(0, 0)
            load_x(act, x3T)
            load_pair(1, 1)
            w_highs(0, 0)
            load_next = lambda pr, par: (act.wait_ge(S["ww_ready"], pr * 2 - 2), load_pair(pr, par))
            load_next(2, 0)
            with act.Fori(0, (NP2 - LAG) // 2) as i:
                for s in range(2):
                    n = i * 16 + (H_UV + 8 * s)
                    for e in range(2):
                        gelu_out(i * 2 + (LAG + s), n + 2 * e, e, 2 * e)
                        store_gelu(i * 2 + (LAG + s), i * 4 + (B_UV + 2 * s + e), e)
                    w_highs(i * 2 + (s + 1), 1 - s)
                    load_next(i * 2 + (s + 3), 1 - s)
                    for dh in range(2):
                        act.wait_ge(S["used"], n + used(6 + 2 * dh))
                        high2(n + (8 + 2 * dh), 2 * dh)

            def v_stage(pr, n, par, load=True, more=True):
                w_highs(pr + 1, 1 - par)
                if load:
                    load_next(pr + 3, 1 - par)
                for dh in range(2):
                    act.wait_ge(S["used"], n + used(2 + 2 * dh))
                    high2(n + (4 + 2 * dh), 2 * dh)

            looped = LAG // 2 - 2
            with act.Fori(0, looped) as i:
                for s in range(2):
                    v_stage(i * 2 + (NP2 - LAG + s), i * 8 + (H_V + 4 * s), s)
            for k in range(2 * looped, LAG - 1):
                v_stage(NP2 - LAG + k, H_V + 4 * k, k % 2, load=NP2 - LAG + k + 3 < NP2)

            for b in range(KB):
                act.wait_ge(S["v_free"], 2 + 16 * (NP2 - 1) + b + 1)
                square(4, b, X)
            root(4)
            for b, end in ((0, 4), (4, 8), (8, 12), (12, 14), (14, 16)):
                act.wait_ge(S["t_ready"], 80 + end)
                act.dma_start(yT[b:end].rearrange("k p t -> p k t"), X[:, b:end, :]).then_inc(S["out_y"], 16)
            act.wait_ge(S["out_y"], 16 * 5)

        @block.vector
        def _(dve):
            step = Steps(dve, S["dve_step"])
            link = step.link
            tt, ts, stt = dve.tensor_tensor, dve.tensor_scalar, dve.scalar_tensor_tensor
            dve.sem_inc(S["v_free"], 2)
            dve.sem_inc(S["b_done"], 1)
            dve.sem_inc(S["rvar_ready"], 1)
            dve.sem_inc(S["cand_done"], 1)
            dve.wait_ge(S["in_const"], 48)

            def add_square(k, b, n=T):
                dve.wait_ge(S["sq_ready"], 16 * k + b + 1)
                if b:
                    dve.wait_ge(S["sq_used"], 16 * k + b)
                    tt(NACC[:, 0:n], NACC[:, 0:n], NSQ[:, b % 2, 0:n], ALU.add).then_inc(S["sq_used"], 1)
                else:
                    dve.tensor_copy(NACC[:, 0:n], NSQ[:, 0, 0:n]).then_inc(S["sq_used"], 1)

            def newton(r, v, t):
                link(tt(t, v, r, ALU.mult))
                link(tt(t, t, r, ALU.mult))
                link(ts(t, t, -0.5, 1.5, ALU.mult, ALU.add))
                link(tt(r, r, t, ALU.mult))

            def rstd(k, n=T, summed=False):
                if not summed:
                    for b in range(KB):
                        add_square(k, b, n)
                dve.wait_ge(S["sum_done"], k + 1)
                if n == T:
                    ts(halves(NVAR), pair(3), EPS, None, ALU.add).then_inc(S["var_ready"], 1)
                else:
                    ts(NVAR[:, 0:n], bank(6, n), EPS, None, ALU.add).then_inc(S["var_ready"], 1)
                dve.wait_ge(S["sd_ready"], k + 1)
                link(dve.reciprocal(NRS[:, 0:n], NRS[:, 0:n]))
                newton(NRS[:, 0:n], NVAR[:, 0:n], NACC[:, 0:n])

            def scaled(out, x, gain, b, at=0, n=T):
                stt(out, x[:, b, at:at + n], GAINS[:, gain + b:gain + b + 1], NRS[:, at:at + n], ALU.mult, ALU.mult)\
                    .then_inc(S["t_ready"], 1)

            def normed(x, gain, lo, at=0, n=T):
                def low(b):
                    dve.wait_ge(S["hi_ready"], lo + b + 1)
                    tt(HL[:, 1, b, at:at + n], NT[:, b % 3, at:at + n], HL[:, 0, b, at:at + n].bitcast(F32),
                       ALU.subtract).then_inc(S["lo_ready"], 1)
                for b in range(KB):
                    if b >= 3:
                        dve.wait_ge(S["lo_ready"], lo + b - 2)
                    scaled(NT[:, b % 3, at:at + n], x, gain, b, at, n)
                    if b:
                        low(b - 1)
                low(KB - 1)

            def lows(slots, lo, first, end):
                for b in range(first, end):
                    dve.wait_ge(S["hi_ready"], lo + b + 1)
                    tt(HL[:, 1, b, :], slots[b % len(slots)], HL[:, 0, b, :].bitcast(F32), ALU.subtract)\
                        .then_inc(S["lo_ready"], 1)

            rstd(0, MEM)
            normed(XM, G_SRC, LO_MEM, 0, MEM)
            rstd(1)
            normed(X, G_MIX, LO_MIX, MEM, T - MEM)
            dve.wait_ge(S["used"], used(H_POOL))
            dve.wait_ge(S["lo_ready"], LO_MIX + 16)
            normed(X, G_MIX, LO_MIX + 16, 0, MEM)
            dve.wait_ge(S["lo_ready"], LO_MIX + 32)
            dve.memset(PEX[:, :, 0:BUF], 0.0).then_inc(S["x_added"], 1)
            for g in range(GROUPS):
                w = 2 << g
                if g:
                    dve.wait_ge(S["pool_d"], g)
                dve.wait_ge(S["lin_evac"], B_POOL + 2 * g + 4)
                dve.wait_ge(S["in_pool"], 32 * (g + 1))
                src, ssrc, other = PEX, PSX, [(PTA, PSA), (PTB, PSB)]
                lo = 0
                for s in range(g + 1):
                    sh = 1 << s
                    lo += sh
                    dst, sdst = other[s % 2]
                    tt(dst[:, :, lo:], src[:, :, lo:], src[:, :, lo - sh:BUF + TP - sh], ALU.add)
                    link(tt(sdst[:, :, :, lo:], ssrc[:, :, :, lo:], ssrc[:, :, :, lo - sh:BUF + SQ - sh], ALU.add))
                    src, ssrc = dst, sdst
                if g:
                    dve.wait_ge(S["pool_mm"], g)
                link(stt(DT[:, :, 0:TP], src[:, :, BUF:], 1.0 / w, PEX[:, :, BUF:], ALU.mult, ALU.subtract))
                tmp = other[(g + 1) % 2][0][:, :, 0:w - 1]
                link(tt(tmp, src[:, :, BUF:BUF + w - 1], RC[:, 0:w - 1].unsqueeze(1).to_broadcast([P, 2, w - 1]), ALU.mult))
                tt(DT[:, :, 0:w - 1], tmp, PEX[:, :, BUF:BUF + w - 1], ALU.subtract)
                for c in range(2):
                    ins = stt(DT[:, c, TP:T].rearrange("p (b q) -> p b q", b=SB), ssrc[:, c, :, BUF:], 1.0 / w,
                              PSX[:, c, :, BUF:], ALU.mult, ALU.subtract)
                ins.then_inc(S["pool_d"], 1)
            dve.wait_ge(S["pool_d"], GROUPS)
            dve.wait_ge(S["pool_mm"], GROUPS)
            dve.wait_ge(S["out_a"], 16 * GROUPS)
            dve.wait_ge(S["out_pool"], 64 * GROUPS)
            dve.wait_ge(S["in_rot"], 16)
            cos, sin = CS[:, 0, :], CS[:, 1, :]
            def retention(h, more):
                for r, x1, x2, m in ((RQ, RAWQ[:, 0], RAWQ[:, 1], 2), (RK, RAWQ[:, 2], RAWQ[:, 3], 4)):
                    dve.wait_ge(S["lin_evac"], h * 8 + (B_HEAD + m + 2))
                    for o, a, b, op in ((0, cos, sin, ALU.subtract), (1, sin, cos, ALU.add)):
                        tt(r[:, o, :], x1, a, ALU.mult)
                        link(tt(RT[:, o, :], x2, b, ALU.mult))
                        ins = tt(r[:, o, :], r[:, o, :], RT[:, o, :], op)
                    link(ins)
                dve.sem_inc(S["rot_done"], 1)
                dve.wait_ge(S["in_tab"], h * 16 + 16)
                tt(QX, RQ[:, :, TP:T], TAB[:, T_XI:T_XI + TS].unsqueeze(1).to_broadcast([P, 2, TS]), ALU.mult)\
                    .then_inc(S["qx_done"], 1)
                dve.wait_ge(S["k_evac"], h + 1)
                for b in range(SB):
                    ins = ts(KM[:, b, :], KTOK[0:TS, 4, :], TAB[0:TS, T_ZETAS + b:T_ZETAS + b + 1], None, ALU.mult)
                ins.then_inc(S["km_done"], 1)
                if not more:
                    lows(Z_OUT, LO_OUT, 0, 6)
                dve.wait_ge(S["qk_done"], h + 1)
                for j in range(4):
                    tt(INNER[j], bank(4 + j, TP - P * j), TAB[:, T_DEC:T_DEC + TP - P * j], ALU.mult)
                tt(INNERS, bank(7, TS, TS, 256), TAB[0:TS, T_DECS:T_DECS + TS], ALU.mult).then_inc(S["inner_done"], 1)
                if not more:
                    lows(Z_OUT, LO_OUT, 6, OUT_EARLY)
                dve.wait_ge(S["o_evac"], h + 1)
                dve.wait_ge(S["mean_done"], h + 1)
                for c in range(2):
                    ins = tt(halves(OT[:, c, :]), halves(OT[:, c, :]), pair(3), ALU.subtract)
                link(ins)
                tt(SQD, OT, OT, ALU.mult).then_inc(S["sqd_ready"], 1)
                for b in range(SB):
                    dve.wait_ge(S["ks_mm"], h * SB + (b + 1))
                    stt(SST[:, b], SST[:, b], TAB[:, T_G8:T_G8 + 1], bank(4 + b % 2).rearrange("p (c n) -> p c n", c=2),
                        ALU.mult, ALU.add).then_inc(S["sst_new"], 1)
                dve.wait_ge(S["rvar_done"], h + 1)
                ts(halves(RVAR), pair(3), EPS, None, ALU.add).then_inc(S["rvar_ready"], 1)
                dve.wait_ge(S["rsd_ready"], h + 1)
                link(dve.reciprocal(RSD, RSD))
                newton(RSD, RVAR, RT[:, 0, :])
                gr = GAINS[:, bass.ds(h * 2 + G_RET, 2)]
                for c in range(2):
                    ins = tt(OT[:, c, :], OT[:, c, :], RSD, ALU.mult)
                link(ins)
                link(tt(OT, OT, wide(gr, T), ALU.mult))
                link(tt(OT, OT, RAWQ[:, 6:8, :], ALU.mult))
                dve.sem_inc(S["b_done"], 1)

            with step.loop(RH - 1, 15) as h:
                retention(h, True)
            retention(RH - 1, False)
            dve.sem_inc(S["rvar_ready"], 1)

            def add_residual(k, first):
                for n in range(KB):
                    dve.wait_ge(S["used"], used(first + 2 * n + 2))
                    if n % 4 == 0:
                        dve.wait_ge(S[f"in_x{n // 4}"], 16 * k)
                    tt(halves(X[:, n, :]), halves(X[:, n, :]), pair(n % 2), ALU.add).then_inc(S["lin_evac"], 1)
                    if n:
                        add_square(k, n - 1)
                add_square(k, KB - 1)

            lows((OT[:, 0, :], OT[:, 1, :]), LO_OUT, OUT_EARLY, KB)
            dve.wait_ge(S["out_sst"], 128 * RH)
            add_residual(2, H_OUT)
            rstd(2, summed=True)
            normed(X, G_MEM, LO_MQ)
            dve.wait_ge(S["lo_ready"], LO_MQ + 16)
            dve.wait_ge(S["out_x"], 16)
            dve.memset(AR[:, 17280:17300], 1.0)
            link(dve.memset(QZ, 0.0))
            def attention(h, more):
                dve.wait_ge(S["lin_evac"], h * 4 + (B_MQ + 4 + 2))
                for b in range(SB):
                    ins = dve.tensor_copy(QZ[:, b, :, SQ * b:SQ * (b + 1)], QM[:, :, TP + SQ * b:TP + SQ * (b + 1)])
                ins.then_inc(S["qz_done"], 1)
                if not more:
                    lows(Z_MO, LO_MO, 0, MO_EARLY)
                dve.wait_ge(S["ks_used"], h * SB + (SB + 4))
                dve.tensor_reduce(MX[:, 0:4], PS[:, 2048:3072].rearrange("p (t n) -> p t n", t=4), AX.X, ALU.max)
                link(dve.tensor_reduce(MX[0:TS, 4:5], bank(6, MEM, TS), AX.X, ALU.max))
                ts(NMX, MX, -(MD ** -0.5), None, ALU.mult).then_inc(S["mx_done"], 1)
                dve.wait_ge(S["p_exp"], h + 1)
                link(dve.reciprocal(RSM, SM))
                for t in range(TILES):
                    w = P if t < 4 else TS
                    ins = ts(PR[0:w, t, :], PR[0:w, t, :], RSM[0:w, t:t + 1], None, ALU.mult)
                link(ins)
                dve.sem_inc(S["p_done"], 1)

            with step.loop(MH - 1, 3) as h:
                attention(h, True)
            attention(MH - 1, False)
            lows([OB[:, c, :] for c in range(4)], LO_MO, MO_EARLY, KB)
            add_residual(3, H_MO)
            rstd(3, summed=True)
            normed(X, G_FFN, LO_FFN)

            dve.wait_ge(S["lo_ready"], LO_FFN + 16)
            for s in range(2):
                dve.wait_ge(S[f"out_p{s}"], 16)
            dve.memset(AR[:, 1152:2912], 0.0).then_inc(S["x_added"], 1)
            dve.wait_ge(S["x_added"], 2)

            def top16(items):
                def holds():
                    dve.sem_inc(S["waited_v"], 1)

                holds()
                for vals, sv, _ in items:
                    ins = dve.max(sv[:, 0:8], vals)
                link(ins)
                holds()
                for vals, sv, si in items:
                    ins = dve.max_index(si[:, 0:8], sv[:, 0:8], vals)
                link(ins)
                holds()
                for vals, sv, _ in items:
                    ins = dve.match_replace(vals, sv[:, 0:8], vals, LOWEST)
                link(ins)
                holds()
                for vals, sv, _ in items:
                    ins = dve.max(sv[:, 8:16], vals)
                link(ins)
                holds()
                for vals, sv, si in items:
                    ins = dve.max_index(si[:, 8:16], sv[:, 8:16], vals)
                link(ins)

            with step.loop(EH, 16) as h:
                dve.wait_ge(S["sc_evac"], h + 2)
                top16([(SC[:, c, t, :], SV[:, c, t, :], SI[:, c, t, :]) for c in range(2) for t in range(TILES)])
                dve.sem_inc(S["cand_done"], 1)
                dve.tensor_copy(SIF, SI)
                for t in range(TILES):
                    ins = tt(CAND[:, t, :].rearrange("p (a b) -> p a b", a=TOPK), wide(SV[:, 0, t, :], TOPK),
                             SV[:, 1, t, :].unsqueeze(1).to_broadcast([P, TOPK, TOPK]), ALU.add)
                link(ins)
                top16([(CAND[:, t, :], TV[:, t, :], TI[:, t, :]) for t in range(TILES)])
                ti = TI.rearrange("p t k -> p (t k)")
                ts(TA[:, 0, :], ti, 4, None, ALU.logical_shift_right)
                link(ts(TA[:, 1, :], ti, 15, None, ALU.bitwise_and))
                link(dve.tensor_copy(TAF, TA))
                dve.tensor_copy(GS[:, :, bass.ts(h, TOPK)], TV)
                iota16 = IOTA[:, 0:TOPK].unsqueeze(1).to_broadcast([P, TILES * TOPK, TOPK])
                for c, eq in ((0, EQ), (1, EQ2)):
                    ins = tt(eq, wide(TAF[:, c, :], TOPK), iota16, ALU.is_equal)
                link(ins)
                for c, eq in ((0, EQ), (1, EQ2)):
                    for t in range(TILES):
                        v = eq[:, TOPK * t:TOPK * (t + 1), :]
                        ins = tt(v, v, SIF[:, c, t, :].unsqueeze(1).to_broadcast([P, TOPK, TOPK]), ALU.mult)
                link(ins)
                for c, eq in ((0, EQ), (1, EQ2)):
                    ins = dve.tensor_reduce(IJ[:, c, :, bass.ts(h, TOPK)], eq.rearrange("p (t k) a -> p t k a", t=TILES),
                                            AX.X, ALU.add)
                link(ins)
            gs3 = GS.rearrange("p t (h k) -> p (t h) k", k=TOPK)
            eq3 = EQ[:, 0:TILES * EH, :]
            ex3 = CAND.rearrange("p t n -> p (t n)")[:, 0:640].rearrange("p (a k) -> p a k", k=TOPK)
            tt(eq3, gs3, gs3[:, :, 0:1].to_broadcast([P, TILES * EH, TOPK]), ALU.subtract).then_inc(S["soft_in"], 1)
            dve.wait_ge(S["soft_exp"], 1)
            link(dve.tensor_reduce(SMX, ex3, AX.X, ALU.add))
            link(dve.reciprocal(SMX, SMX))
            tt(gs3, ex3, wide(SMX, TOPK), ALU.mult).then_inc(S["soft_done"], 1)
            dve.wait_ge(S["gt_evac"], 1)
            with dve.Fori(0, NPG) as g:
                for q in range(PG // 4):
                    dve.wait_ge(S["p_mm"], g * (PG // 4) + (q + 1))
                    for k in range(4):
                        t = g * PG + (4 * q + k)
                        ins = ts(AA[:, q % 2, k, :], IOTA, GIJ[:, 1, bass.ds(t, 1)], GIJ[:, 0, bass.ds(t, 1)],
                                 ALU.is_equal, ALU.mult)
                    tt(BB[:, q % 2], IOTA.unsqueeze(1).to_broadcast([P, 4, P]),
                       wide(GIJ[:, 2, bass.ds(g * PG + 4 * q, 4)], P), ALU.is_equal).then_inc(S["pa_ready"], 1)

            def product(pr, par, e):
                gi = GI[:, par, e, :].rearrange("p (g t) -> p g t", t=PG)
                tt(gi, gi, PP[:, par, :, e, :], ALU.mult).then_inc(S["w_done"], 1)

            def low(pr, par, e):
                dve.wait_ge(S["whi_done"], pr * 2 + (e + 1))
                tt(WW[:, par, e, 1, :], GI[:, par, e, :], WW[:, par, e, 0, :].bitcast(F32), ALU.subtract)\
                    .then_inc(S["ww_ready"], 1)

            def accumulate(pr, n, par, loads=None, last=False):
                for d in range(KB):
                    if d % 8 < 7:
                        dve.wait_ge(S["v_done"], pr * 14 + (d + 1 - d // 8))
                    else:
                        dve.wait_ge(S["used"], n + used(2 * (d // 8) + 2))
                    tt(halves(X[:, d, :]), halves(X[:, d, :]), pair(2 + d % 2), ALU.add).then_inc(S["v_free"], 1)
                    if last and d:
                        add_square(4, d - 1)
                    if loads is not None:
                        if d == 0:
                            dve.wait_ge(S[f"in_p{1 - par}"], loads)
                        if d in (0, 1):
                            product(pr + 1, 1 - par, d)
                        if d in (4, 5):
                            low(pr + 1, 1 - par, d - 4)

            dve.wait_ge(S["in_p0"], 32)
            for e in range(2):
                product(0, 0, e)
            for e in range(2):
                low(0, 0, e)
            for q in range(4):
                dve.wait_ge(S[f"in_x{q}"], 64)
            with dve.Fori(0, (NP2 - LAG) // 2) as i:
                for s in range(2):
                    accumulate(i * 2 + s, i * 16 + (H_UV + 4 + 8 * s), s, loads=i * 32 + 32 * (s + 1))
            with dve.Fori(0, LAG // 2 - 1) as i:
                for s in range(2):
                    pr = NP2 - LAG + s
                    accumulate(i * 2 + pr, i * 8 + (H_V + 4 * s), s, loads=i * 32 + 32 * ((pr + 1) // 2 + 1))
            accumulate(NP2 - 2, H_ALL - 8, 0, loads=32 * (NP2 // 2))
            accumulate(NP2 - 1, H_ALL - 4, 1, last=True)
            add_square(4, KB - 1)
            rstd(4, summed=True)
            for b in range(KB):
                scaled(X[:, b, :], X, G_FIN, b)


def rotary_tables():
    half = RD // 2
    inv = (np.float32(1.0) / (np.float32(10000.0) ** (np.arange(half, dtype=np.float32) / np.float32(half)))).astype(np.float32)
    pos = np.concatenate([np.arange(TP), np.tile(PAST + np.arange(SQ), SB)]).astype(np.float32)
    ang = (inv[:, None] * pos[None, :]).astype(np.float32).astype(np.float64)
    return np.ascontiguousarray(np.stack([np.cos(ang), np.sin(ang)], 1).astype(np.float32))


def retention_tables():
    tab = np.zeros((RH, P, T_END), np.float32)
    lgs = np.log((1.0 - 2.0 ** (-5.0 - np.arange(RH))).astype(np.float32)).astype(np.float32)
    power = lambda lg, n: np.exp(np.float64(lg) * n).astype(np.float32)
    p, i = np.arange(P)[:, None], np.arange(TP)[None, :]
    s, q = np.arange(TS)[:, None], np.arange(TS)[None, :]
    for h in range(RH):
        lg = lgs[h]
        tab[h, :, T_DEC:T_DEC + TP] = np.where(i >= p, power(lg, np.maximum(i - p, 0)), 0.0)
        same = (s // SQ == q // SQ) & (q >= s)
        tab[h, :TS, T_DECS:T_DECS + TS] = np.where(same, power(lg, np.maximum(q - s, 0)), 0.0)
        tab[h, :, T_XI:T_XI + TS] = power(lg, np.arange(TS) % SQ + 1.0)[None]
        tab[h, :, T_ZETA:T_ZETA + 4] = power(lg, TP - 1.0 - (np.arange(4)[None] * P + p))
        tab[h, :TS, T_ZETAS:T_ZETAS + SB] = np.where(s // SQ == np.arange(SB)[None], power(lg, SQ - 1.0 - s % SQ), 0.0)
        tab[h, :, T_G8] = power(lg, float(SQ))
    return tab


def constants():
    c = np.zeros((P, 272), np.float32)
    c[:, 0:128] = np.eye(P)
    c[:, 128:256] = np.arange(P)[None]
    c[:, 256:272] = 1.0 / (np.arange(16) + 1.0)
    return c


def kernel(**inputs):
    import concourse.bacc as bacc
    from concourse.bass_utils import run_bass_kernel_spmd as run

    a = {k: np.asarray(v) for k, v in inputs.items()}

    def blocks(w):
        n = w.shape[1] // P
        return w.reshape(2, KB // 2, P, n, P).transpose(3, 0, 2, 1, 4).reshape(2 * n, P, HW)

    def blocks_wide(w):
        n = w.shape[1] // 512
        return w.reshape(KB // 2, 2, P, n, 512).transpose(3, 0, 2, 1, 4).reshape(8 * n, P, HW)

    w_in = blocks(a["w_in"][0])
    q, k, v, gate = w_in[16:].reshape(4, RH, 4, P, HW)
    heads = [v[0]]
    for h in range(RH):
        heads += [q[h], k[h], gate[h]] + ([v[h + 1]] if h + 1 < RH else [])
    w_lin = np.concatenate([blocks(a["w_mk"][0]), blocks_wide(a["w_mv"][0]), w_in[:16], *heads,
                            blocks(a["w_out"][0]), blocks(a["w_mq"][0]), blocks(a["w_mo"][0]), blocks(a["peer_wq"][0])])
    xs = np.concatenate([a["x_prompt"][0], a["x_sample"].reshape(TS, D)], 0)
    gains = np.concatenate([a[n].reshape(-1, P).T for n in
                            ("norm_mix_g", "norm_mem_g", "norm_memsrc_g", "norm_ffn_g", "norm_final_g",
                             "pool_scale", "ret_norm_g")], 1)
    arrays = {
        "xT": xs.T.reshape(KB, P, T),
        "memT": a["mem_prompt"][0].T.reshape(KB, P, MEM),
        "w_lin": w_lin,
        "gains": gains,
        "consts": constants(),
        "spoolT": a["state_pool"][0].transpose(2, 0, 1).reshape(8, P, SB, BUF),
        "sret": a["state_ret"][0],
        "kcT": a["cache_mem_k"][0].transpose(0, 2, 3, 1),
        "vc": a["cache_mem_v"][0].reshape(SB, MEM, D),
        "pool_w": a["pool_w"][0],
        "rot": rotary_tables(),
        "tabs": retention_tables(),
        "subk": a["peer_subkeys"][0].reshape(2 * EH, NK, P).transpose(2, 0, 1),
        "uT": a["peer_u"][0].reshape(NK, P, 2, KB // 2, P).transpose(0, 2, 4, 3, 1).reshape(2 * NK, P, HW),
        "vE": a["peer_v"][0].reshape(NK, P, D),
    }
    outs = {
        "yT": (KB, P, T), "npoolT_p": (8, P, BUF), "nret_p": (RH, RD, RD), "mkT": (KB, P, MEM), "mv": (MEM, D),
        "npoolT_s": (8, P, SB, BUF), "nret_s": (SB, RH, RD, RD),
    }
    nc = bacc.Bacc("TRN2", target_bir_lowering=False, num_devices=1)
    ins, args = {}, []
    for name, v in arrays.items():
        v = np.ascontiguousarray(v)
        ins[f"in_{name}"] = v
        args.append(nc.dram_tensor(f"in_{name}", v.shape, mybir.dt.from_np(v.dtype), kind="ExternalInput").ap())
    for name, shape in outs.items():
        args.append(nc.dram_tensor(f"out_{name}", shape, F32, kind="ExternalOutput").ap())
    build(nc, *args)
    r = run(nc, [ins], core_ids=[0]).results[0]
    o = {name: r[f"out_{name}"] for name in outs}
    y = o["yT"].reshape(D, T).T
    return (
        np.ascontiguousarray(y[:TP]).reshape(1, TP, D),
        np.ascontiguousarray(y[TP:]).reshape(SB, SQ, D),
        np.ascontiguousarray(o["npoolT_p"].reshape(1024, BUF).T).reshape(1, 1, BUF, 1024),
        o["nret_p"].reshape(1, 1, RH, RD, RD),
        np.ascontiguousarray(o["mkT"].reshape(D, MEM).T).reshape(1, 1, MEM, MH, MD),
        o["mv"].reshape(1, 1, MEM, MH, MD),
        np.ascontiguousarray(o["npoolT_s"].reshape(1024, SB, BUF).transpose(1, 2, 0)).reshape(1, SB, BUF, 1024),
        o["nret_s"].reshape(1, SB, RH, RD, RD),
    )
```
